# Optimizing a Trainium2 kernel written in Bass

```python
import jax
import jax.numpy as jnp
from jax import lax
import numpy as np

D_MODEL = 2048
BATCH = 1
SEQ = 256
DEPTH = 1

HEAD_DIM = 128
HA = 8
HA_KV = 2
H_IDX = 16
D_IDX = 64
TOPK_MAX = 256
HB = 8
ROPE_THETA = 500000.0
ROT_A = HEAD_DIM // 4
ROT_IDX = D_IDX // 4
Q_BLOCK = 128
D_FF = -(-8 * D_MODEL // (3 * 256)) * 256
D_PLE = 256
EPS = 1e-6
NEG_INF = float('-inf')

SPLIT_SIZES = (
    HA * HEAD_DIM,
    HA_KV * HEAD_DIM,
    HA_KV * HEAD_DIM,
    H_IDX * D_IDX,
    D_IDX,
    H_IDX,
    HB * HEAD_DIM,
    HB * HEAD_DIM,
    HB * HEAD_DIM,
    HB,
    D_MODEL,
    D_MODEL,
)
N_IN = sum(SPLIT_SIZES)

kernel_name = 'hybrid_dsa_fox_gated_block'

def rmsnorm(x, g):
    xf = x.astype(jnp.float32)
    xf = xf * lax.rsqrt(jnp.mean(xf * xf, axis=-1, keepdims=True) + EPS)
    return (xf * g.astype(jnp.float32)).astype(x.dtype)

def partial_rope(x, pos, rot):
    half = rot // 2
    inv_freq = ROPE_THETA ** (-jnp.arange(half, dtype=jnp.float32) / half)
    ang = pos.astype(jnp.float32)[:, :, None] * inv_freq
    cos = jnp.cos(ang)[:, :, None, :]
    sin = jnp.sin(ang)[:, :, None, :]
    x1 = x[..., :half].astype(jnp.float32)
    x2 = x[..., half:rot].astype(jnp.float32)
    rotated = jnp.concatenate([x1 * cos - x2 * sin, x2 * cos + x1 * sin], axis=-1).astype(x.dtype)
    return jnp.concatenate([rotated, x[..., rot:]], axis=-1)

def to_blocks(a):
    b, t = a.shape[:2]
    return jnp.moveaxis(a.reshape(b, t // Q_BLOCK, Q_BLOCK, *a.shape[2:]), 1, 0)

def from_blocks(a):
    a = jnp.moveaxis(a, 0, 1)
    return a.reshape(a.shape[0], a.shape[1] * a.shape[2], *a.shape[3:])

def dsa_sparse_attention(q, k, v, q_idx, k_idx, w_idx, top_k):
    t_len = q.shape[1]
    group = HA // HA_KV
    scale = HEAD_DIM ** -0.5
    key_pos = jnp.arange(t_len)
    t_blocks = key_pos.reshape(t_len // Q_BLOCK, Q_BLOCK)
    gather = jax.vmap(lambda table, idx: table[idx])

    def block(args):
        qb, qib, wib, tb = args
        nb = qb.shape[0]
        dots = jnp.einsum('bqhd,bsd->bqhs', qib, k_idx).astype(jnp.float32)
        score = jnp.einsum('bqh,bqhs->bqs', wib.astype(jnp.float32), jax.nn.relu(dots))
        causal = key_pos[None, :] <= tb[:, None]
        score = jnp.where(causal[None], score, NEG_INF)
        _, sel = lax.top_k(score, top_k)
        valid = sel <= tb[None, :, None]
        k_sel = gather(k, sel)
        v_sel = gather(v, sel)
        qg = qb.reshape(nb, Q_BLOCK, HA_KV, group, HEAD_DIM)
        logits = jnp.einsum('bqngd,bqsnd->bqngs', qg, k_sel).astype(jnp.float32) * scale
        logits = jnp.where(valid[:, :, None, None, :], logits, NEG_INF)
        prob = jax.nn.softmax(logits, axis=-1).astype(v.dtype)
        out = jnp.einsum('bqngs,bqsnd->bqngd', prob, v_sel)
        return out.reshape(nb, Q_BLOCK, HA * HEAD_DIM)

    out = lax.map(block, (to_blocks(q), to_blocks(q_idx), to_blocks(w_idx), t_blocks))
    return from_blocks(out)

def forgetting_attention(q, k, v, log_fcum):
    t_len = q.shape[1]
    scale = HEAD_DIM ** -0.5
    key_pos = jnp.arange(t_len)
    t_blocks = key_pos.reshape(t_len // Q_BLOCK, Q_BLOCK)
    c_keys = jnp.swapaxes(log_fcum, 1, 2)

    def block(args):
        qb, cb, tb = args
        nb = qb.shape[0]
        logits = jnp.einsum('bqhd,bshd->bhqs', qb, k).astype(jnp.float32) * scale
        logits = logits + jnp.swapaxes(cb, 1, 2)[..., None] - c_keys[:, :, None, :]
        causal = key_pos[None, :] <= tb[:, None]
        logits = jnp.where(causal[None, None], logits, NEG_INF)
        prob = jax.nn.softmax(logits, axis=-1).astype(v.dtype)
        out = jnp.einsum('bhqs,bshd->bqhd', prob, v)
        return out.reshape(nb, Q_BLOCK, HB * HEAD_DIM)

    out = lax.map(block, (to_blocks(q), to_blocks(log_fcum), t_blocks))
    return from_blocks(out)

def setup_inputs(seed: int = 0) -> dict:
    key = jax.random.key(seed)
    ks = jax.random.split(key, 17)
    f32 = jnp.float32

    def normal(k, shape, fan_in):
        return jax.random.normal(k, shape, f32) * fan_in ** -0.5

    def gain(k, shape):
        return 1.0 + 0.05 * jax.random.normal(k, shape, f32)

    wa = HA * HEAD_DIM
    wb = HB * HEAD_DIM
    return {
        'x': jax.random.normal(ks[0], (BATCH, SEQ, D_MODEL), f32),
        'p': jax.random.normal(ks[1], (DEPTH, BATCH, SEQ, D_PLE), f32),
        'positions': jnp.broadcast_to(jnp.arange(SEQ, dtype=jnp.int32), (BATCH, SEQ)),
        'g_mix': gain(ks[2], (DEPTH, D_MODEL)),
        'w_in': normal(ks[3], (DEPTH, D_MODEL, N_IN), D_MODEL),
        'b_f': 1.0 + 0.5 * jax.random.normal(ks[4], (DEPTH, HB), f32),
        'w_o_a': normal(ks[5], (DEPTH, wa, D_MODEL), wa),
        'w_o_b': normal(ks[6], (DEPTH, wb, D_MODEL), wb),
        'w_out': normal(ks[7], (DEPTH, D_MODEL, D_MODEL), D_MODEL),
        'g_ffn': gain(ks[8], (DEPTH, D_MODEL)),
        'w_ffn_gate': normal(ks[9], (DEPTH, D_MODEL, D_FF), D_MODEL),
        'w_ffn_up': normal(ks[10], (DEPTH, D_MODEL, D_FF), D_MODEL),
        'w_ffn_down': normal(ks[11], (DEPTH, D_FF, D_MODEL), D_FF),
        'g_ple': gain(ks[12], (DEPTH, D_MODEL)),
        'w_ple_gate': normal(ks[13], (DEPTH, D_MODEL, D_MODEL), D_MODEL),
        'w_ple_proj': normal(ks[14], (DEPTH, D_PLE, D_MODEL), D_PLE),
        'g_final': gain(ks[15], (D_MODEL,)),
    }

def reference(x, p, positions, g_mix, w_in, b_f, w_o_a, w_o_b, w_out, g_ffn,
              w_ffn_gate, w_ffn_up, w_ffn_down, g_ple, w_ple_gate, w_ple_proj, g_final):
    b, t_len, _ = x.shape
    top_k = min(TOPK_MAX, t_len // 4)
    split_at = [int(s) for s in np.cumsum(SPLIT_SIZES)[:-1]]
    for i in range(DEPTH):
        h = rmsnorm(x, g_mix[i])
        proj = h @ w_in[i]
        (q_a, k_a, v_a, q_i, k_i, w_i, q_b, k_b, v_b, f_b, gate_a, gate_b) = jnp.split(proj, split_at, axis=-1)

        q_a = partial_rope(q_a.reshape(b, t_len, HA, HEAD_DIM), positions, ROT_A)
        k_a = partial_rope(k_a.reshape(b, t_len, HA_KV, HEAD_DIM), positions, ROT_A)
        v_a = v_a.reshape(b, t_len, HA_KV, HEAD_DIM)
        q_i = partial_rope(q_i.reshape(b, t_len, H_IDX, D_IDX), positions, ROT_IDX)
        k_i = partial_rope(k_i[:, :, None, :], positions, ROT_IDX)[:, :, 0, :]
        w_i = w_i * (H_IDX ** -0.5 * D_IDX ** -0.5)
        out_a = dsa_sparse_attention(q_a, k_a, v_a, q_i, k_i, w_i, top_k)

        log_f = jax.nn.log_sigmoid(f_b.astype(jnp.float32) + b_f[i].astype(jnp.float32))
        log_fcum = jnp.cumsum(log_f, axis=1)
        out_b = forgetting_attention(q_b.reshape(b, t_len, HB, HEAD_DIM),
                                     k_b.reshape(b, t_len, HB, HEAD_DIM),
                                     v_b.reshape(b, t_len, HB, HEAD_DIM), log_fcum)

        y_a = out_a @ w_o_a[i]
        y_b = out_b @ w_o_b[i]
        mixed = jax.nn.sigmoid(gate_a) * y_a + jax.nn.sigmoid(gate_b) * y_b
        x = x + mixed @ w_out[i]

        h = rmsnorm(x, g_ffn[i])
        x = x + (jax.nn.silu(h @ w_ffn_gate[i]) * (h @ w_ffn_up[i])) @ w_ffn_down[i]

        h = rmsnorm(x, g_ple[i])
        x = x + jax.nn.sigmoid(h @ w_ple_gate[i]) * (p[i] @ w_ple_proj[i])
    return rmsnorm(x, g_final)


_drawn_inputs = setup_inputs


def setup_inputs(seed=0):
    import zlib

    import numpy as np

    out = dict(_drawn_inputs(seed))
    spreads = {}
    factors = {'g_ple': 7.262}
    for name, (base, spread) in spreads.items():
        noise = np.random.default_rng([zlib.crc32(name.encode()), seed]).standard_normal(out[name].shape)
        drawn = base * np.exp(spread * noise) if base else spread * noise
        out[name] = jnp.asarray(drawn.astype(out[name].dtype))
    for name, factor in factors.items():
        out[name] = (out[name] * factor).astype(out[name].dtype)
    return out
```

```python
import concourse.bass as bass
from concourse import mybir

F32 = mybir.dt.float32
F32R = mybir.dt.float32r
I32 = mybir.dt.int32
ALU = mybir.AluOpType
ACT = mybir.ActivationFunctionType
AX_X = mybir.AxisListType.X
ds = bass.ds

P = 128
D_MODEL, TOK, D_FF, D_PLE = 2048, 256, 5632, 256
HA, HA_KV, H_IDX, D_IDX, HB, HEAD = 8, 2, 16, 64, 8, 128
ROT_A, ROT_IDX, THETA = HEAD // 4, D_IDX // 4, 500000.0
TOP_K = 64
EPS = 1e-6
KT = D_MODEL // P
KT_O = HA * HEAD // P
KT_FF = D_FF // P
KT_PLE = D_PLE // P
GROUP = 256
SLOTS = 4
KC = 4
CHUNK = KC * GROUP
SCALE = HEAD ** -0.5
MASKED = -3.0e38
TAKEN = -3.4e38
TAKEN_BELOW = -3.2e38
F_ROWS = slice(32, 32 + HB)
FREE = 1
CAT = P + TOK

AT_QA = 0
AT_KA = AT_QA + HA * HEAD
AT_VA = AT_KA + HA_KV * HEAD
AT_QI = AT_VA + HA_KV * HEAD
AT_KI = AT_QI + H_IDX * D_IDX
AT_WI = AT_KI + D_IDX
AT_QB = AT_WI + H_IDX
AT_KB = AT_QB + HB * HEAD
AT_VB = AT_KB + HB * HEAD
AT_FB = AT_VB + HB * HEAD
AT_GA = AT_FB + HB
AT_GB = AT_GA + D_MODEL

U_SMALL = 0
U_QI = U_SMALL + 1
U_QB = U_QI + 4
U_KB = U_QB + 4
U_VB = U_KB + 4
U_GA = U_VB + 4
U_QA = U_GA + 8
U_KA = U_QA + 4
U_VA = U_KA + 1
U_GB = U_VA + 1
U_WO = U_GB + 8
U_OUT = U_WO + 8
U_FFN = U_OUT + 8
N_FFN = D_FF // GROUP
U_DOWN = U_FFN + 2 * N_FFN
U_PROJ = U_DOWN + 3 * 8
U_PLE = U_PROJ + 1
U_END = U_PLE + 8
G_DOWN = U_DOWN
G_PROJ = G_DOWN + 8
G_PLE = G_PROJ + SLOTS
G_END = G_PLE + 8
DOWN_TILES = [4] * 8 + [3] * 4
HEADS = HB + HA
F_ROW = 32
STEPS_IDX = H_IDX * D_IDX // P


class Count:

    def __init__(self, eng, sem):
        self.eng, self.sem, self.fixed, self.moving = eng, sem, 0, 0

    def step(self, ins):
        ins.then_inc(self.sem, 1)
        self.fixed += 1
        self.eng.wait_ge(self.sem, self.moving + self.fixed)

    def enter(self, i, steps):
        self.start, self.steps, self.moving = self.fixed, steps, i * steps

    def leave(self, trips):
        assert self.fixed - self.start == self.steps, self.fixed - self.start
        self.fixed, self.moving = self.start + trips * self.steps, 0


def hybrid_layer(nc, x, p, positions, g_mix, w_in, b_f, w_o_a, w_o_b, w_out, g_ffn, w_ffn_gate,
                 w_ffn_up, w_ffn_down, g_ple, w_ple_gate, w_ple_proj, g_final, rope_rows, out):
    x_rows = x[0].rearrange("(b q) n -> q b n", q=P)
    p_rows = p[0, 0].rearrange("(b q) n -> q b n", q=P)
    out_rows = out[0].rearrange("(b q) n -> q b n", q=P)

    def tiles_of(w):
        return w[0].rearrange("(t q) n -> q t n", q=P)

    win_t, woa_t, wob_t, wout_t = map(tiles_of, (w_in, w_o_a, w_o_b, w_out))
    wgate_t, wup_t, wdown_t = map(tiles_of, (w_ffn_gate, w_ffn_up, w_ffn_down))
    wpg_t, wpp_t = map(tiles_of, (w_ple_gate, w_ple_proj))

    base = (nc.sbuf_base + 31) // 32 * 32

    def sb(name, kb, shape, dt=F32):
        return nc.alloc_sbuf_tensor_at(name, [P, *shape], dt, offset=base + int(kb * 1024))

    res = sb("res", 0, [KT, TOK])
    heads_o = sb("heads_o", 16, [KT, 2 * TOK], F32R)
    xg = sb("xg", 16, [KT, 2 * TOK], F32R)
    hn = sb("hn", 48, [KT, 2 * TOK], F32R)
    mixed = sb("mixed", 48, [KT, 2 * TOK], F32R)
    ff = sb("ff", 48, [KT_FF, 2 * TOK], F32R)
    gates = sb("gates", 80, [2, KT, TOK])
    q_idx = sb("q_idx", 80, [KT_O, TOK])
    rope = sb("rope", 104, [4, 2 * TOK])
    ang = sb("ang", 88, [2, TOK])
    ang_r = sb("ang_r", 90, [4, TOK])
    turn = sb("turn", 94, [2, TOK])
    relu_sb = sb("relu_sb", 96, [3 * TOK])
    kib = sb("kib", 99, [2 * TOK])
    junk = sb("junk", 64, [2, D_MODEL])
    x_tok = sb("x_tok", 112, [2, D_MODEL])
    q_cols = sb("q_cols", 112, [8, TOK])
    k_cols = sb("k_cols", 120, [8, TOK])
    v_rows = sb("v_rows", 128, [2, HB * HEAD])
    y_ple = sb("y_ple", 48, [KT, TOK])
    out_tok = sb("out_tok", 64, [2, D_MODEL])
    fin = sb("fin", 80, [2, 2, TOK])
    ws = sb("ws", 136, [SLOTS, CHUNK])
    hs = sb("hs", 152, [SLOTS, CHUNK], F32R)
    ls = sb("ls", 168, [SLOTS, CHUNK], F32R)
    lo = sb("lo", 184, [2, 2 * TOK])
    s_a = sb("s_a", 188, [2 * TOK])
    s_b = sb("s_b", 190, [2 * TOK])
    lg = sb("lg", 192, [CAT])
    pt = sb("pt", 193.5, [CAT])
    cm = sb("cm", 195, [CAT])
    mask = sb("mask", 196.5, [CAT])
    sel = sb("sel", 198, [CAT])
    q_st = sb("q_st", 199.5, [TOK])
    k_st = sb("k_st", 200.5, [TOK])
    v_st = sb("v_st", 201.5, [2, P])
    p_tok = sb("p_tok", 192, [2, D_PLE])
    silu_g = sb("silu_g", 192, [2 * TOK])
    lo_b = sb("lo_b", 194, [2, 2 * TOK])
    p_cols = sb("p_cols", 194, [KT_PLE, 2 * TOK], F32R)
    sq_sum = sb("sq_sum", 198, [2 * TOK])
    rms = sb("rms", 200, [2 * TOK])
    ident = sb("ident", 202.5, [P])
    ones = sb("ones", 203, [P])
    neg_id = sb("neg_id", 203.5, [P])
    c_cat = sb("c_cat", 204, [CAT])
    gains = sb("gains", 205.5, [4 * KT])
    w_tok = sb("w_tok", 205.75, [2, H_IDX])
    c_tok = sb("c_tok", 205.875, [2, HB])
    top8 = sb("top8", 205.9375, [2, 8])
    neg_max = sb("neg_max", 206, [2])
    sums = sb("sums", 206 + 1 / 32, [2])
    rsum = sb("rsum", 206 + 2 / 32, [2])
    r_tok = sb("r_tok", 206 + 3 / 32, [4])
    eps = sb("eps", 206 + 4 / 32, [1])
    half_pi = sb("half_pi", 206 + 5 / 32, [1])
    bias_f = sb("bias_f", 206 + 6 / 32, [1])
    rope_c = sb("rope_c", 206 + 7 / 32, [4])
    sq = sb("sq", 206.25, [TOK])
    pos_i = sb("pos_i", 101, [TOK], I32)
    pos_f = sb("pos_f", 102, [TOK])
    gain_rows = sb("gain_rows", 103, [P])
    diag = sb("diag", 193.5, [2, P])
    f_w = sb("f_w", 88, [4, TOK])

    acc = nc.alloc_psum_tensor("acc", [P, 4, 512], F32)
    side = nc.alloc_psum_tensor("side", [P, 4, 512], F32)

    S = nc.alloc_semaphore
    x_loaded = [S(f"x_loaded{b}") for b in range(2)]
    gains_loaded = S("gains_loaded")
    const_loaded, p_loaded, out_stored = S("const_loaded"), S("p_loaded"), S("out_stored")
    w_loaded = [S(f"w_loaded{j}") for j in range(SLOTS)]
    h_split, l_split, chunk_used = S("h_split"), S("l_split"), S("chunk_used")
    lo_ready, combined = S("lo_ready"), S("combined")
    consts, ring_zero = S("consts"), S("ring_zero")
    pool_step, dve_step, act_step = S("pool_step"), S("dve_step"), S("act_step")
    angles, rope_sin = S("angles"), S("rope_sin")
    gain_t, gain_ready = S("gain_t"), S("gain_ready")
    x_squares, x_rms, diag_ready, rms_b, rms_sb = map(S, (
        "x_squares", "x_rms", "diag_ready", "rms_b", "rms_sb"))
    x_t, res_ready, hn_f, hn_high, hn_ready = map(S, ("x_t", "res_ready", "hn_f", "hn_high", "hn_ready"))
    f_z, f_e, f_l, f_c, small_t, small_ready, c_t = map(S, (
        "f_z", "f_e", "f_l", "f_c", "small_t", "small_ready", "c_t"))
    small_s = S("small_s")
    staged, v_staged, rope_done = S("staged"), S("v_staged"), S("rope_done")
    dots_done, relu_done, idx_done = S("dots_done"), S("relu_done"), S("idx_done")
    cm_ready, qk_done, max_ready, exp_done = map(S, ("cm_ready", "qk_done", "max_ready", "exp_done"))
    prob_ready, pt_done, pt_ready, pv_done, o_high, o_ready = map(S, (
        "prob_ready", "pt_done", "pt_ready", "pv_done", "o_high", "o_ready"))
    gate_ready = S("gate_ready")
    mix_s, mix_high, mix_ready = S("mix_s"), S("mix_high"), S("mix_ready")
    x_new, xg_high, xg_ready, sq_done = S("x_new"), S("xg_high"), S("xg_ready"), S("sq_done")
    ms_done, ms_sqrt, rms_ready = S("ms_done"), S("ms_sqrt"), S("rms_ready")
    p_t, p_high, p_ready = S("p_t"), S("p_high"), S("p_ready")
    ffg_s, ffg_silu, ff_s, ff_high, ff_ready = map(S, ("ffg_s", "ffg_silu", "ff_s", "ff_high", "ff_ready"))
    pg_s, pg_sig, fin_ready, fin_t, fin_read = map(S, ("pg_s", "pg_sig", "fin_ready", "fin_t", "fin_read"))
    tok_done, tok_sqrt, tok_ready, y_ready = map(S, ("tok_done", "tok_sqrt", "tok_ready", "y_ready"))

    block = nc.Block()
    block.__enter__()

    @block.sync
    def _(sp):
        for b in range(2):
            sp.dma_start(x_tok[:, b, :], x_rows[:, b, :]).then_inc(x_loaded[b], 16)

        def slot_free(u, j):
            sp.wait_ge(l_split, 4 * (u - 1) + j + 1)

        def load(j, src, n=CHUNK):
            parts = src.shape[1]
            sp.dma_start(ws[:, j, 0:n].rearrange("p (t n) -> p t n", t=parts), src).then_inc(w_loaded[j], 16)

        sp.wait_ge(ring_zero, 1)
        for j in range(SLOTS):
            slot = ws[:, j, :].rearrange("p (t n) -> p t n", t=KC)
            rows = win_t[:, KC * j:KC * j + KC, :]
            for at, col, n in ((0, AT_KI, D_IDX), (D_IDX, AT_KI, D_IDX + H_IDX), (P + F_ROW, AT_FB, HB)):
                sp.dma_start(slot[:, :, at:at + n], rows[:, :, col:col + n]).then_inc(w_loaded[j], 16)

        def columns(u0, units, w, col0):
            with sp.Fori(0, units) as i:
                for j in range(SLOTS):
                    slot_free(u0 + i, j)
                    load(j, w[:, KC * j:KC * j + KC, ds(col0 + i * GROUP, GROUP)])

        columns(U_QI, 4, win_t, AT_QI)
        columns(U_QB, 12, win_t, AT_QB)
        columns(U_GA, 8, win_t, AT_GA)
        columns(U_QA, 6, win_t, AT_QA)
        columns(U_GB, 8, win_t, AT_GB)
        with sp.Fori(0, 8) as i:
            for j in range(SLOTS):
                slot_free(U_WO + i, j)
                w, t = (wob_t, woa_t)[j // 2], KC * (j % 2)
                load(j, w[:, t:t + KC, ds(i * GROUP, GROUP)])
        sp.wait_ge(o_ready, FREE + HEADS)
        sp.dma_start(p_tok[:, :, :], p_rows).then_inc(p_loaded, 16)
        columns(U_OUT, 8, wout_t, 0)
        with sp.Fori(0, N_FFN) as i:
            for half, w in enumerate((wgate_t, wup_t)):
                for j in range(SLOTS):
                    slot_free(U_FFN + half + i * 2, j)
                    load(j, w[:, KC * j:KC * j + KC, ds(i * GROUP, GROUP)])
        with sp.Fori(0, 8) as i:
            t = 0
            for c, n in enumerate(DOWN_TILES):
                slot_free(U_DOWN + c // SLOTS + i * 3, c % SLOTS)
                load(c % SLOTS, wdown_t[:, t:t + n, ds(i * GROUP, GROUP)], n * GROUP)
                t += n
        for j in range(SLOTS):
            slot_free(U_PROJ, j)
            load(j, wpp_t[:, :, 2 * GROUP * j:2 * GROUP * (j + 1)])
        columns(U_PLE, 8, wpg_t, 0)
        for n in range(4):
            sp.wait_ge(y_ready, n + 1)
            half = slice(D_MODEL // 2 * (n // 2), D_MODEL // 2 * (n // 2 + 1))
            sp.dma_start(out_rows[:, n % 2, half], out_tok[:, n % 2, half]).then_inc(out_stored, 16)
        sp.wait_ge(out_stored, 4 * 16)

    @block.gpsimd
    def _(pool):
        chain = Count(pool, pool_step)
        for sem in (dots_done, idx_done, relu_done, qk_done, pv_done, prob_ready, pt_ready, o_ready):
            pool.sem_inc(sem, FREE)
        ring = ws[:, :, :].rearrange("p s (t n) -> p (s t) n", n=GROUP)
        pool.memset(ring[:, :, P:GROUP], 0.0).then_inc(ring_zero, 1)
        pool.memset(ones[:, :], 1.0).then_inc(consts, 1)
        pool.memset(eps[:, :], EPS).then_inc(consts, 1)
        pool.memset(c_cat[:, :], 0.0).then_inc(consts, 1)
        pool.memset(kib[:, :], 0.0).then_inc(consts, 1)
        pool.memset(mask[:, :], 0.0).then_inc(consts, 1)
        pool.memset(neg_id[:, :], 0.0).then_inc(consts, 1)
        chain.step(pool.memset(ident[:, :], 0.0))
        pool.wait_ge(consts, 6)
        pool.affine_select(out=ident[:, :], in_=ident[:, :], compare_op=ALU.not_equal, fill=1.0, base=0,
                           pattern=[[-1, P]], channel_multiplier=1).then_inc(consts, 1)
        pool.affine_select(out=neg_id[:, :], in_=neg_id[:, :], compare_op=ALU.not_equal, fill=-1.0, base=0,
                           pattern=[[-1, P]], channel_multiplier=1).then_inc(consts, 1)
        for at in (0, CAT - P):
            tri = mask[:, at:at + P]
            pool.affine_select(out=tri, in_=tri, compare_op=ALU.is_ge, fill=MASKED, base=0,
                               pattern=[[-1, P]], channel_multiplier=1).then_inc(consts, 1)

        pool.wait_ge(rope_done, 4)
        with pool.Fori(0, STEPS_IDX) as e:
            pool.wait_ge(dots_done, FREE + e)
            pool.tensor_copy(q_st[:, :], q_idx[:, ds(e, 1), :]).then_inc(staged, 1)

        def stage_head(head, q_at, kv_at, values):
            pool.wait_ge(qk_done, FREE + head)
            pool.tensor_copy(q_st[:, :], q_cols[:, ds(q_at, 1), :]).then_inc(staged, 1)
            pool.tensor_copy(k_st[:, :], k_cols[:, ds(kv_at, 1), :]).then_inc(staged, 1)
            pool.wait_ge(combined, values)
            pool.wait_ge(pv_done, FREE + head)
            pool.tensor_copy(v_st[:, :, :], v_rows[:, :, ds(kv_at * P, P)]).then_inc(v_staged, 1)

        pool.wait_ge(dots_done, FREE + STEPS_IDX)
        pool.wait_ge(combined, U_VB)
        with pool.Fori(0, HB) as h:
            stage_head(h, h, h, U_VB + 4)
        pool.wait_ge(rope_done, 9)
        with pool.Fori(0, HA) as h:
            stage_head(HB + h, h, h // (HA // HA_KV), U_VA + 1)

        def square_sums(n0):
            pool.wait_ge(x_new, n0 + 1)
            chain.step(pool.tensor_tensor(sq_sum[:, 0:TOK], res[:, 0, :], res[:, 0, :], ALU.mult))
            pool.tensor_tensor(sq_sum[:, TOK:2 * TOK], res[:, 1, :], res[:, 1, :], ALU.mult).then_inc(sq_done, 1)
            with pool.Fori(0, 7) as i:
                chain.enter(i, 3)
                pool.wait_ge(sq_done, n0 + 1 + i)
                pool.wait_ge(x_new, n0 + 2 + i)
                even, odd = res[:, ds(i * 2 + 2, 1), :], res[:, ds(i * 2 + 3, 1), :]
                chain.step(pool.tensor_tensor(sq[:, :], even, even, ALU.mult))
                chain.step(pool.tensor_tensor(sq_sum[:, 0:TOK], sq_sum[:, 0:TOK], sq[:, :], ALU.add))
                chain.step(pool.tensor_tensor(sq[:, :], odd, odd, ALU.mult))
                pool.tensor_tensor(sq_sum[:, TOK:2 * TOK], sq_sum[:, TOK:2 * TOK], sq[:, :], ALU.add).then_inc(sq_done, 1)
            chain.leave(7)

        pool.wait_ge(o_ready, FREE + HEADS)
        square_sums(0)
        pool.wait_ge(ms_done, 1)
        square_sums(8)
        pool.wait_ge(ms_done, 2)
        square_sums(16)

    @block.scalar
    def _(act):
        chain = Count(act, act_step)

        def split_high(u, j, n=CHUNK, first=False):
            if first:
                act.wait_ge(w_loaded[j], 3 * 16)
            else:
                act.wait_ge(w_loaded[j], 3 * 16 + 16 * u)
                act.wait_ge(chunk_used, 4 * (u - 1) + j + 1)
            act.activation(hs[:, j, 0:n], ws[:, j, 0:n], ACT.Copy).then_inc(h_split, 1)

        def take_lo(u_done, g, pair, scale=1.0, bank=acc, dst=None, when=None):
            act.wait_ge(chunk_used, 4 * (u_done + 1) if when is None else when)
            dst = lo[:, pair, :] if dst is None else dst
            act.activation(dst.rearrange("p (m n) -> p m n", m=2), bank[:, 2 * pair:2 * pair + 2, TOK:2 * TOK],
                           ACT.Copy, scale=scale).then_inc(lo_ready, 1)

        for n, g in enumerate((g_mix[0], g_ffn[0], g_ple[0], g_final)):
            act.dma_start(gain_rows[n * KT:(n + 1) * KT, :], g.rearrange("(t q) -> t q", q=P)).then_inc(gains_loaded, 16)
        act.dma_start(pos_i[:, :], positions.partition_broadcast(P)).then_inc(const_loaded, 16)
        act.dma_start(rope_c[:, :], rope_rows).then_inc(const_loaded, 16)
        act.dma_start(bias_f[F_ROWS, :], b_f[0].rearrange("(h o) -> h o", o=1)).then_inc(const_loaded, 16)

        act.wait_ge(consts, 10)
        for b in range(2):
            act.wait_ge(x_loaded[b], 16)
            act.activation(junk[:, b, :], x_tok[:, b, :], ACT.Square, accum_out=r_tok[:, b:b + 1]).then_inc(x_squares, 1)
        act.wait_ge(x_squares, 2)
        act.activation(r_tok[:, 2:4], r_tok[:, 0:2], ACT.Sqrt, bias=eps[:, 0:1], scale=1.0 / D_MODEL).then_inc(x_rms, 1)
        act.wait_ge(gain_t, 1)
        act.activation(gains[:, :], side[:, 0, 0:4 * KT], ACT.Copy).then_inc(gain_ready, 1)
        for t in range(KT // 2 + 1):
            if t < KT // 2:
                act.wait_ge(x_t, t + 1)
                act.activation(res[:, 2 * t:2 * t + 2, :].rearrange("p m n -> p (m n)"), acc[:, t % 4, :],
                               ACT.Copy).then_inc(res_ready, 1)
            if t == 0:
                act.wait_ge(rms_b, 1)
                act.activation(s_b[:, 0:TOK], side[:, 1, 0:TOK], ACT.Copy).then_inc(rms_sb, 1)
            if t % 2 == 0 and t < 2 * SLOTS:
                split_high(0, t // 2, first=True)
            if t > 0:
                act.wait_ge(hn_f, t)
                act.activation(hn[:, 2 * t - 2:2 * t, 0:TOK],
                               (s_a, lo[:, 0, :])[(t - 1) % 2][:, 0:2 * TOK].rearrange("p (m n) -> p m n", m=2),
                               ACT.Copy).then_inc(hn_high, 1)
        split_high(1, 0)
        act.wait_ge(angles, 1)
        for k in range(4):
            at = (0, 2, 1, 3)[k]
            for d in range(2):
                act.activation(rope[:, at, d * TOK:(d + 1) * TOK], ang_r[:, k, :], ACT.Sin).then_inc(rope_sin, 1)
        for j in range(1, SLOTS):
            split_high(1, j)

        take_lo(U_SMALL, 0, 0)
        act.wait_ge(f_z, 1)
        act.activation(f_w[F_ROWS, 1, :], f_w[F_ROWS, 0, :], ACT.Abs).then_inc(act_step, 1)
        chain.fixed += 1
        act.wait_ge(act_step, chain.fixed)
        act.activation(f_w[F_ROWS, 2, :], f_w[F_ROWS, 1, :], ACT.Exp, scale=-1.0).then_inc(f_e, 1)
        act.wait_ge(f_l, 1)
        act.activation(f_w[F_ROWS, 1, :], f_w[F_ROWS, 3, :], ACT.Ln).then_inc(f_e, 1)

        def plain_units(u0, units, scale=1.0):
            with act.Fori(0, units // 2) as i:
                for e in range(2):
                    for j in range(SLOTS):
                        split_high(u0 + e + 1 + i * 2, j)
                    take_lo(u0 + e + i * 2, None, (u0 + e) % 2, scale)

        plain_units(U_QI, 4)

        def indexer_units(u0, scale, step0):
            with act.Fori(0, 2) as i:
                for e in range(2):
                    step = step0 + e + i * 2
                    for j in range(SLOTS):
                        split_high(u0 + e + 1 + i * 2, j)
                    take_lo(u0 + e + i * 2, None, (u0 + e) % 2, scale)
                    act.wait_ge(dots_done, FREE + 1 + step)
                    act.wait_ge(idx_done, FREE + step)
                    act.activation(relu_sb[:, 0:TOK], side[:, 0, 0:TOK], ACT.Relu).then_inc(relu_done, 1)
                    act.activation(relu_sb[:, TOK:3 * TOK], side[:, 1, :], ACT.Relu).then_inc(relu_done, 1)

        indexer_units(U_QB, SCALE, 0)
        indexer_units(U_KB, 1.0, 4)
        with act.Fori(0, 4) as i:
            for j in range(SLOTS):
                split_high(U_VB + 1 + i, j)

        def head_units(u0, head0):
            with act.Fori(0, 4) as i:
                for e in range(2):
                    head = head0 + e + i * 2
                    act.wait_ge(max_ready, 2 * head + 2)
                    for b, cols in enumerate((slice(0, P), slice(P, CAT))):
                        act.activation(lg[:, cols], lg[:, cols], ACT.Exp, bias=neg_max[:, b:b + 1],
                                       accum_out=sums[:, b:b + 1]).then_inc(exp_done, 1)
                    split_high(u0 + e + 1 + i * 2, 0)
                    split_high(u0 + e + 1 + i * 2, 1)
                    split_high(u0 + e + 1 + i * 2, 2)
                    act.wait_ge(pt_done, head + 1)
                    act.activation(pt[:, :], side[:, 2, 0:CAT], ACT.Copy).then_inc(pt_ready, 1)
                    split_high(u0 + e + 1 + i * 2, 3)
                    take_lo(u0 + e + i * 2, None, (u0 + e) % 2)
                    act.wait_ge(pv_done, FREE + 1 + head)
                    tile = (KT_O if head0 == 0 else -HB) + head
                    act.activation(heads_o[:, ds(tile, 1), 0:TOK], side[:, 3, 0:TOK], ACT.Copy).then_inc(o_high, 1)

        head_units(U_GA, 0)
        plain_units(U_QA, 4, SCALE)
        for j in range(SLOTS):
            split_high(U_KA + 1, j)
        take_lo(U_KA, None, U_KA % 2)
        for j in range(SLOTS):
            split_high(U_VA + 1, j)
        head_units(U_GB, HB)

        with act.Fori(0, 4) as i:
            for e in range(2):
                u = U_WO + e + i * 2
                both = gates[:, :, ds((e + i * 2) * 2, 2), :]
                act.wait_ge(combined, U_WO)
                for b in range(2):
                    act.activation(both[:, b], both[:, b], ACT.Sigmoid).then_inc(gate_ready, 1)
                for j in range(SLOTS):
                    split_high(u + 1, j)
                pair = (U_WO + e) % 2
                take_lo(u, None, pair)
                take_lo(u, None, pair, 1.0, side, lo_b[:, pair, :])
                act.wait_ge(mix_s, 1 + e + i * 2)
                act.activation(mixed[:, ds((e + i * 2) * 2, 2), 0:TOK],
                               s_a[:, :].rearrange("p (m n) -> p m n", m=2), ACT.Copy).then_inc(mix_high, 1)

        def new_x(n, gain):
            act.wait_ge(x_new, n + 1)
            tile = (n - (0 if gain == KT else 8)) * 2
            for m in range(2):
                act.activation(xg[:, ds(tile + m, 1), 0:TOK], res[:, ds(tile + m, 1), :], ACT.Copy,
                               scale=gains[:, ds(tile + (gain + m), 1)]).then_inc(xg_high, 1)

        with act.Fori(0, 4) as i:
            for e in range(2):
                for j in range(SLOTS):
                    split_high(U_OUT + e + 1 + i * 2, j)
                take_lo(U_OUT + e + i * 2, None, (U_OUT + e) % 2)
                new_x(e + i * 2, KT)
        act.wait_ge(p_t, 1)
        act.activation(p_cols[:, :, 0:TOK], side[:, 2, :].rearrange("p (m n) -> p m n", m=2), ACT.Copy).then_inc(p_high, 1)

        def root(n):
            act.wait_ge(ms_done, n)
            act.activation(sq[:, :], side[:, 0, 0:TOK], ACT.Sqrt, bias=eps[:, 0:1], scale=1.0 / D_MODEL).then_inc(ms_sqrt, 1)

        def ffn_pair(i, last=False):
            u = U_FFN + i * 2
            for j in range(SLOTS):
                split_high(u + 1, j)
            take_lo(u, None, U_FFN % 2)
            act.wait_ge(ffg_s, 1 + i)
            act.activation(silu_g[:, :], s_a[:, :], ACT.Silu).then_inc(ffg_silu, 1)
            for j in range(SLOTS):
                split_high(u + 2, j)
            take_lo(u + 1, None, (U_FFN + 1) % 2)
            act.wait_ge(ff_s, 1 + i)
            act.activation(ff[:, ds(i * 2, 2), 0:TOK], s_b[:, :].rearrange("p (m n) -> p m n", m=2),
                           ACT.Copy).then_inc(ff_high, 1)

        root(1)
        with act.Fori(0, N_FFN) as i:
            ffn_pair(i)

        with act.Fori(0, 4) as i:
            for e in range(2):
                u = U_DOWN + 3 * e + i * 6
                for j in range(SLOTS):
                    split_high(u + 1, j)
                for j in range(SLOTS):
                    split_high(u + 2, j, 3 * GROUP)
                for j in range(SLOTS):
                    split_high(u + 3, j)
                take_lo(u + 2, None, (G_DOWN + e) % 2)
                new_x(8 + e + i * 2, 2 * KT)
        for c in range(SLOTS):
            split_high(U_PLE, c)
            act.wait_ge(chunk_used, 4 * U_PROJ + c + 1)
            act.wait_ge(combined, G_PROJ + c)
            act.activation(lo[:, :, :].rearrange("p a (m n) -> p (a m) n", m=2), (side, acc)[c % 2][:, :, TOK:2 * TOK],
                           ACT.Copy).then_inc(lo_ready, 1)
        root(2)

        def ple_unit(i, e, first=False, last=False):
            n = e + i * 2
            if not last:
                for j in range(SLOTS):
                    split_high(U_PLE + 1 + n, j)
            if not first:
                take_fin(n - 1)
            take_lo(U_PLE + n, None, (G_PLE + e) % 2)
            act.wait_ge(pg_s, n + 1)
            act.activation(s_b[:, :], s_a[:, :], ACT.Sigmoid).then_inc(pg_sig, 1)
            act.wait_ge(x_new, 17 + n)
            for m in range(2):
                act.activation(fin[:, e, m, :], res[:, ds(n * 2 + m, 1), :], ACT.Copy,
                               scale=gains[:, ds(n * 2 + (3 * KT + m), 1)]).then_inc(fin_ready, 1)

        def take_fin(n):
            act.wait_ge(fin_t, n + 1)
            act.activation(out_tok[:, :, ds(n * GROUP, GROUP)], side[:, 1, :].rearrange("p (b n) -> p b n", b=2),
                           ACT.Copy).then_inc(fin_read, 1)

        ple_unit(0, 0, first=True)
        ple_unit(0, 1)
        with act.Fori(1, 3) as i:
            ple_unit(i, 0)
            ple_unit(i, 1)
        ple_unit(3, 0)
        ple_unit(3, 1, last=True)
        take_fin(7)
        act.wait_ge(tok_done, 1)
        act.activation(r_tok[:, 2:4], side[:, 2, 0:2], ACT.Sqrt, bias=eps[:, 0:1], scale=1.0 / D_MODEL).then_inc(tok_sqrt, 1)

    @block.vector
    def _(dve):
        chain = Count(dve, dve_step)

        def split_low(u, j, n=CHUNK):
            dve.wait_ge(h_split, 4 * u + j + 1)
            dve.tensor_tensor(ls[:, j, 0:n], ws[:, j, 0:n], hs[:, j, 0:n].bitcast(F32), ALU.subtract).then_inc(l_split, 1)

        def two(t):
            return t.rearrange("p (m n) -> p m n", m=2)

        def combine(dst, g, pair, lo_count, scale=1.0, tables=False):
            dve.wait_ge(lo_ready, lo_count)
            ins = dve.scalar_tensor_tensor(dst, acc[:, 2 * pair:2 * pair + 2, 0:TOK], scale, two(lo[:, pair, :]),
                                           ALU.mult, ALU.add)
            ins.then_inc(combined, 1)
            if tables:
                dve.wait_ge(rope_sin, 10)
            dve.wait_ge(combined, g + 1)

        dve.wait_ge(x_rms, 1)
        chain.step(dve.reciprocal(r_tok[:, 0:2], r_tok[:, 2:4]))
        for b in range(2):
            dve.tensor_scalar(diag[:, b, :], ident[:, :], r_tok[:, b:b + 1], None, ALU.mult).then_inc(diag_ready, 1)
        dve.wait_ge(rms_sb, 1)
        dve.wait_ge(gain_ready, 1)
        for t in range(KT // 2 + 1):
            if t < KT // 2:
                dve.wait_ge(res_ready, t + 1)
                full = (s_a, lo[:, 0, :])[t % 2]
                if t >= 2:
                    dve.wait_ge(hn_ready, t - 1)
                for m in range(2):
                    k = 2 * t + m
                    dve.scalar_tensor_tensor(full[:, m * TOK:(m + 1) * TOK], res[:, k, :], gains[:, k:k + 1], s_b[:, 0:TOK],
                                             ALU.mult, ALU.mult).then_inc(*((hn_f, 1) if m else (dve_step, 1)))
                chain.fixed += 1
            if t > 0:
                full = (s_a, lo[:, 0, :])[(t - 1) % 2]
                dve.wait_ge(hn_high, t)
                dve.tensor_tensor(hn[:, 2 * t - 2:2 * t, TOK:2 * TOK], two(full[:, 0:2 * TOK]),
                                  hn[:, 2 * t - 2:2 * t, 0:TOK].bitcast(F32), ALU.subtract).then_inc(hn_ready, 1)
            if t % 2 == 0 and t < 2 * SLOTS:
                split_low(0, t // 2)
        dve.wait_ge(const_loaded, 3 * 16)
        chain.step(dve.tensor_copy(pos_f[:, :], pos_i[:, :]))
        for k, col in enumerate((2, 0)):
            chain.step(dve.tensor_scalar(ang[:, k, :], pos_f[:, :], rope_c[:, col:col + 1], None, ALU.mult))
        two_pi = 6.283185307179586
        parts = (6.28125, 0.0019350051879882812, 3.0199159819568e-07)
        rounder = 12582912.0
        for k, quarter in enumerate((0.25, 0.0)):
            chain.step(dve.tensor_scalar(turn[:, :, :], ang[:, :, :], 1.0 / two_pi, quarter, ALU.mult, ALU.add))
            chain.step(dve.tensor_scalar(turn[:, :, :], turn[:, :, :], rounder, None, ALU.add))
            chain.step(dve.tensor_scalar(turn[:, :, :], turn[:, :, :], rounder, None, ALU.subtract))
            r = ang_r[:, 2 * k:2 * k + 2, :]
            src = ang[:, :, :]
            for part in parts:
                chain.step(dve.scalar_tensor_tensor(r, turn[:, :, :], -part, src, ALU.mult, ALU.add))
                src = r
            chain.step(dve.tensor_scalar(r, r, quarter * two_pi, 3.1415925, ALU.add, ALU.min))
            ins = dve.tensor_scalar(r, r, -3.1415925, None, ALU.max)
            if k == 0:
                chain.step(ins)
            else:
                ins.then_inc(angles, 1)
        for j in range(SLOTS):
            split_low(1, j)
        dve.wait_ge(rope_sin, 8)
        for at, col in ((1, 3), (3, 1)):
            dve.tensor_scalar(rope[:, at, :], rope[:, at, :], rope_c[:, col:col + 1], None, ALU.mult).then_inc(rope_sin, 1)

        swap_idx = [8 + i if i < 8 else i - 8 if i < 16 else i for i in range(32)]
        swap_a = [(i + 16) % 32 for i in range(32)]

        combine(two(s_a[:, :]), 0, 0, 1)
        dve.wait_ge(rope_sin, 10)
        chain.step(dve.stream_shuffle(s_b[:, 0:TOK], s_a[:, 0:TOK], swap_idx))
        chain.step(dve.tensor_tensor(s_b[:, 0:TOK], s_b[:, 0:TOK], rope[:, 1, 0:TOK], ALU.mult))
        chain.step(dve.tensor_tensor(s_b[:, TOK:2 * TOK], s_a[:, 0:TOK], rope[:, 0, 0:TOK], ALU.mult))
        for m in range(2):
            half = slice(64 * m, 64 * m + 64)
            dve.tensor_tensor(kib[half, m * TOK:(m + 1) * TOK], s_b[half, 0:TOK], s_b[half, TOK:2 * TOK],
                              ALU.add).then_inc(small_s, 1)
        dve.tensor_scalar(f_w[F_ROWS, 0, :], s_a[F_ROWS, TOK:2 * TOK], bias_f[F_ROWS, 0:1], None, ALU.add).then_inc(f_z, 1)
        dve.wait_ge(f_e, 1)
        dve.tensor_scalar(f_w[F_ROWS, 3, :], f_w[F_ROWS, 2, :], 1.0, None, ALU.add).then_inc(f_l, 1)
        dve.wait_ge(f_e, 2)
        chain.step(dve.scalar_tensor_tensor(f_w[F_ROWS, 2, :], f_w[F_ROWS, 0, :], 0.0, f_w[F_ROWS, 1, :], ALU.min, ALU.subtract))
        chain.step(dve.memset(f_w[F_ROWS, 3, :], 1.0))
        chain.step(dve.tensor_tensor_scan(c_cat[F_ROWS, P:CAT], f_w[F_ROWS, 3, :], f_w[F_ROWS, 2, :], 0.0, ALU.mult, ALU.add))
        dve.tensor_copy(c_cat[F_ROWS, 0:P], c_cat[F_ROWS, P:2 * P]).then_inc(f_c, 1)
        dve.wait_ge(f_c, 1)
        dve.wait_ge(small_t, 1)
        for b in range(2):
            chain.step(dve.tensor_scalar(w_tok[:, b, :], side[:, 2, b * P:b * P + H_IDX],
                                         H_IDX ** -0.5 * D_IDX ** -0.5, None, ALU.mult))
        chain.step(dve.memset(sel[:, :], 0.0))

        def rotate(dst, t, table, swap, mask_rows):
            rows = slice(0, mask_rows)
            chain.step(dve.stream_shuffle(s_b[rows, :], t[rows, :], swap))
            chain.step(dve.tensor_tensor(s_b[rows, :], s_b[rows, :], rope[rows, table + 1, :], ALU.mult))
            chain.step(dve.tensor_tensor(t[rows, :], t[rows, :], rope[rows, table, :], ALU.mult))
            dve.tensor_tensor(dst[rows], two(t[rows, :]), two(s_b[rows, :]), ALU.add).then_inc(rope_done, 1)

        dve.wait_ge(small_s, 2)
        with dve.Fori(0, 2) as i:
            chain.enter(i, 6)
            for e in range(2):
                g = U_QI + e + i * 2
                for j in range(SLOTS):
                    split_low(g + 1, j)
                combine(two(s_a[:, :]), g, (U_QI + e) % 2, g + 1, tables=True)
                rotate(q_idx[:, ds((e + i * 2) * 2, 2), :], s_a, 0, swap_idx, P)
                dve.wait_ge(rope_done, 1 + e + i * 2)
        chain.leave(2)

        cats = (slice(0, P), slice(P, CAT))

        def indexer_units(u0, dst, scale, step0):
            with dve.Fori(0, 2) as i:
                chain.enter(i, 6)
                for e in range(2):
                    step = step0 + e + i * 2
                    g = u0 + e + i * 2
                    for j in range(SLOTS):
                        split_low(g + 1, j)
                    combine(dst[:, ds((e + i * 2) * 2, 2), :], g, (u0 + e) % 2, g + 1, scale)
                    dve.wait_ge(relu_done, FREE + 2 + step * 2)
                    for hh in range(2):
                        w_col = step * 2 + hh
                        dots = (relu_sb[:, hh * P:(hh + 1) * P], relu_sb[:, TOK * (1 + hh):TOK * (2 + hh)])
                        for b in range(2):
                            ins = dve.scalar_tensor_tensor(sel[:, cats[b]], dots[b], w_tok[:, b, ds(w_col, 1)],
                                                           sel[:, cats[b]], ALU.mult, ALU.add)
                            if hh == 1 and b == 1:
                                ins.then_inc(idx_done, 1)
                                dve.wait_ge(idx_done, FREE + 1 + step)
                            else:
                                chain.step(ins)
            chain.leave(2)

        indexer_units(U_QB, q_cols, SCALE, 0)
        indexer_units(U_KB, k_cols, 1.0, 4)
        chain.step(dve.tensor_tensor(sel[:, :], sel[:, :], mask[:, :], ALU.add))

        dve.wait_ge(c_t, 1)
        for b in range(2):
            chain.step(dve.tensor_copy(c_tok[:, b, :], side[:, 3, b * P + F_ROW:b * P + F_ROW + HB]))
        dve.tensor_scalar(cm[:, :], c_cat[:, :], neg_id[:, F_ROW:F_ROW + 1], None, ALU.mult).then_inc(cm_ready, 1)

        for i in range(4):
            g = U_VB + i
            for _ in range(TOP_K // 8 // 4):
                for b in range(2):
                    chain.step(dve.max(top8[:, b, :], sel[:, cats[b]]))
                    chain.step(dve.match_replace(sel[:, cats[b]], top8[:, b, :], sel[:, cats[b]], TAKEN))
            for j in range(SLOTS):
                split_low(g + 1, j)
            dve.wait_ge(chunk_used, 4 * g + 4)
            dve.tensor_copy(v_rows[:, :, i * GROUP:(i + 1) * GROUP],
                            acc[:, 2 * (g % 2):2 * (g % 2) + 2, 0:TOK]).then_inc(combined, 1)
        chain.step(dve.tensor_scalar(sel[:, :], sel[:, :], TAKEN_BELOW, 1.0, ALU.is_le, ALU.subtract))
        chain.step(dve.scalar_tensor_tensor(sel[:, :], sel[:, :], -MASKED, mask[:, :], ALU.mult, ALU.min))

        def head_units(u0, head0, lo_off, per_pass):
            forget = head0 == 0
            with dve.Fori(0, 4) as i:
                chain.enter(i, per_pass)
                for e in range(2):
                    h = e + i * 2
                    head = head0 + h
                    g = u0 + h
                    dve.wait_ge(qk_done, FREE + 1 + head)
                    if forget:
                        chain.step(dve.tensor_tensor(lg[:, :], side[:, 1, 0:CAT], mask[:, :], ALU.add))
                        for b in range(2):
                            chain.step(dve.scalar_tensor_tensor(lg[:, cats[b]], side[:, 0, cats[b]], c_tok[:, b, ds(h, 1)],
                                                                lg[:, cats[b]], ALU.add, ALU.add))
                        dve.tensor_scalar(cm[:, :], c_cat[:, :], neg_id[:, ds(h + (F_ROW + 1), 1)], None, ALU.mult).then_inc(cm_ready, 1)
                    else:
                        chain.step(dve.tensor_tensor(lg[:, :], side[:, 0, 0:CAT], sel[:, :], ALU.add))
                    for b in range(2):
                        dve.tensor_reduce(neg_max[:, b:b + 1], lg[:, cats[b]], AX_X, ALU.max, negate=True).then_inc(max_ready, 1)
                    dve.wait_ge(exp_done, 2 * head + 2)
                    chain.step(dve.reciprocal(rsum[:, :], sums[:, :]))
                    for b in range(2):
                        dve.tensor_scalar(lg[:, cats[b]], lg[:, cats[b]], rsum[:, b:b + 1], None, ALU.mult).then_inc(prob_ready, 1)
                    for j in range(SLOTS):
                        split_low(g + 1, j)
                    combine(gates[:, head0 // HB, ds(h * 2, 2), :], g, (u0 + e) % 2, g + 1 - lo_off)
                    dve.wait_ge(o_high, head + 1)
                    tile = (KT_O if forget else 0) + h
                    dve.tensor_tensor(heads_o[:, ds(tile, 1), TOK:2 * TOK], side[:, 3:4, 0:TOK],
                                      heads_o[:, ds(tile, 1), 0:TOK].bitcast(F32), ALU.subtract).then_inc(o_ready, 1)
            chain.leave(4)

        head_units(U_GA, 0, 4, 8)

        def rotate_a(dst):
            rows = slice(0, ROT_A)
            chain.step(dve.stream_shuffle(s_b[rows, :], s_a[rows, :], swap_a))
            chain.step(dve.tensor_tensor(s_b[rows, :], s_b[rows, :], rope[rows, 3, :], ALU.mult))
            chain.step(dve.tensor_tensor(s_a[rows, :], s_a[rows, :], rope[rows, 2, :], ALU.mult))
            chain.step(dve.tensor_tensor(s_a[rows, :], s_a[rows, :], s_b[rows, :], ALU.add))
            dve.tensor_copy(dst, two(s_a[:, :])).then_inc(rope_done, 1)

        with dve.Fori(0, 2) as i:
            chain.enter(i, 8)
            for e in range(2):
                g = U_QA + e + i * 2
                for j in range(SLOTS):
                    split_low(g + 1, j)
                dve.wait_ge(rope_done, 4 + e + i * 2)
                combine(two(s_a[:, :]), g, (U_QA + e) % 2, g + 1 - 4, SCALE, tables=True)
                rotate_a(q_cols[:, ds((e + i * 2) * 2, 2), :])
        chain.leave(2)
        for j in range(SLOTS):
            split_low(U_KA + 1, j)
        dve.wait_ge(rope_done, 8)
        combine(two(s_a[:, :]), U_KA, U_KA % 2, U_KA + 1 - 4)
        rotate_a(k_cols[:, 0:2, :])
        dve.wait_ge(rope_done, 9)
        for j in range(SLOTS):
            split_low(U_VA + 1, j)
        dve.wait_ge(chunk_used, 4 * U_VA + 4)
        pair = U_VA % 2
        dve.wait_ge(v_staged, HB)
        dve.tensor_copy(v_rows[:, :, 0:GROUP], acc[:, 2 * pair:2 * pair + 2, 0:TOK]).then_inc(combined, 1)
        head_units(U_GB, HB, 5, 4)

        with dve.Fori(0, 4) as i:
            chain.enter(i, 6)
            for e in range(2):
                n = e + i * 2
                g = U_WO + n
                for j in range(SLOTS):
                    split_low(g + 1, j)
                pair = (U_WO + e) % 2
                dve.wait_ge(lo_ready, U_WO - 5 + 1 + n * 2)
                chain.step(dve.tensor_tensor(two(s_a[:, :]), acc[:, 2 * pair:2 * pair + 2, 0:TOK], two(lo[:, pair, :]), ALU.add))
                dve.wait_ge(lo_ready, U_WO - 5 + 2 + n * 2)
                dve.tensor_tensor(two(s_b[:, :]), side[:, 2 * pair:2 * pair + 2, 0:TOK], two(lo_b[:, pair, :]),
                                  ALU.add).then_inc(combined, 1)
                dve.wait_ge(gate_ready, 2 * n + 2)
                chain.step(dve.tensor_tensor(two(s_a[:, :]), two(s_a[:, :]), gates[:, 1, ds(n * 2, 2), :], ALU.mult))
                dve.wait_ge(combined, g + 1)
                chain.step(dve.tensor_tensor(two(s_b[:, :]), two(s_b[:, :]), gates[:, 0, ds(n * 2, 2), :], ALU.mult))
                dve.tensor_tensor(s_a[:, :], s_a[:, :], s_b[:, :], ALU.add).then_inc(mix_s, 1)
                dve.wait_ge(mix_high, n + 1)
                dve.tensor_tensor(mixed[:, ds(n * 2, 2), TOK:2 * TOK], two(s_a[:, :]),
                                  mixed[:, ds(n * 2, 2), 0:TOK].bitcast(F32), ALU.subtract).then_inc(mix_ready, 1)
                dve.wait_ge(mix_ready, n + 1)
        chain.leave(4)

        LO_OUT = U_OUT - 5 + 8

        def new_x(n, n0, gain):
            tile = (n - n0) * 2
            dve.tensor_tensor(res[:, ds(tile, 2), :], two(s_a[:, :]), res[:, ds(tile, 2), :], ALU.add).then_inc(x_new, 1)
            dve.wait_ge(xg_high, 2 * n + 2)
            for m in range(2):
                dve.scalar_tensor_tensor(xg[:, ds(tile + m, 1), TOK:2 * TOK], res[:, ds(tile + m, 1), :],
                                         gains[:, ds(tile + (gain + m), 1)], xg[:, ds(tile + m, 1), 0:TOK].bitcast(F32),
                                         ALU.mult, ALU.subtract).then_inc(xg_ready, 1)

        with dve.Fori(0, 4) as i:
            for e in range(2):
                n = e + i * 2
                for j in range(SLOTS):
                    split_low(U_OUT + 1 + n, j)
                combine(two(s_a[:, :]), U_OUT + n, (U_OUT + e) % 2, LO_OUT + 1 + n)
                new_x(n, 0, KT)
        dve.wait_ge(p_high, 1)
        dve.tensor_tensor(p_cols[:, :, TOK:2 * TOK], two(side[:, 2, :]), p_cols[:, :, 0:TOK].bitcast(F32),
                          ALU.subtract).then_inc(p_ready, 1)

        def reciprocal_rms(n):
            dve.wait_ge(ms_sqrt, n)
            for d in range(2):
                dve.reciprocal(rms[:, d * TOK:(d + 1) * TOK], sq[:, :]).then_inc(rms_ready, 1)
            dve.wait_ge(rms_ready, 2 * n)

        reciprocal_rms(1)
        LO_FFN = LO_OUT + 8
        dve.wait_ge(x_new, 8)
        with dve.Fori(0, N_FFN) as i:
            chain.enter(i, 1)
            g = U_FFN + i * 2
            for j in range(SLOTS):
                split_low(g + 1, j)
            combine(two(s_a[:, :]), g, U_FFN % 2, LO_FFN + 1 + i * 2)
            dve.tensor_tensor(s_a[:, :], s_a[:, :], rms[:, :], ALU.mult).then_inc(ffg_s, 1)
            for j in range(SLOTS):
                split_low(g + 2, j)
            combine(two(s_b[:, :]), g + 1, (U_FFN + 1) % 2, LO_FFN + 2 + i * 2)
            chain.step(dve.tensor_tensor(s_b[:, :], s_b[:, :], rms[:, :], ALU.mult))
            dve.wait_ge(ffg_silu, 1 + i)
            dve.tensor_tensor(s_b[:, :], s_b[:, :], silu_g[:, :], ALU.mult).then_inc(ff_s, 1)
            dve.wait_ge(ff_high, 1 + i)
            dve.tensor_tensor(ff[:, ds(i * 2, 2), TOK:2 * TOK], two(s_b[:, :]), ff[:, ds(i * 2, 2), 0:TOK].bitcast(F32),
                              ALU.subtract).then_inc(ff_ready, 1)
            dve.wait_ge(ff_ready, 1 + i)
        chain.leave(N_FFN)

        LO_DOWN = LO_FFN + 2 * N_FFN
        with dve.Fori(0, 4) as i:
            for e in range(2):
                u = U_DOWN + 3 * e + i * 6
                n = e + i * 2
                for j in range(SLOTS):
                    split_low(u + 1, j)
                for j in range(SLOTS):
                    split_low(u + 2, j, 3 * GROUP)
                for j in range(SLOTS):
                    split_low(u + 3, j)
                combine(two(s_a[:, :]), G_DOWN + n, (G_DOWN + e) % 2, LO_DOWN + 1 + n)
                new_x(8 + n, 8, 2 * KT)
        LO_PROJ = LO_DOWN + 8
        dve.wait_ge(x_new, 16)
        for c in range(SLOTS):
            split_low(U_PLE, c)
            dve.wait_ge(lo_ready, LO_PROJ + 1 + c)
            dve.tensor_tensor(y_ple[:, 4 * c:4 * c + 4, :], (side, acc)[c % 2][:, :, 0:TOK],
                              lo[:, :, :].rearrange("p a (m n) -> p (a m) n", m=2), ALU.add).then_inc(combined, 1)
        reciprocal_rms(2)
        LO_PLE = LO_PROJ + SLOTS

        def ple_unit(i, e, last=False):
            n = e + i * 2
            if not last:
                for j in range(SLOTS):
                    split_low(U_PLE + 1 + n, j)
            combine(two(s_a[:, :]), G_PLE + n, (G_PLE + e) % 2, LO_PLE + 1 + n)
            dve.tensor_tensor(s_a[:, :], s_a[:, :], rms[:, :], ALU.mult).then_inc(pg_s, 1)
            dve.wait_ge(pg_sig, n + 1)
            chain.step(dve.tensor_tensor(two(s_b[:, :]), two(s_b[:, :]), y_ple[:, ds(n * 2, 2), :], ALU.mult))
            dve.tensor_tensor(res[:, ds(n * 2, 2), :], two(s_b[:, :]), res[:, ds(n * 2, 2), :], ALU.add).then_inc(x_new, 1)

        with dve.Fori(0, 3) as i:
            chain.enter(i, 2)
            ple_unit(i, 0)
            ple_unit(i, 1)
        chain.leave(3)
        ple_unit(3, 0)
        ple_unit(3, 1, last=True)
        dve.wait_ge(tok_sqrt, 1)
        chain.step(dve.reciprocal(r_tok[:, 0:2], r_tok[:, 2:4]))
        dve.wait_ge(fin_read, 8)
        for n in range(4):
            half = slice(D_MODEL // 2 * (n // 2), D_MODEL // 2 * (n // 2 + 1))
            dve.tensor_scalar(out_tok[:, n % 2, half], out_tok[:, n % 2, half], r_tok[:, n % 2:n % 2 + 1], None,
                              ALU.mult).then_inc(y_ready, 1)

    @block.tensor
    def _(pe):
        def bank_free(g):
            pe.wait_ge(combined, g - 1)

        def consume(u, j, bank, banks, tiles, src, first, last, width=GROUP, col=0, signal=True, wait=True):
            if wait:
                pe.wait_ge(l_split, 4 * u + j + 1)
            for m in range(banks):
                for q, k in enumerate(tiles):
                    at = slice(q * width + col + m * P, q * width + col + (m + 1) * P)
                    begins, ends = first and q == 0, last and q == len(tiles) - 1
                    high, low = (hs[:, j, at], src[:, k, :]), (ls[:, j, at], src[:, k, 0:TOK])
                    whole, half = acc_of(bank + m, 2 * TOK), acc_of(bank + m, TOK)
                    if ends:
                        pe.matmul(half, *low, start=False, stop=False)
                        mm = pe.matmul(whole, *high, start=False, stop=True)
                    else:
                        pe.matmul(whole, *high, start=begins, stop=False)
                        mm = pe.matmul(half, *low, start=False, stop=False)
            if signal:
                mm.then_inc(chunk_used, 1)

        def acc_of(bank, n):
            return (acc if bank < 4 else side)[:, bank % 4, 0:n]

        def unit(u, g, src, pair, between=None, needs=None):
            if not isinstance(g, int) or g >= 2:
                bank_free(g)
            for j in range(SLOTS):
                if needs is not None:
                    pe.wait_ge(needs[0], needs[1](j))
                consume(u, j, 2 * pair, 2, range(KC * j, KC * j + KC), src, j == 0, j == 3)
                if between is not None and j == between[0]:
                    between[1]()

        pe.wait_ge(gains_loaded, 4 * 16)
        pe.wait_ge(consts, 10)
        pe.transpose(side[:, 0, 0:4 * KT], gain_rows[0:4 * KT, :], ident[0:4 * KT, 0:4 * KT]).then_inc(gain_t, 1)

        def x_transposes(t):
            if t >= 4:
                pe.wait_ge(res_ready, t - 3)
            for m in range(2):
                for b in range(2):
                    mm = pe.transpose(acc[:, t % 4, m * TOK + b * P:m * TOK + (b + 1) * P],
                                      x_tok[:, b, (2 * t + m) * P:(2 * t + m + 1) * P], ident[:, :])
            mm.then_inc(x_t, 1)

        for b in range(2):
            pe.wait_ge(x_loaded[b], 16)
        for t in range(4):
            x_transposes(t)
        pe.wait_ge(diag_ready, 2)
        for b in range(2):
            mm = pe.matmul(side[:, 1, b * P:(b + 1) * P], ones[:, :], diag[:, b, :], start=True, stop=True)
        mm.then_inc(rms_b, 1)
        for t in range(4, KT // 2):
            x_transposes(t)

        pe.wait_ge(res_ready, KT // 2)
        for j in range(SLOTS):
            pe.wait_ge(hn_ready, 2 * j + 2)
            consume(0, j, 0, 2, range(KC * j, KC * j + KC), hn, j == 0, j == 3)

        def small_by_token():
            pe.wait_ge(combined, 1)
            for b in range(2):
                mm = pe.transpose(side[:, 2, b * P:(b + 1) * P], s_a[:, TOK + b * P:TOK + (b + 1) * P], ident[:, :])
            mm.then_inc(small_t, 1)

        unit(U_QI, U_QI, hn, U_QI % 2, between=(1, small_by_token))

        def decay_by_token():
            pe.wait_ge(f_c, 1)
            for b in range(2):
                mm = pe.transpose(side[:, 3, b * P:(b + 1) * P], c_cat[:, (1 + b) * P:(2 + b) * P], ident[:, :])
            mm.then_inc(c_t, 1)

        unit(U_QI + 1, U_QI + 1, hn, (U_QI + 1) % 2, between=(1, decay_by_token))
        for e in range(2, 4):
            unit(U_QI + e, U_QI + e, hn, (U_QI + e) % 2)

        def dots(step):
            pe.wait_ge(staged, step + 1)
            pe.wait_ge(relu_done, FREE + step * 2)
            keys = kib[:, :].rearrange("p (h n) -> p h n", h=2)
            pe.matmul(side[:, 0, 0:TOK].rearrange("p (h n) -> p h n", h=2), q_st[:, 0:P], keys[:, :, 0:P], start=True, stop=True)
            pe.matmul(side[:, 1, :], q_st[:, P:TOK], kib[:, :], start=True, stop=True).then_inc(dots_done, 1)

        pe.wait_ge(small_s, 2)
        with pe.Fori(0, 4) as i:
            for e in range(2):
                n = e + i * 2
                unit(U_QB + n, U_QB + n, hn, (U_QB + e) % 2)
                dots(n)

        def by_token(u, pair):
            bank_free(u)
            for j in range(SLOTS):
                pe.wait_ge(l_split, 4 * u + j + 1)
                for t in range(2):
                    for q in range(KC):
                        k = KC * j + q
                        wh, wl = hs[:, j, q * GROUP:(q + 1) * GROUP], ls[:, j, q * GROUP:(q + 1) * GROUP]
                        xh, xl = hn[:, k, t * P:(t + 1) * P], hn[:, k, TOK + t * P:TOK + (t + 1) * P]
                        dst = acc[:, 2 * pair + t, 0:TOK]
                        pe.matmul(dst, xh, wh, start=k == 0, stop=False)
                        pe.matmul(dst, xh, wl, start=False, stop=False)
                        mm = pe.matmul(dst, xl, wh, start=False, stop=k == KT - 1)
                mm.then_inc(chunk_used, 1)

        with pe.Fori(0, 2) as i:
            for e in range(2):
                by_token(U_VB + e + i * 2, (U_VB + e) % 2)

        def scores(head, forget):
            pe.wait_ge(staged, STEPS_IDX + 2 + head * 2)
            pe.wait_ge(prob_ready, FREE + head * 2)
            if forget:
                pe.wait_ge(cm_ready, head + 1)
                pe.matmul(side[:, 1, 0:CAT], ones[:, :], cm[:, :], start=True, stop=True)
            pe.matmul(side[:, 0, 0:P], q_st[:, 0:P], k_st[:, 0:P], start=True, stop=True)
            pe.matmul(side[:, 0, P:CAT], q_st[:, P:TOK], k_st[:, :], start=True, stop=True).then_inc(qk_done, 1)

        def probs_by_key(head):
            pe.wait_ge(prob_ready, FREE + 2 + head * 2)
            pe.wait_ge(pt_ready, FREE + head)
            for c in range(3):
                mm = pe.transpose(side[:, 2, c * P:(c + 1) * P], lg[:, c * P:(c + 1) * P], ident[:, :])
            mm.then_inc(pt_done, 1)

        def values(head):
            pe.wait_ge(pt_ready, FREE + 1 + head)
            pe.wait_ge(v_staged, head + 1)
            pe.wait_ge(o_ready, FREE + head)
            pe.matmul(side[:, 3, 0:P], v_st[:, 0, :], pt[:, 0:P], start=True, stop=True)
            pe.matmul(side[:, 3, P:TOK], v_st[:, 0, :], pt[:, P:2 * P], start=True, stop=False)
            pe.matmul(side[:, 3, P:TOK], v_st[:, 1, :], pt[:, 2 * P:CAT], start=False, stop=True).then_inc(pv_done, 1)

        def head_units(u0, head0):
            forget = head0 == 0
            scores(head0, forget)

            def two_heads(i, last=False):
                for e in range(2):
                    h = e + i * 2

                    def between():
                        probs_by_key(head0 + h)
                        if not (last and e == 1):
                            scores(head0 + h + 1, forget)

                    unit(u0 + h, u0 + h, hn, (u0 + e) % 2, between=(2, between))
                    values(head0 + h)

            with pe.Fori(0, 3) as i:
                two_heads(i)
            two_heads(3, last=True)

        head_units(U_GA, 0)
        with pe.Fori(0, 2) as i:
            for e in range(2):
                unit(U_QA + e + i * 2, U_QA + e + i * 2, hn, (U_QA + e) % 2)
        unit(U_KA, U_KA, hn, U_KA % 2)
        by_token(U_VA, U_VA % 2)
        head_units(U_GB, HB)

        def merge_units(i, first=False):
            for e in range(2):
                u = U_WO + e + i * 2
                pair = (U_WO + e) % 2
                bank_free(u)
                for j in range(SLOTS):
                    if first and e == 0 and j == 2:
                        pe.wait_ge(o_ready, FREE + HEADS)
                    t = KC * ((j + 2) % SLOTS)
                    consume(u, j, 2 * pair + 4 * (j // 2), 2, range(t, t + KC), heads_o, j % 2 == 0, j % 2 == 1)

        merge_units(0, first=True)
        with pe.Fori(1, 4) as i:
            merge_units(i)

        def out_units(i, needs=None):
            for e in range(2):
                unit(U_OUT + e + i * 2, U_OUT + e + i * 2, mixed, (U_OUT + e) % 2, needs=None if e else needs)

        out_units(0, needs=(mix_ready, lambda j: 2 * j + 2))
        with pe.Fori(1, 4) as i:
            out_units(i)
        pe.wait_ge(p_loaded, 16)
        for t in range(KT_PLE):
            for b in range(2):
                mm = pe.transpose(side[:, 2, t * TOK + b * P:t * TOK + (b + 1) * P], p_tok[:, b, t * P:(t + 1) * P], ident[:, :])
        mm.then_inc(p_t, 1)

        def mean_squares(n):
            pe.wait_ge(sq_done, 8 * n)
            pe.matmul(side[:, 0, 0:TOK], ones[:, :], sq_sum[:, 0:TOK], start=True, stop=False)
            pe.matmul(side[:, 0, 0:TOK], ones[:, :], sq_sum[:, TOK:2 * TOK], start=False, stop=True).then_inc(ms_done, 1)

        def ffn_pair(i, first=False):
            for e in range(2):
                opening = first and e == 0
                unit(U_FFN + e + i * 2, U_FFN + e + i * 2, xg, (U_FFN + e) % 2,
                     needs=(xg_ready, lambda j: 4 * j + 4) if opening else None,
                     between=(3, lambda: mean_squares(1)) if opening else None)

        ffn_pair(0, first=True)
        with pe.Fori(1, N_FFN) as i:
            ffn_pair(i)

        def down_groups(i, first=False):
            for e in range(2):
                bank_free(G_DOWN + e + i * 2)
                t = 0
                for c, n in enumerate(DOWN_TILES):
                    if first and e == 0:
                        pe.wait_ge(ff_ready, (t + n + 1) // 2)
                    consume(U_DOWN + 3 * e + c // SLOTS + i * 6, c % SLOTS, 2 * ((G_DOWN + e) % 2), 2,
                            range(t, t + n), ff, c == 0, c == len(DOWN_TILES) - 1)
                    t += n

        down_groups(0, first=True)
        with pe.Fori(1, 4) as i:
            down_groups(i)
        pe.wait_ge(p_ready, 1)
        for c in range(SLOTS):
            if c > 0:
                pe.wait_ge(combined, G_PROJ + c - 1)
            consume(U_PROJ, c, 4 * (1 - c % 2), 4, range(KT_PLE), p_cols, True, True, width=2 * GROUP)
        pe.wait_ge(combined, G_PLE)

        def final_t(n, par):
            pe.wait_ge(fin_ready, 2 * n + 2)
            if not isinstance(n, int) or n > 0:
                pe.wait_ge(fin_read, n)
            for b in range(2):
                for m in range(2):
                    mm = pe.transpose(side[:, 1, b * TOK + m * P:b * TOK + (m + 1) * P], fin[:, par, m, b * P:(b + 1) * P], ident[:, :])
            mm.then_inc(fin_t, 1)

        def ple_unit(i, e, first=False):
            n = e + i * 2
            unit(U_PLE + n, G_PLE + n, xg, (G_PLE + e) % 2,
                 needs=(xg_ready, lambda j: 16 + 4 * j + 4) if first else None,
                 between=(3, (lambda: mean_squares(2)) if first else (lambda: final_t(n - 1, 1 - e))))

        ple_unit(0, 0, first=True)
        ple_unit(0, 1)
        with pe.Fori(1, 4) as i:
            ple_unit(i, 0)
            ple_unit(i, 1)
        final_t(7, 1)
        pe.wait_ge(sq_done, 24)
        for b in range(2):
            for m in range(2):
                mm = pe.matmul(side[:, 2, b:b + 1], sq_sum[:, m * TOK + b * P:m * TOK + (b + 1) * P], ones[:, 0:1],
                               start=m == 0, stop=m == 1)
        mm.then_inc(tok_done, 1)

    block.__exit__(None, None, None)


def rope_constants():
    import numpy as np

    rows = np.zeros((P, 4), np.float32)

    def frequencies(half):
        return np.float32(THETA) ** (-np.arange(half, dtype=np.float32) / np.float32(half))

    for rot, col, starts in ((ROT_A, 0, (0,)), (ROT_IDX, 2, (0, D_IDX))):
        half = rot // 2
        for at in starts:
            for side in range(2):
                rows[at + side * half:at + (side + 1) * half, col] = frequencies(half)
                rows[at + side * half:at + (side + 1) * half, col + 1] = 1.0 if side else -1.0
    return rows


_INS = ["x", "p", "positions", "g_mix", "w_in", "b_f", "w_o_a", "w_o_b", "w_out", "g_ffn", "w_ffn_gate",
        "w_ffn_up", "w_ffn_down", "g_ple", "w_ple_gate", "w_ple_proj", "g_final"]


def kernel(**inputs):
    import numpy as np
    import concourse.bacc as bacc
    from concourse.bass_utils import run_bass_kernel_spmd

    nc = bacc.Bacc("TRN2", target_bir_lowering=False, num_devices=1)
    arrays, args = {}, []
    for name in [*_INS, "rope_rows"]:
        a = rope_constants() if name == "rope_rows" else np.ascontiguousarray(inputs[name])
        arrays[f"in_{name}"] = a
        args.append(nc.dram_tensor(f"in_{name}", a.shape, mybir.dt.from_np(a.dtype), kind="ExternalInput").ap())
    out = nc.dram_tensor("out_0", inputs["x"].shape, F32, kind="ExternalOutput").ap()
    hybrid_layer(nc, *args, out)
    r = run_bass_kernel_spmd(nc, [arrays], core_ids=[0])
    return np.asarray(r.results[0]["out_0"])
```

```python
import concourse.bass as bass
from concourse import mybir

F32 = mybir.dt.float32
F32R = mybir.dt.float32r
I32 = mybir.dt.int32
ALU = mybir.AluOpType
ACT = mybir.ActivationFunctionType
AX_X = mybir.AxisListType.X
ds = bass.ds

P = 128
D_MODEL, TOK, D_FF, D_PLE = 2048, 256, 5632, 256
HA, HA_KV, H_IDX, D_IDX, HB, HEAD = 8, 2, 16, 64, 8, 128
ROT_A, ROT_IDX, THETA = HEAD // 4, D_IDX // 4, 500000.0
TOP_K = 64
EPS = 1e-6
KT = D_MODEL // P
KT_O = HA * HEAD // P
KT_FF = D_FF // P
KT_PLE = D_PLE // P
GROUP = 256
SLOTS = 4
KC = 4
CHUNK = KC * GROUP
SCALE = HEAD ** -0.5
MASKED = -3.0e38
TAKEN = -3.4e38
TAKEN_BELOW = -3.2e38
FREE = 1
CAT = P + TOK

AT_QA = 0
AT_KA = AT_QA + HA * HEAD
AT_VA = AT_KA + HA_KV * HEAD
AT_QI = AT_VA + HA_KV * HEAD
AT_KI = AT_QI + H_IDX * D_IDX
AT_WI = AT_KI + D_IDX
AT_QB = AT_WI + H_IDX
AT_KB = AT_QB + HB * HEAD
AT_VB = AT_KB + HB * HEAD
AT_FB = AT_VB + HB * HEAD
AT_GA = AT_FB + HB
AT_GB = AT_GA + D_MODEL

U_SMALL = 0
U_QI = U_SMALL + 1
U_QB = U_QI + 4
U_KB = U_QB + 4
U_VB = U_KB + 4
U_GA = U_VB + 4
U_QA = U_GA + 8
U_KA = U_QA + 4
U_VA = U_KA + 1
U_GB = U_VA + 1
U_WO = U_GB + 8
U_OUT = U_WO + 8
U_FFN = U_OUT + 8
N_FFN = D_FF // GROUP
U_DOWN = U_FFN + 2 * N_FFN
U_PROJ = U_DOWN + 3 * 8
U_PLE = U_PROJ + 1
U_END = U_PLE + 8
G_DOWN = U_DOWN
G_PROJ = G_DOWN + 8
G_PLE = G_PROJ + 2 * SLOTS
HALVES = (G_PLE % 2, 1 - G_PLE % 2)
G_END = G_PLE + 8
DOWN_TILES = [4] * 8 + [3] * 4
HEADS = HB + HA
W_ROW = D_IDX
F_ROW = 96
F_ROWS = slice(F_ROW, F_ROW + HB)
SMALL = KC * P
STEPS_IDX = H_IDX * D_IDX // P


class Count:

    def __init__(self, eng, sem):
        self.eng, self.sem, self.fixed, self.moving = eng, sem, 0, 0

    def step(self, ins):
        ins.then_inc(self.sem, 1)
        self.fixed += 1
        self.eng.wait_ge(self.sem, self.moving + self.fixed)

    def enter(self, i, steps, first=0):
        self.fixed -= first * steps
        self.start, self.steps, self.moving = self.fixed, steps, i * steps

    def leave(self, end):
        assert self.fixed - self.start == self.steps, self.fixed - self.start
        self.fixed, self.moving = self.start + end * self.steps, 0


def hybrid_layer(nc, x, p, positions, g_mix, w_in, b_f, w_o_a, w_o_b, w_out, g_ffn, w_ffn_gate,
                 w_ffn_up, w_ffn_down, g_ple, w_ple_gate, w_ple_proj, g_final, rope_rows, out):
    x_rows = x[0].rearrange("(b q) n -> q b n", q=P)
    p_rows = p[0, 0].rearrange("(b q) n -> q b n", q=P)
    out_rows = out[0].rearrange("(b q) n -> q b n", q=P)

    def tiles_of(w):
        return w[0].rearrange("(t q) n -> q t n", q=P)

    win_t, woa_t, wob_t, wout_t = map(tiles_of, (w_in, w_o_a, w_o_b, w_out))
    wgate_t, wup_t, wdown_t = map(tiles_of, (w_ffn_gate, w_ffn_up, w_ffn_down))
    wpg_t, wpp_t = map(tiles_of, (w_ple_gate, w_ple_proj))

    base = (nc.sbuf_base + 31) // 32 * 32

    def sb(name, kb, shape, dt=F32):
        return nc.alloc_sbuf_tensor_at(name, [P, *shape], dt, offset=base + int(kb * 1024))

    res = sb("res", 0, [KT, TOK])
    heads_o = sb("heads_o", 16, [KT, 2 * TOK], F32R)
    xg = sb("xg", 16, [KT, 2 * TOK], F32R)
    hn = sb("hn", 48, [KT, 2 * TOK], F32R)
    mixed = sb("mixed", 48, [KT, 2 * TOK], F32R)
    ff = sb("ff", 48, [KT_FF, 2 * TOK], F32R)
    gates = sb("gates", 80, [2, KT, TOK])
    q_idx = sb("q_idx", 80, [KT_O, TOK])
    rope = sb("rope", 104, [4, 2 * TOK])
    ang = sb("ang", 88, [2, TOK])
    ang_r = sb("ang_r", 90, [4, TOK])
    turn = sb("turn", 94, [2, TOK])
    relu_sb = sb("relu_sb", 96, [3 * TOK])
    kib = sb("kib", 99, [2 * TOK])
    junk = sb("junk", 64, [2, D_MODEL])
    x_tok = sb("x_tok", 112, [2, D_MODEL])
    q_cols = sb("q_cols", 112, [8, TOK])
    k_cols = sb("k_cols", 120, [8, TOK])
    v_rows = sb("v_rows", 128, [2, HB * HEAD])
    lo_ple = sb("lo_ple", 64, [4, 4 * TOK])
    y_ple = sb("y_ple", 48, [KT, TOK])
    out_tok = sb("out_tok", 64, [2, D_MODEL])
    fin = sb("fin", 80, [2, 2, TOK])
    ws = sb("ws", 136, [SLOTS, CHUNK])
    hs = sb("hs", 152, [SLOTS, CHUNK], F32R)
    ls = sb("ls", 168, [SLOTS, CHUNK], F32R)
    lo = sb("lo", 184, [2, 2 * TOK])
    s_a = sb("s_a", 188, [2 * TOK])
    s_b = sb("s_b", 190, [2 * TOK])
    lg = sb("lg", 192, [CAT])
    pt = sb("pt", 193.5, [CAT])
    cm = sb("cm", 195, [CAT])
    mask = sb("mask", 196.5, [CAT])
    sel = sb("sel", 198, [CAT])
    q_st = sb("q_st", 199.5, [TOK])
    k_st = sb("k_st", 200.5, [TOK])
    v_st = sb("v_st", 201.5, [2, P])
    p_tok = sb("p_tok", 192, [2, D_PLE])
    silu_g = sb("silu_g", 192, [2 * TOK])
    lo_b = sb("lo_b", 194, [2, 2 * TOK])
    p_cols = sb("p_cols", 194, [KT_PLE, 2 * TOK], F32R)
    sq_sum = sb("sq_sum", 198, [2 * TOK])
    rms = sb("rms", 200, [2 * TOK])
    ident = sb("ident", 202.5, [P])
    ones = sb("ones", 203, [P])
    neg_id = sb("neg_id", 203.5, [P])
    c_cat = sb("c_cat", 204, [CAT])
    gains = sb("gains", 205.5, [4 * KT])
    w_tok = sb("w_tok", 205.75, [2, H_IDX])
    c_tok = sb("c_tok", 205.875, [2, HB])
    top8 = sb("top8", 205.9375, [2, 8])
    neg_max = sb("neg_max", 206, [2])
    sums = sb("sums", 206 + 1 / 32, [2])
    rsum = sb("rsum", 206 + 2 / 32, [2])
    r_tok = sb("r_tok", 206 + 3 / 32, [4])
    eps = sb("eps", 206 + 4 / 32, [1])
    half_pi = sb("half_pi", 206 + 5 / 32, [1])
    bias_f = sb("bias_f", 206 + 6 / 32, [1])
    rope_c = sb("rope_c", 206 + 7 / 32, [4])
    sq = sb("sq", 206.25, [TOK])
    pos_i = sb("pos_i", 101, [TOK], I32)
    pos_f = sb("pos_f", 102, [TOK])
    gain_rows = sb("gain_rows", 103, [P])
    full = sb("full", 80, [2, 2 * TOK])
    rms_x = sb("rms_x", 84, [2 * TOK])
    diag = sb("diag", 86, [2, P])
    f_w = sb("f_w", 88, [4, TOK])

    acc = nc.alloc_psum_tensor("acc", [P, 4, 512], F32)
    side = nc.alloc_psum_tensor("side", [P, 4, 512], F32)

    def x_bank(t):
        return (acc, side)[t % 4 // 2][:, 2 + t % 2, :]

    S = nc.alloc_semaphore
    x_loaded = [S(f"x_loaded{b}") for b in range(2)]
    gains_loaded = S("gains_loaded")
    bias_loaded = S("bias_loaded")
    const_loaded, p_loaded, out_stored = S("const_loaded"), S("p_loaded"), S("out_stored")
    w_loaded = [S(f"w_loaded{j}") for j in range(SLOTS)]
    h_split, l_split, chunk_used = S("h_split"), S("l_split"), S("chunk_used")
    lo_ready, combined = S("lo_ready"), S("combined")
    consts, ring_zero = S("consts"), S("ring_zero")
    pool_step, dve_step, act_step = S("pool_step"), S("dve_step"), S("act_step")
    angles, rope_sin = S("angles"), S("rope_sin")
    gain_t, gain_ready = S("gain_t"), S("gain_ready")
    x_squares, x_rms, diag_ready, rms_b, rms_sb = map(S, (
        "x_squares", "x_rms", "diag_ready", "rms_b", "rms_sb"))
    x_t, res_ready, hn_full, hn_high, hn_ready = map(S, ("x_t", "res_ready", "hn_full", "hn_high", "hn_ready"))
    f_z, f_e, f_l, f_c, small_t, small_ready, c_t = map(S, (
        "f_z", "f_e", "f_l", "f_c", "small_t", "small_ready", "c_t"))
    small_s = S("small_s")
    staged, v_staged, rope_done = S("staged"), S("v_staged"), S("rope_done")
    dots_done, relu_done, idx_done = S("dots_done"), S("relu_done"), S("idx_done")
    cm_ready, qk_done, max_ready, exp_done = map(S, ("cm_ready", "qk_done", "max_ready", "exp_done"))
    prob_ready, pt_done, pt_ready, pv_done, o_high, o_ready = map(S, (
        "prob_ready", "pt_done", "pt_ready", "pv_done", "o_high", "o_ready"))
    gate_ready = S("gate_ready")
    mix_s, mix_high, mix_ready = S("mix_s"), S("mix_high"), S("mix_ready")
    x_new, xg_high, xg_ready, sq_done = S("x_new"), S("xg_high"), S("xg_ready"), S("sq_done")
    ms_done, ms_sqrt, rms_ready = S("ms_done"), S("ms_sqrt"), S("rms_ready")
    p_t, p_high, p_ready = S("p_t"), S("p_high"), S("p_ready")
    ffg_s, ffg_silu, ff_s, ff_high, ff_ready = map(S, ("ffg_s", "ffg_silu", "ff_s", "ff_high", "ff_ready"))
    pg_s, pg_sig, fin_ready, fin_t, fin_read = map(S, ("pg_s", "pg_sig", "fin_ready", "fin_t", "fin_read"))
    tok_done, tok_sqrt, tok_ready, last_sq = map(S, ("tok_done", "tok_sqrt", "tok_ready", "last_sq"))
    y_ready_0, y_ready_1 = S("y_ready_0"), S("y_ready_1")

    block = nc.Block()
    block.__enter__()

    @block.sync
    def _(sp):
        for b in range(2):
            sp.dma_start(x_tok[:, b, :], x_rows[:, b, :]).then_inc(x_loaded[b], 16)

        def slot_free(u, j):
            sp.wait_ge(l_split, 4 * (u - 1) + j + 1)

        def load(j, src, n=CHUNK):
            parts = src.shape[1]
            sp.dma_start(ws[:, j, 0:n].rearrange("p (t n) -> p t n", t=parts), src).then_inc(w_loaded[j], 16)

        sp.wait_ge(ring_zero, SLOTS)
        for j in range(SLOTS):
            slot = ws[:, j, 0:SMALL].rearrange("p (t n) -> p t n", t=KC)
            rows = win_t[:, KC * j:KC * j + KC, :]
            for at, col, n in ((0, AT_KI, D_IDX + H_IDX), (F_ROW, AT_FB, HB)):
                sp.dma_start(slot[:, :, at:at + n], rows[:, :, col:col + n]).then_inc(w_loaded[j], 16)

        def columns(u0, units, w, col0):
            with sp.Fori(0, units) as i:
                for j in range(SLOTS):
                    slot_free(u0 + i, j)
                    load(j, w[:, KC * j:KC * j + KC, ds(col0 + i * GROUP, GROUP)])

        columns(U_QI, 4, win_t, AT_QI)
        columns(U_QB, 12, win_t, AT_QB)
        columns(U_GA, 8, win_t, AT_GA)
        columns(U_QA, 6, win_t, AT_QA)
        columns(U_GB, 8, win_t, AT_GB)
        with sp.Fori(0, 8) as i:
            for j in range(SLOTS):
                slot_free(U_WO + i, j)
                w, t = (wob_t, woa_t)[j // 2], KC * (j % 2)
                load(j, w[:, t:t + KC, ds(i * GROUP, GROUP)])
        sp.wait_ge(o_ready, FREE + HEADS)
        sp.dma_start(p_tok[:, :, :], p_rows).then_inc(p_loaded, 16)
        columns(U_OUT, 8, wout_t, 0)
        with sp.Fori(0, N_FFN) as i:
            for half, w in enumerate((wgate_t, wup_t)):
                for j in range(SLOTS):
                    slot_free(U_FFN + half + i * 2, j)
                    load(j, w[:, KC * j:KC * j + KC, ds(i * GROUP, GROUP)])
        with sp.Fori(0, 8) as i:
            t = 0
            for c, n in enumerate(DOWN_TILES):
                slot_free(U_DOWN + c // SLOTS + i * 3, c % SLOTS)
                load(c % SLOTS, wdown_t[:, t:t + n, ds(i * GROUP, GROUP)], n * GROUP)
                t += n
        for j in range(SLOTS):
            slot_free(U_PROJ, j)
            load(j, wpp_t[:, :, 2 * GROUP * j:2 * GROUP * (j + 1)])
        columns(U_PLE, 8, wpg_t, 0)
        for n in range(4):
            sp.wait_ge((y_ready_0, y_ready_1)[n % 2], n // 2 + 1)
            half = slice(D_MODEL // 2 * (n // 2), D_MODEL // 2 * (n // 2 + 1))
            sp.dma_start(out_rows[:, n % 2, half], out_tok[:, n % 2, half]).then_inc(out_stored, 16)
        sp.wait_ge(out_stored, 4 * 16)

    @block.gpsimd
    def _(pool):
        chain = Count(pool, pool_step)
        for sem in (dots_done, idx_done, relu_done, qk_done, pv_done, prob_ready, pt_ready, o_ready):
            pool.sem_inc(sem, FREE)
        for j in range(SLOTS):
            slot = ws[:, j, 0:SMALL].rearrange("p (t n) -> p t n", t=KC)
            pool.memset(slot[:, :, W_ROW + H_IDX:P], 0.0).then_inc(ring_zero, 1)
        pool.memset(ones[:, :], 1.0).then_inc(consts, 1)
        pool.memset(eps[:, :], EPS).then_inc(consts, 1)
        pool.memset(c_cat[:, :], 0.0).then_inc(consts, 1)
        pool.memset(kib[:, :], 0.0).then_inc(consts, 1)
        pool.memset(mask[:, :], 0.0).then_inc(consts, 1)
        pool.memset(neg_id[:, :], 0.0).then_inc(consts, 1)
        chain.step(pool.memset(ident[:, :], 0.0))
        pool.wait_ge(consts, 6)
        pool.affine_select(out=ident[:, :], in_=ident[:, :], compare_op=ALU.not_equal, fill=1.0, base=0,
                           pattern=[[-1, P]], channel_multiplier=1).then_inc(consts, 1)
        pool.affine_select(out=neg_id[:, :], in_=neg_id[:, :], compare_op=ALU.not_equal, fill=-1.0, base=0,
                           pattern=[[-1, P]], channel_multiplier=1).then_inc(consts, 1)
        for at in (0, CAT - P):
            tri = mask[:, at:at + P]
            pool.affine_select(out=tri, in_=tri, compare_op=ALU.is_ge, fill=MASKED, base=0,
                               pattern=[[-1, P]], channel_multiplier=1).then_inc(consts, 1)

        pool.wait_ge(rms_sb, 2)
        for t in range(KT // 2):
            pool.wait_ge(res_ready, t + 1)
            if t >= 2:
                pool.wait_ge(hn_ready, 2 * t - 2)
            pool.tensor_tensor(full[:, t % 2, :], res[:, 2 * t:2 * t + 2, :].rearrange("p m n -> p (m n)"), rms_x[:, :],
                               ALU.mult).then_inc(hn_full, 1)

        pool.wait_ge(rope_done, 4)
        with pool.Fori(0, STEPS_IDX) as e:
            pool.wait_ge(dots_done, FREE + e)
            pool.tensor_copy(q_st[:, :], q_idx[:, ds(e, 1), :]).then_inc(staged, 1)

        def stage_head(head, q_at, kv_at, values):
            pool.wait_ge(qk_done, FREE + head)
            pool.tensor_copy(q_st[:, :], q_cols[:, ds(q_at, 1), :]).then_inc(staged, 1)
            pool.tensor_copy(k_st[:, :], k_cols[:, ds(kv_at, 1), :]).then_inc(staged, 1)
            pool.wait_ge(combined, values)
            pool.wait_ge(pv_done, FREE + head)
            pool.tensor_copy(v_st[:, :, :], v_rows[:, :, ds(kv_at * P, P)]).then_inc(v_staged, 1)

        pool.wait_ge(dots_done, FREE + STEPS_IDX)
        pool.wait_ge(combined, U_VB)
        with pool.Fori(0, HB) as h:
            stage_head(h, h, h, U_VB + 4)
        pool.wait_ge(rope_done, 9)
        with pool.Fori(0, HA) as h:
            stage_head(HB + h, h, h // (HA // HA_KV), U_VA + 1)

        def square_sums(n0, groups=8):
            pool.wait_ge(x_new, n0 + 1)
            chain.step(pool.tensor_tensor(sq_sum[:, 0:TOK], res[:, 0, :], res[:, 0, :], ALU.mult))
            pool.tensor_tensor(sq_sum[:, TOK:2 * TOK], res[:, 1, :], res[:, 1, :], ALU.mult).then_inc(sq_done, 1)
            with pool.Fori(0, groups - 1) as i:
                chain.enter(i, 3)
                pool.wait_ge(sq_done, n0 + 1 + i)
                pool.wait_ge(x_new, n0 + 2 + i)
                even, odd = res[:, ds(i * 2 + 2, 1), :], res[:, ds(i * 2 + 3, 1), :]
                chain.step(pool.tensor_tensor(sq[:, :], even, even, ALU.mult))
                chain.step(pool.tensor_tensor(sq_sum[:, 0:TOK], sq_sum[:, 0:TOK], sq[:, :], ALU.add))
                chain.step(pool.tensor_tensor(sq[:, :], odd, odd, ALU.mult))
                pool.tensor_tensor(sq_sum[:, TOK:2 * TOK], sq_sum[:, TOK:2 * TOK], sq[:, :], ALU.add).then_inc(sq_done, 1)
            chain.leave(groups - 1)

        pool.wait_ge(o_ready, FREE + HEADS)
        square_sums(0)
        pool.wait_ge(ms_done, 1)
        square_sums(8)
        pool.wait_ge(ms_done, 2)
        square_sums(16, 7)

    @block.scalar
    def _(act):
        chain = Count(act, act_step)

        def split_high(u, j, n=CHUNK, first=False):
            if first:
                act.wait_ge(w_loaded[j], 2 * 16)
            else:
                act.wait_ge(w_loaded[j], 2 * 16 + 16 * u)
                act.wait_ge(chunk_used, 4 * (u - 1) + j + 1)
            act.activation(hs[:, j, 0:n], ws[:, j, 0:n], ACT.Copy).then_inc(h_split, 1)

        def take_lo(u_done, g, pair, scale=1.0, bank=acc, dst=None, when=None):
            act.wait_ge(chunk_used, 4 * (u_done + 1) if when is None else when)
            dst = lo[:, pair, :] if dst is None else dst
            act.activation(dst.rearrange("p (m n) -> p m n", m=2), bank[:, 2 * pair:2 * pair + 2, TOK:2 * TOK],
                           ACT.Copy, scale=scale).then_inc(lo_ready, 1)

        act.dma_start(pos_i[:, :], positions.partition_broadcast(P)).then_inc(const_loaded, 16)
        act.dma_start(rope_c[:, :], rope_rows).then_inc(const_loaded, 16)
        for n, g in enumerate((g_mix[0], g_ffn[0], g_ple[0], g_final)):
            act.dma_start(gain_rows[n * KT:(n + 1) * KT, :], g.rearrange("(t q) -> t q", q=P)).then_inc(gains_loaded, 16)
        act.dma_start(bias_f[F_ROWS, :], b_f[0].rearrange("(h o) -> h o", o=1)).then_inc(bias_loaded, 16)

        act.wait_ge(consts, 10)
        act.activation(neg_max[:, 0:1], eps[:, 0:1], ACT.Sqrt).then_inc(act_step, 1)
        chain.fixed += 1
        for b in range(2):
            act.wait_ge(x_loaded[b], 16)
            act.activation(junk[:, b, :], x_tok[:, b, :], ACT.Square, accum_out=r_tok[:, b:b + 1]).then_inc(x_squares, 1)
        act.wait_ge(x_squares, 2)
        act.activation(r_tok[:, 2:4], r_tok[:, 0:2], ACT.Sqrt, bias=eps[:, 0:1], scale=1.0 / D_MODEL).then_inc(x_rms, 1)
        act.wait_ge(gain_t, 1)
        act.activation(gains[:, :], side[:, 0, 0:4 * KT], ACT.Copy).then_inc(gain_ready, 1)
        act.wait_ge(gain_ready, 1)
        for t in range(KT // 2 + 1):
            if t < KT // 2:
                act.wait_ge(x_t, t + 1)
                act.activation(res[:, 2 * t:2 * t + 2, :].rearrange("p m n -> p (m n)"), x_bank(t),
                               ACT.Copy).then_inc(res_ready, 1)
            if t == 0:
                act.wait_ge(rms_b, 1)
                for m in range(2):
                    act.activation(rms_x[:, m * TOK:(m + 1) * TOK], side[:, 1, 0:TOK], ACT.Copy).then_inc(rms_sb, 1)
            if t % 2 == 0 and t < 2 * SLOTS:
                split_high(0, t // 2, SMALL, first=True)
            if t > 0:
                act.wait_ge(hn_full, t)
                for m in range(2):
                    k = 2 * t - 2 + m
                    act.activation(hn[:, k, 0:TOK], full[:, (t - 1) % 2, m * TOK:(m + 1) * TOK], ACT.Copy,
                                   scale=gains[:, k:k + 1]).then_inc(hn_high, 1)
        for j in range(SLOTS):
            split_high(1, j)
        act.wait_ge(angles, 1)
        for k in range(4):
            at = (0, 2, 1, 3)[k]
            for d in range(2):
                act.activation(rope[:, at, d * TOK:(d + 1) * TOK], ang_r[:, k, :], ACT.Sin).then_inc(rope_sin, 1)

        act.wait_ge(chunk_used, SLOTS)
        act.activation(lo[:, 0, 0:TOK], acc[:, 0, TOK:2 * TOK], ACT.Copy).then_inc(lo_ready, 1)
        split_high(2, 0)
        act.wait_ge(f_z, 1)
        act.activation(f_w[F_ROWS, 1, :], f_w[F_ROWS, 0, :], ACT.Abs).then_inc(act_step, 1)
        chain.fixed += 1
        act.wait_ge(act_step, chain.fixed)
        act.activation(f_w[F_ROWS, 2, :], f_w[F_ROWS, 1, :], ACT.Exp, scale=-1.0).then_inc(f_e, 1)
        split_high(2, 1)
        act.wait_ge(f_l, 1)
        act.activation(f_w[F_ROWS, 1, :], f_w[F_ROWS, 3, :], ACT.Ln).then_inc(f_e, 1)
        split_high(2, 2)
        split_high(2, 3)
        take_lo(U_QI, None, U_QI % 2)
        for u in range(U_QI + 1, U_QB):
            for j in range(SLOTS):
                split_high(u + 1, j)
            take_lo(u, None, u % 2)

        def plain_units(u0, units, scale=1.0):
            with act.Fori(0, units // 2) as i:
                for e in range(2):
                    for j in range(SLOTS):
                        split_high(u0 + e + 1 + i * 2, j)
                    take_lo(u0 + e + i * 2, None, (u0 + e) % 2, scale)

        def indexer_units(u0, scale, step0):
            with act.Fori(0, 2) as i:
                for e in range(2):
                    step = step0 + e + i * 2
                    for j in range(SLOTS):
                        split_high(u0 + e + 1 + i * 2, j)
                    take_lo(u0 + e + i * 2, None, (u0 + e) % 2, scale)
                    act.wait_ge(dots_done, FREE + 1 + step)
                    act.wait_ge(idx_done, FREE + step)
                    act.activation(relu_sb[:, 0:TOK], side[:, 0, 0:TOK], ACT.Relu).then_inc(relu_done, 1)
                    act.activation(relu_sb[:, TOK:3 * TOK], side[:, 1, :], ACT.Relu).then_inc(relu_done, 1)

        indexer_units(U_QB, SCALE, 0)
        indexer_units(U_KB, 1.0, 4)
        with act.Fori(0, 4) as i:
            for j in range(SLOTS):
                split_high(U_VB + 1 + i, j)

        def head_units(u0, head0):
            with act.Fori(0, 4) as i:
                for e in range(2):
                    head = head0 + e + i * 2
                    act.wait_ge(max_ready, 2 * head + 2)
                    for b, cols in enumerate((slice(0, P), slice(P, CAT))):
                        act.activation(lg[:, cols], lg[:, cols], ACT.Exp, bias=neg_max[:, b:b + 1],
                                       accum_out=sums[:, b:b + 1]).then_inc(exp_done, 1)
                    split_high(u0 + e + 1 + i * 2, 0)
                    split_high(u0 + e + 1 + i * 2, 1)
                    split_high(u0 + e + 1 + i * 2, 2)
                    act.wait_ge(pt_done, head + 1)
                    act.activation(pt[:, :], side[:, 2, 0:CAT], ACT.Copy).then_inc(pt_ready, 1)
                    split_high(u0 + e + 1 + i * 2, 3)
                    take_lo(u0 + e + i * 2, None, (u0 + e) % 2)
                    act.wait_ge(pv_done, FREE + 1 + head)
                    tile = (KT_O if head0 == 0 else -HB) + head
                    act.activation(heads_o[:, ds(tile, 1), 0:TOK], side[:, 3, 0:TOK], ACT.Copy).then_inc(o_high, 1)

        head_units(U_GA, 0)
        plain_units(U_QA, 4, SCALE)
        for j in range(SLOTS):
            split_high(U_KA + 1, j)
        take_lo(U_KA, None, U_KA % 2)
        for j in range(SLOTS):
            split_high(U_VA + 1, j)
        head_units(U_GB, HB)

        with act.Fori(0, 4) as i:
            for e in range(2):
                u = U_WO + e + i * 2
                both = gates[:, :, ds((e + i * 2) * 2, 2), :]
                split_high(u + 1, 0)
                split_high(u + 1, 1)
                act.wait_ge(combined, U_WO)
                for b in range(2):
                    act.activation(both[:, b], both[:, b], ACT.Sigmoid).then_inc(gate_ready, 1)
                split_high(u + 1, 2)
                split_high(u + 1, 3)
                pair = (U_WO + e) % 2
                take_lo(u, None, pair)
                take_lo(u, None, pair, 1.0, side, lo_b[:, pair, :])
                act.wait_ge(mix_s, 1 + e + i * 2)
                act.activation(mixed[:, ds((e + i * 2) * 2, 2), 0:TOK],
                               s_a[:, :].rearrange("p (m n) -> p m n", m=2), ACT.Copy).then_inc(mix_high, 1)

        def new_x(n, gain):
            act.wait_ge(x_new, n + 1)
            tile = (n - (0 if gain == KT else 8)) * 2
            for m in range(2):
                act.activation(xg[:, ds(tile + m, 1), 0:TOK], res[:, ds(tile + m, 1), :], ACT.Copy,
                               scale=gains[:, ds(tile + (gain + m), 1)]).then_inc(xg_high, 1)

        with act.Fori(0, 4) as i:
            for e in range(2):
                for j in range(SLOTS):
                    split_high(U_OUT + e + 1 + i * 2, j)
                take_lo(U_OUT + e + i * 2, None, (U_OUT + e) % 2)
                new_x(e + i * 2, KT)
        act.wait_ge(p_t, 1)
        act.activation(p_cols[:, :, 0:TOK], side[:, 2, :].rearrange("p (m n) -> p m n", m=2), ACT.Copy).then_inc(p_high, 1)

        def root(n):
            act.wait_ge(ms_done, n)
            act.activation(sq[:, :], side[:, 0, 0:TOK], ACT.Sqrt, bias=eps[:, 0:1], scale=1.0 / D_MODEL).then_inc(ms_sqrt, 1)

        def ffn_pair(i, first=False):
            u = U_FFN + i * 2
            for j in range(SLOTS):
                if first and j == 3:
                    root(1)
                split_high(u + 1, j)
            take_lo(u, None, U_FFN % 2)
            act.wait_ge(ffg_s, 1 + i)
            act.activation(silu_g[:, :], s_a[:, :], ACT.Silu).then_inc(ffg_silu, 1)
            for j in range(SLOTS):
                split_high(u + 2, j)
            take_lo(u + 1, None, (U_FFN + 1) % 2)
            act.wait_ge(ff_s, 1 + i)
            act.activation(ff[:, ds(i * 2, 2), 0:TOK], s_b[:, :].rearrange("p (m n) -> p m n", m=2),
                           ACT.Copy).then_inc(ff_high, 1)

        ffn_pair(0, first=True)
        with act.Fori(1, N_FFN) as i:
            ffn_pair(i)

        def proj_lo(c):
            act.wait_ge(chunk_used, 4 * U_PROJ + c + 1)
            for m in HALVES:
                act.activation(lo_ple[:, c, 2 * m * TOK:2 * (m + 1) * TOK].rearrange("p (m n) -> p m n", m=2),
                               (side, acc)[c % 2][:, 2 * m:2 * m + 2, TOK:2 * TOK], ACT.Copy).then_inc(lo_ready, 1)

        def down_group(i, e, last=False):
            u = U_DOWN + 3 * e + i * 6
            for j in range(SLOTS):
                split_high(u + 1, j)
            for j in range(SLOTS):
                split_high(u + 2, j, 3 * GROUP)
            for j in range(SLOTS):
                split_high(u + 3, j)
            take_lo(u + 2, None, (G_DOWN + e) % 2)
            if last:
                proj_lo(0)
            new_x(8 + e + i * 2, 2 * KT)

        with act.Fori(0, 3) as i:
            down_group(i, 0)
            down_group(i, 1)
        down_group(3, 0)
        down_group(3, 1, last=True)
        for c in range(SLOTS):
            if c > 0:
                proj_lo(c)
            split_high(U_PLE, c)
        root(2)

        def ple_unit(i, e, first=False, last=False):
            n = e + i * 2
            if not last:
                for j in range(SLOTS):
                    split_high(U_PLE + 1 + n, j)
            if not first:
                take_fin(n - 1)
            take_lo(U_PLE + n, None, (G_PLE + e) % 2)
            act.wait_ge(pg_s, n + 1)
            act.activation(s_b[:, :], s_a[:, :], ACT.Sigmoid).then_inc(pg_sig, 1)
            if last:
                act.activation(neg_max[:, 0:1], eps[:, 0:1], ACT.Sqrt).then_inc(act_step, 1)
            act.wait_ge(x_new, 17 + n)
            for m in range(2):
                act.activation(fin[:, e, m, :], res[:, ds(n * 2 + m, 1), :], ACT.Copy,
                               scale=gains[:, ds(n * 2 + (3 * KT + m), 1)]).then_inc(fin_ready, 1)

        def take_fin(n):
            act.wait_ge(fin_t, n + 1)
            act.activation(out_tok[:, :, ds(n * GROUP, GROUP)], side[:, 1, :].rearrange("p (b n) -> p b n", b=2),
                           ACT.Copy).then_inc(fin_read, 1)

        ple_unit(0, 0, first=True)
        ple_unit(0, 1)
        with act.Fori(1, 3) as i:
            ple_unit(i, 0)
            ple_unit(i, 1)
        ple_unit(3, 0)
        ple_unit(3, 1, last=True)
        take_fin(7)
        act.wait_ge(tok_done, 1)
        act.activation(r_tok[:, 2:4], side[:, 2, 0:2], ACT.Sqrt, bias=eps[:, 0:1], scale=1.0 / D_MODEL).then_inc(tok_sqrt, 1)
        act.wait_ge(tok_ready, 1)
        act.wait_ge(fin_read, 8)
        for n in range(2):
            half = slice(D_MODEL // 2 * n, D_MODEL // 2 * (n + 1))
            act.activation(out_tok[:, 1, half], out_tok[:, 1, half], ACT.Copy, scale=r_tok[:, 1:2]).then_inc(y_ready_1, 1)

    @block.vector
    def _(dve):
        chain = Count(dve, dve_step)

        def split_low(u, j, n=CHUNK):
            dve.wait_ge(h_split, 4 * u + j + 1)
            dve.tensor_tensor(ls[:, j, 0:n], ws[:, j, 0:n], hs[:, j, 0:n].bitcast(F32), ALU.subtract).then_inc(l_split, 1)

        def two(t):
            return t.rearrange("p (m n) -> p m n", m=2)

        def combine(dst, g, pair, lo_count, scale=1.0, tables=False):
            dve.wait_ge(lo_ready, lo_count)
            ins = dve.scalar_tensor_tensor(dst, acc[:, 2 * pair:2 * pair + 2, 0:TOK], scale, two(lo[:, pair, :]),
                                           ALU.mult, ALU.add)
            ins.then_inc(combined, 1)
            if tables:
                dve.wait_ge(rope_sin, 10)
            dve.wait_ge(combined, g + 1)

        dve.wait_ge(const_loaded, 2 * 16)
        chain.step(dve.tensor_copy(pos_f[:, :], pos_i[:, :]))
        for k, col in enumerate((2, 0)):
            chain.step(dve.tensor_scalar(ang[:, k, :], pos_f[:, :], rope_c[:, col:col + 1], None, ALU.mult))
        two_pi = 6.283185307179586
        parts = (6.28125, 0.0019350051879882812, 3.0199159819568e-07)
        rounder = 12582912.0
        for k, quarter in enumerate((0.25, 0.0)):
            chain.step(dve.tensor_scalar(turn[:, :, :], ang[:, :, :], 1.0 / two_pi, quarter, ALU.mult, ALU.add))
            chain.step(dve.tensor_scalar(turn[:, :, :], turn[:, :, :], rounder, None, ALU.add))
            chain.step(dve.tensor_scalar(turn[:, :, :], turn[:, :, :], rounder, None, ALU.subtract))
            r = ang_r[:, 2 * k:2 * k + 2, :]
            src = ang[:, :, :]
            for part in parts:
                chain.step(dve.scalar_tensor_tensor(r, turn[:, :, :], -part, src, ALU.mult, ALU.add))
                src = r
            chain.step(dve.tensor_scalar(r, r, quarter * two_pi, 3.1415925, ALU.add, ALU.min))
            ins = dve.tensor_scalar(r, r, -3.1415925, None, ALU.max)
            if k == 0:
                chain.step(ins)
            else:
                ins.then_inc(angles, 1)
        dve.wait_ge(x_rms, 1)
        chain.step(dve.reciprocal(r_tok[:, 0:2], r_tok[:, 2:4]))
        for b in range(2):
            dve.tensor_scalar(diag[:, b, :], ident[:, :], r_tok[:, b:b + 1], None, ALU.mult).then_inc(diag_ready, 1)
        dve.wait_ge(gain_ready, 1)
        for t in range(KT // 2):
            if t % 2 == 0:
                split_low(0, t // 2, SMALL)
            dve.wait_ge(hn_full, t + 1)
            for m in range(2):
                k = 2 * t + m
                dve.wait_ge(hn_high, k + 1)
                dve.scalar_tensor_tensor(hn[:, k, TOK:2 * TOK], full[:, t % 2, m * TOK:(m + 1) * TOK], gains[:, k:k + 1],
                                         hn[:, k, 0:TOK].bitcast(F32), ALU.mult, ALU.subtract).then_inc(hn_ready, 1)
        for j in range(SLOTS):
            split_low(1, j)
        dve.wait_ge(rope_sin, 8)
        for at, col in ((1, 3), (3, 1)):
            dve.tensor_scalar(rope[:, at, :], rope[:, at, :], rope_c[:, col:col + 1], None, ALU.mult).then_inc(rope_sin, 1)

        swap_idx = [8 + i if i < 8 else i - 8 if i < 16 else i for i in range(32)]
        swap_a = [(i + 16) % 32 for i in range(32)]

        dve.wait_ge(lo_ready, 1)
        dve.tensor_tensor(s_a[:, 0:TOK], acc[:, 0, 0:TOK], lo[:, 0, 0:TOK], ALU.add).then_inc(combined, 1)
        dve.wait_ge(combined, 1)
        dve.wait_ge(bias_loaded, 16)
        dve.tensor_scalar(f_w[F_ROWS, 0, :], s_a[F_ROWS, 0:TOK], bias_f[F_ROWS, 0:1], None, ALU.add).then_inc(f_z, 1)
        dve.wait_ge(rope_sin, 10)
        k_rows = slice(0, D_IDX)
        chain.step(dve.stream_shuffle(s_b[k_rows, 0:TOK], s_a[k_rows, 0:TOK], swap_idx))
        chain.step(dve.tensor_tensor(s_b[k_rows, 0:TOK], s_b[k_rows, 0:TOK], rope[k_rows, 1, 0:TOK], ALU.mult))
        chain.step(dve.tensor_tensor(s_b[k_rows, TOK:2 * TOK], s_a[k_rows, 0:TOK], rope[k_rows, 0, 0:TOK], ALU.mult))
        for m in range(2):
            dve.tensor_tensor(kib[D_IDX * m:D_IDX * (m + 1), m * TOK:(m + 1) * TOK], s_b[k_rows, 0:TOK],
                              s_b[k_rows, TOK:2 * TOK], ALU.add).then_inc(small_s, 1)

        def forget_exp():
            dve.wait_ge(f_e, 1)
            dve.tensor_scalar(f_w[F_ROWS, 3, :], f_w[F_ROWS, 2, :], 1.0, None, ALU.add).then_inc(f_l, 1)

        def forget_sums():
            dve.wait_ge(f_e, 2)
            chain.step(dve.scalar_tensor_tensor(f_w[F_ROWS, 2, :], f_w[F_ROWS, 0, :], 0.0, f_w[F_ROWS, 1, :], ALU.min, ALU.subtract))
            chain.step(dve.memset(f_w[F_ROWS, 3, :], 1.0))
            chain.step(dve.tensor_tensor_scan(c_cat[F_ROWS, P:CAT], f_w[F_ROWS, 3, :], f_w[F_ROWS, 2, :], 0.0, ALU.mult, ALU.add))
            dve.tensor_copy(c_cat[F_ROWS, 0:P], c_cat[F_ROWS, P:2 * P]).then_inc(f_c, 1)

        def index_weights():
            dve.wait_ge(small_t, 1)
            for b in range(2):
                chain.step(dve.tensor_scalar(w_tok[:, b, :], side[:, 2, b * P + W_ROW:b * P + W_ROW + H_IDX],
                                             H_IDX ** -0.5 * D_IDX ** -0.5, None, ALU.mult))
            chain.step(dve.memset(sel[:, :], 0.0))

        def rotate(dst, t, table, swap, mask_rows):
            rows = slice(0, mask_rows)
            chain.step(dve.stream_shuffle(s_b[rows, :], t[rows, :], swap))
            chain.step(dve.tensor_tensor(s_b[rows, :], s_b[rows, :], rope[rows, table + 1, :], ALU.mult))
            chain.step(dve.tensor_tensor(t[rows, :], t[rows, :], rope[rows, table, :], ALU.mult))
            dve.tensor_tensor(dst[rows], two(t[rows, :]), two(s_b[rows, :]), ALU.add).then_inc(rope_done, 1)

        dve.wait_ge(small_s, 2)
        for n in range(4):
            g = U_QI + n
            for j in range(SLOTS):
                split_low(g + 1, j)
                if n == 0 and j == 0:
                    forget_exp()
            if n == 0:
                index_weights()
            if n == 1:
                forget_sums()
            combine(two(s_a[:, :]), g, g % 2, g + 1)
            rotate(q_idx[:, 2 * n:2 * n + 2, :], s_a, 0, swap_idx, P)
            dve.wait_ge(rope_done, 1 + n)
        dve.wait_ge(f_c, 1)

        cats = (slice(0, P), slice(P, CAT))

        def indexer_units(u0, dst, scale, step0):
            with dve.Fori(0, 2) as i:
                chain.enter(i, 6)
                for e in range(2):
                    step = step0 + e + i * 2
                    g = u0 + e + i * 2
                    for j in range(SLOTS):
                        split_low(g + 1, j)
                    combine(dst[:, ds((e + i * 2) * 2, 2), :], g, (u0 + e) % 2, g + 1, scale)
                    dve.wait_ge(relu_done, FREE + 2 + step * 2)
                    for hh in range(2):
                        w_col = step * 2 + hh
                        dots = (relu_sb[:, hh * P:(hh + 1) * P], relu_sb[:, TOK * (1 + hh):TOK * (2 + hh)])
                        for b in range(2):
                            ins = dve.scalar_tensor_tensor(sel[:, cats[b]], dots[b], w_tok[:, b, ds(w_col, 1)],
                                                           sel[:, cats[b]], ALU.mult, ALU.add)
                            if hh == 1 and b == 1:
                                ins.then_inc(idx_done, 1)
                                dve.wait_ge(idx_done, FREE + 1 + step)
                            else:
                                chain.step(ins)
            chain.leave(2)

        indexer_units(U_QB, q_cols, SCALE, 0)
        indexer_units(U_KB, k_cols, 1.0, 4)
        chain.step(dve.tensor_tensor(sel[:, :], sel[:, :], mask[:, :], ALU.add))

        dve.wait_ge(c_t, 1)
        for b in range(2):
            chain.step(dve.tensor_copy(c_tok[:, b, :], side[:, 3, b * P + F_ROW:b * P + F_ROW + HB]))
        dve.tensor_scalar(cm[:, :], c_cat[:, :], neg_id[:, F_ROW:F_ROW + 1], None, ALU.mult).then_inc(cm_ready, 1)

        for i in range(4):
            g = U_VB + i
            for _ in range(TOP_K // 8 // 4):
                for b in range(2):
                    chain.step(dve.max(top8[:, b, :], sel[:, cats[b]]))
                    chain.step(dve.match_replace(sel[:, cats[b]], top8[:, b, :], sel[:, cats[b]], TAKEN))
            for j in range(SLOTS):
                split_low(g + 1, j)
            dve.wait_ge(chunk_used, 4 * g + 4)
            dve.tensor_copy(v_rows[:, :, i * GROUP:(i + 1) * GROUP],
                            acc[:, 2 * (g % 2):2 * (g % 2) + 2, 0:TOK]).then_inc(combined, 1)
        chain.step(dve.tensor_scalar(sel[:, :], sel[:, :], TAKEN_BELOW, 1.0, ALU.is_le, ALU.subtract))
        chain.step(dve.scalar_tensor_tensor(sel[:, :], sel[:, :], -MASKED, mask[:, :], ALU.mult, ALU.min))

        def head_units(u0, head0, lo_off, per_pass):
            forget = head0 == 0
            with dve.Fori(0, 4) as i:
                chain.enter(i, per_pass)
                for e in range(2):
                    h = e + i * 2
                    head = head0 + h
                    g = u0 + h
                    dve.wait_ge(qk_done, FREE + 1 + head)
                    if forget:
                        chain.step(dve.tensor_tensor(lg[:, :], side[:, 1, 0:CAT], mask[:, :], ALU.add))
                        for b in range(2):
                            chain.step(dve.scalar_tensor_tensor(lg[:, cats[b]], side[:, 0, cats[b]], c_tok[:, b, ds(h, 1)],
                                                                lg[:, cats[b]], ALU.add, ALU.add))
                        dve.tensor_scalar(cm[:, :], c_cat[:, :], neg_id[:, ds(h + (F_ROW + 1), 1)], None, ALU.mult).then_inc(cm_ready, 1)
                    else:
                        chain.step(dve.tensor_tensor(lg[:, :], side[:, 0, 0:CAT], sel[:, :], ALU.add))
                    for b in range(2):
                        dve.tensor_reduce(neg_max[:, b:b + 1], lg[:, cats[b]], AX_X, ALU.max, negate=True).then_inc(max_ready, 1)
                    dve.wait_ge(exp_done, 2 * head + 2)
                    chain.step(dve.reciprocal(rsum[:, :], sums[:, :]))
                    for b in range(2):
                        dve.tensor_scalar(lg[:, cats[b]], lg[:, cats[b]], rsum[:, b:b + 1], None, ALU.mult).then_inc(prob_ready, 1)
                    for j in range(SLOTS):
                        split_low(g + 1, j)
                    combine(gates[:, head0 // HB, ds(h * 2, 2), :], g, (u0 + e) % 2, g + 1 - lo_off)
                    dve.wait_ge(o_high, head + 1)
                    tile = (KT_O if forget else 0) + h
                    dve.tensor_tensor(heads_o[:, ds(tile, 1), TOK:2 * TOK], side[:, 3:4, 0:TOK],
                                      heads_o[:, ds(tile, 1), 0:TOK].bitcast(F32), ALU.subtract).then_inc(o_ready, 1)
            chain.leave(4)

        head_units(U_GA, 0, 4, 8)

        def rotate_a(dst):
            rows = slice(0, ROT_A)
            chain.step(dve.stream_shuffle(s_b[rows, :], s_a[rows, :], swap_a))
            chain.step(dve.tensor_tensor(s_b[rows, :], s_b[rows, :], rope[rows, 3, :], ALU.mult))
            chain.step(dve.tensor_tensor(s_a[rows, :], s_a[rows, :], rope[rows, 2, :], ALU.mult))
            chain.step(dve.tensor_tensor(s_a[rows, :], s_a[rows, :], s_b[rows, :], ALU.add))
            dve.tensor_copy(dst, two(s_a[:, :])).then_inc(rope_done, 1)

        with dve.Fori(0, 2) as i:
            chain.enter(i, 8)
            for e in range(2):
                g = U_QA + e + i * 2
                for j in range(SLOTS):
                    split_low(g + 1, j)
                dve.wait_ge(rope_done, 4 + e + i * 2)
                combine(two(s_a[:, :]), g, (U_QA + e) % 2, g + 1 - 4, SCALE, tables=True)
                rotate_a(q_cols[:, ds((e + i * 2) * 2, 2), :])
        chain.leave(2)
        for j in range(SLOTS):
            split_low(U_KA + 1, j)
        dve.wait_ge(rope_done, 8)
        combine(two(s_a[:, :]), U_KA, U_KA % 2, U_KA + 1 - 4)
        rotate_a(k_cols[:, 0:2, :])
        dve.wait_ge(rope_done, 9)
        for j in range(SLOTS):
            split_low(U_VA + 1, j)
        dve.wait_ge(chunk_used, 4 * U_VA + 4)
        pair = U_VA % 2
        dve.wait_ge(v_staged, HB)
        dve.tensor_copy(v_rows[:, :, 0:GROUP], acc[:, 2 * pair:2 * pair + 2, 0:TOK]).then_inc(combined, 1)
        head_units(U_GB, HB, 5, 4)

        with dve.Fori(0, 4) as i:
            chain.enter(i, 6)
            for e in range(2):
                n = e + i * 2
                g = U_WO + n
                for j in range(SLOTS):
                    split_low(g + 1, j)
                pair = (U_WO + e) % 2
                dve.wait_ge(lo_ready, U_WO - 5 + 1 + n * 2)
                chain.step(dve.tensor_tensor(two(s_a[:, :]), acc[:, 2 * pair:2 * pair + 2, 0:TOK], two(lo[:, pair, :]), ALU.add))
                dve.wait_ge(lo_ready, U_WO - 5 + 2 + n * 2)
                dve.tensor_tensor(two(s_b[:, :]), side[:, 2 * pair:2 * pair + 2, 0:TOK], two(lo_b[:, pair, :]),
                                  ALU.add).then_inc(combined, 1)
                dve.wait_ge(gate_ready, 2 * n + 2)
                chain.step(dve.tensor_tensor(two(s_a[:, :]), two(s_a[:, :]), gates[:, 1, ds(n * 2, 2), :], ALU.mult))
                dve.wait_ge(combined, g + 1)
                chain.step(dve.tensor_tensor(two(s_b[:, :]), two(s_b[:, :]), gates[:, 0, ds(n * 2, 2), :], ALU.mult))
                dve.tensor_tensor(s_a[:, :], s_a[:, :], s_b[:, :], ALU.add).then_inc(mix_s, 1)
                dve.wait_ge(mix_high, n + 1)
                dve.tensor_tensor(mixed[:, ds(n * 2, 2), TOK:2 * TOK], two(s_a[:, :]),
                                  mixed[:, ds(n * 2, 2), 0:TOK].bitcast(F32), ALU.subtract).then_inc(mix_ready, 1)
                dve.wait_ge(mix_ready, n + 1)
        chain.leave(4)

        LO_OUT = U_OUT - 5 + 8

        def new_x(n, n0, gain, between=None):
            tile = (n - n0) * 2
            dve.tensor_tensor(res[:, ds(tile, 2), :], two(s_a[:, :]), res[:, ds(tile, 2), :], ALU.add).then_inc(x_new, 1)
            if between is not None:
                between()
            dve.wait_ge(xg_high, 2 * n + 2)
            for m in range(2):
                dve.scalar_tensor_tensor(xg[:, ds(tile + m, 1), TOK:2 * TOK], res[:, ds(tile + m, 1), :],
                                         gains[:, ds(tile + (gain + m), 1)], xg[:, ds(tile + m, 1), 0:TOK].bitcast(F32),
                                         ALU.mult, ALU.subtract).then_inc(xg_ready, 1)

        with dve.Fori(0, 4) as i:
            for e in range(2):
                n = e + i * 2
                for j in range(SLOTS):
                    split_low(U_OUT + 1 + n, j)
                combine(two(s_a[:, :]), U_OUT + n, (U_OUT + e) % 2, LO_OUT + 1 + n)
                new_x(n, 0, KT)
        dve.wait_ge(p_high, 1)
        dve.tensor_tensor(p_cols[:, :, TOK:2 * TOK], two(side[:, 2, :]), p_cols[:, :, 0:TOK].bitcast(F32),
                          ALU.subtract).then_inc(p_ready, 1)

        def reciprocal_rms(n):
            dve.wait_ge(ms_sqrt, n)
            dve.reciprocal(rms[:, 0:TOK], sq[:, :]).then_inc(rms_ready, 1)
            dve.wait_ge(rms_ready, 2 * n - 1)
            dve.tensor_copy(rms[:, TOK:2 * TOK], rms[:, 0:TOK]).then_inc(rms_ready, 1)
            dve.wait_ge(rms_ready, 2 * n)

        LO_FFN = LO_OUT + 8
        dve.wait_ge(x_new, 8)

        def ffn_pair(i, first=False):
            g = U_FFN + i * 2
            for j in range(SLOTS):
                if first and j == 3:
                    reciprocal_rms(1)
                split_low(g + 1, j)
            combine(two(s_a[:, :]), g, U_FFN % 2, LO_FFN + 1 + i * 2)
            dve.tensor_tensor(s_a[:, :], s_a[:, :], rms[:, :], ALU.mult).then_inc(ffg_s, 1)
            for j in range(SLOTS):
                split_low(g + 2, j)
            combine(two(s_b[:, :]), g + 1, (U_FFN + 1) % 2, LO_FFN + 2 + i * 2)
            chain.step(dve.tensor_tensor(s_b[:, :], s_b[:, :], rms[:, :], ALU.mult))
            dve.wait_ge(ffg_silu, 1 + i)
            dve.tensor_tensor(s_b[:, :], s_b[:, :], silu_g[:, :], ALU.mult).then_inc(ff_s, 1)
            dve.wait_ge(ff_high, 1 + i)
            dve.tensor_tensor(ff[:, ds(i * 2, 2), TOK:2 * TOK], two(s_b[:, :]), ff[:, ds(i * 2, 2), 0:TOK].bitcast(F32),
                              ALU.subtract).then_inc(ff_ready, 1)
            dve.wait_ge(ff_ready, 1 + i)

        ffn_pair(0, first=True)
        with dve.Fori(1, N_FFN) as i:
            chain.enter(i, 1, first=1)
            ffn_pair(i)
        chain.leave(N_FFN)

        LO_DOWN = LO_FFN + 2 * N_FFN
        LO_PROJ = LO_DOWN + 8

        def proj_chunk(c):
            for at, m in enumerate(HALVES):
                dve.wait_ge(lo_ready, LO_PROJ + 2 * c + at + 1)
                dve.tensor_tensor(y_ple[:, 4 * c + 2 * m:4 * c + 2 * m + 2, :], (side, acc)[c % 2][:, 2 * m:2 * m + 2, 0:TOK],
                                  two(lo_ple[:, c, 2 * m * TOK:2 * (m + 1) * TOK]), ALU.add).then_inc(combined, 1)

        def down_group(i, e, last=False):
            u = U_DOWN + 3 * e + i * 6
            n = e + i * 2
            for j in range(SLOTS):
                split_low(u + 1, j)
            for j in range(SLOTS):
                split_low(u + 2, j, 3 * GROUP)
            for j in range(SLOTS):
                split_low(u + 3, j)
            combine(two(s_a[:, :]), G_DOWN + n, (G_DOWN + e) % 2, LO_DOWN + 1 + n)
            new_x(8 + n, 8, 2 * KT, between=(lambda: proj_chunk(0)) if last else None)

        with dve.Fori(0, 3) as i:
            down_group(i, 0)
            down_group(i, 1)
        down_group(3, 0)
        down_group(3, 1, last=True)
        dve.wait_ge(x_new, 16)
        for c in range(SLOTS):
            if c > 0:
                proj_chunk(c)
            split_low(U_PLE, c)
        reciprocal_rms(2)
        LO_PLE = LO_PROJ + 2 * SLOTS

        def ple_unit(i, e, last=False):
            n = e + i * 2
            if not last:
                for j in range(SLOTS):
                    split_low(U_PLE + 1 + n, j)
            combine(two(s_a[:, :]), G_PLE + n, (G_PLE + e) % 2, LO_PLE + 1 + n)
            dve.tensor_tensor(s_a[:, :], s_a[:, :], rms[:, :], ALU.mult).then_inc(pg_s, 1)
            dve.wait_ge(pg_sig, n + 1)
            chain.step(dve.tensor_tensor(two(s_b[:, :]), two(s_b[:, :]), y_ple[:, ds(n * 2, 2), :], ALU.mult))
            dve.tensor_tensor(res[:, ds(n * 2, 2), :], two(s_b[:, :]), res[:, ds(n * 2, 2), :], ALU.add).then_inc(x_new, 1)
            if last:
                dve.wait_ge(x_new, 17 + n)
                dve.tensor_tensor(two(s_a[:, :]), res[:, 2 * n:2 * n + 2, :], res[:, 2 * n:2 * n + 2, :],
                                  ALU.mult).then_inc(last_sq, 1)

        with dve.Fori(0, 3) as i:
            chain.enter(i, 2)
            ple_unit(i, 0)
            ple_unit(i, 1)
        chain.leave(3)
        ple_unit(3, 0)
        ple_unit(3, 1, last=True)
        dve.wait_ge(tok_sqrt, 1)
        dve.reciprocal(r_tok[:, 0:2], r_tok[:, 2:4]).then_inc(tok_ready, 1)
        dve.wait_ge(tok_ready, 1)
        dve.wait_ge(fin_read, 8)
        for n in range(2):
            half = slice(D_MODEL // 2 * n, D_MODEL // 2 * (n + 1))
            dve.tensor_scalar(out_tok[:, 0, half], out_tok[:, 0, half], r_tok[:, 0:1], None, ALU.mult).then_inc(y_ready_0, 1)

    @block.tensor
    def _(pe):
        def bank_free(g):
            pe.wait_ge(combined, g - 1)

        def consume(u, j, bank, banks, tiles, src, first, last, width=GROUP, col=0, signal=True, wait=True):
            if wait:
                pe.wait_ge(l_split, 4 * u + j + 1)
            for m in range(banks):
                for q, k in enumerate(tiles):
                    at = slice(q * width + col + m * P, q * width + col + (m + 1) * P)
                    begins, ends = first and q == 0, last and q == len(tiles) - 1
                    high, low = (hs[:, j, at], src[:, k, :]), (ls[:, j, at], src[:, k, 0:TOK])
                    whole, half = acc_of(bank + m, 2 * TOK), acc_of(bank + m, TOK)
                    if ends:
                        pe.matmul(half, *low, start=False, stop=False)
                        mm = pe.matmul(whole, *high, start=False, stop=True)
                    else:
                        pe.matmul(whole, *high, start=begins, stop=False)
                        mm = pe.matmul(half, *low, start=False, stop=False)
            if signal:
                mm.then_inc(chunk_used, 1)

        def acc_of(bank, n):
            return (acc if bank < 4 else side)[:, bank % 4, 0:n]

        def unit(u, g, src, pair, between=None, needs=None):
            if not isinstance(g, int) or g >= 2:
                bank_free(g)
            for j in range(SLOTS):
                if needs is not None:
                    pe.wait_ge(needs[0], needs[1](j))
                consume(u, j, 2 * pair, 2, range(KC * j, KC * j + KC), src, j == 0, j == 3)
                if between is not None and j == between[0]:
                    between[1]()

        pe.wait_ge(gains_loaded, 4 * 16)
        pe.wait_ge(consts, 10)
        pe.transpose(side[:, 0, 0:4 * KT], gain_rows[0:4 * KT, :], ident[0:4 * KT, 0:4 * KT]).then_inc(gain_t, 1)

        def x_transposes(t):
            if t >= 4:
                pe.wait_ge(res_ready, t - 3)
            for m in range(2):
                for b in range(2):
                    mm = pe.transpose(x_bank(t)[:, m * TOK + b * P:m * TOK + (b + 1) * P],
                                      x_tok[:, b, (2 * t + m) * P:(2 * t + m + 1) * P], ident[:, :])
            mm.then_inc(x_t, 1)

        for b in range(2):
            pe.wait_ge(x_loaded[b], 16)
        for t in range(4):
            x_transposes(t)
        pe.wait_ge(diag_ready, 2)
        for b in range(2):
            mm = pe.matmul(side[:, 1, b * P:(b + 1) * P], ones[:, :], diag[:, b, :], start=True, stop=True)
        mm.then_inc(rms_b, 1)
        for t in range(4, KT // 2):
            x_transposes(t)

        for j in range(SLOTS):
            pe.wait_ge(hn_ready, 4 * j + 4)
            consume(0, j, 0, 1, range(KC * j, KC * j + KC), hn, j == 0, j == 3, width=P)

        pe.wait_ge(res_ready, KT // 2)

        def small_by_token():
            pe.wait_ge(combined, 1)
            for b in range(2):
                mm = pe.transpose(side[:, 2, b * P:(b + 1) * P], s_a[:, b * P:(b + 1) * P], ident[:, :])
            mm.then_inc(small_t, 1)

        unit(U_QI, U_QI, hn, U_QI % 2, between=(1, small_by_token))

        def decay_by_token():
            pe.wait_ge(f_c, 1)
            for b in range(2):
                mm = pe.transpose(side[:, 3, b * P:(b + 1) * P], c_cat[:, (1 + b) * P:(2 + b) * P], ident[:, :])
            mm.then_inc(c_t, 1)

        for u in range(U_QI + 1, U_QB):
            unit(u, u, hn, u % 2, between=(1, decay_by_token) if u == U_QB - 1 else None)

        def dots(step):
            pe.wait_ge(staged, step + 1)
            pe.wait_ge(relu_done, FREE + step * 2)
            keys = kib[:, :].rearrange("p (h n) -> p h n", h=2)
            pe.matmul(side[:, 0, 0:TOK].rearrange("p (h n) -> p h n", h=2), q_st[:, 0:P], keys[:, :, 0:P], start=True, stop=True)
            pe.matmul(side[:, 1, :], q_st[:, P:TOK], kib[:, :], start=True, stop=True).then_inc(dots_done, 1)

        pe.wait_ge(small_s, 2)
        with pe.Fori(0, 4) as i:
            for e in range(2):
                n = e + i * 2
                unit(U_QB + n, U_QB + n, hn, (U_QB + e) % 2)
                dots(n)

        def by_token(u, pair):
            bank_free(u)
            for j in range(SLOTS):
                pe.wait_ge(l_split, 4 * u + j + 1)
                for t in range(2):
                    for q in range(KC):
                        k = KC * j + q
                        wh, wl = hs[:, j, q * GROUP:(q + 1) * GROUP], ls[:, j, q * GROUP:(q + 1) * GROUP]
                        xh, xl = hn[:, k, t * P:(t + 1) * P], hn[:, k, TOK + t * P:TOK + (t + 1) * P]
                        dst = acc[:, 2 * pair + t, 0:TOK]
                        pe.matmul(dst, xh, wh, start=k == 0, stop=False)
                        pe.matmul(dst, xh, wl, start=False, stop=False)
                        mm = pe.matmul(dst, xl, wh, start=False, stop=k == KT - 1)
                mm.then_inc(chunk_used, 1)

        with pe.Fori(0, 2) as i:
            for e in range(2):
                by_token(U_VB + e + i * 2, (U_VB + e) % 2)

        def scores(head, forget):
            pe.wait_ge(staged, STEPS_IDX + 2 + head * 2)
            pe.wait_ge(prob_ready, FREE + head * 2)
            if forget:
                pe.wait_ge(cm_ready, head + 1)
                pe.matmul(side[:, 1, 0:CAT], ones[:, :], cm[:, :], start=True, stop=True)
            pe.matmul(side[:, 0, 0:P], q_st[:, 0:P], k_st[:, 0:P], start=True, stop=True)
            pe.matmul(side[:, 0, P:CAT], q_st[:, P:TOK], k_st[:, :], start=True, stop=True).then_inc(qk_done, 1)

        def probs_by_key(head):
            pe.wait_ge(prob_ready, FREE + 2 + head * 2)
            pe.wait_ge(pt_ready, FREE + head)
            for c in range(3):
                mm = pe.transpose(side[:, 2, c * P:(c + 1) * P], lg[:, c * P:(c + 1) * P], ident[:, :])
            mm.then_inc(pt_done, 1)

        def values(head):
            pe.wait_ge(pt_ready, FREE + 1 + head)
            pe.wait_ge(v_staged, head + 1)
            pe.wait_ge(o_ready, FREE + head)
            pe.matmul(side[:, 3, 0:P], v_st[:, 0, :], pt[:, 0:P], start=True, stop=True)
            pe.matmul(side[:, 3, P:TOK], v_st[:, 0, :], pt[:, P:2 * P], start=True, stop=False)
            pe.matmul(side[:, 3, P:TOK], v_st[:, 1, :], pt[:, 2 * P:CAT], start=False, stop=True).then_inc(pv_done, 1)

        def head_units(u0, head0):
            forget = head0 == 0
            scores(head0, forget)

            def two_heads(i, last=False):
                for e in range(2):
                    h = e + i * 2

                    def between():
                        probs_by_key(head0 + h)
                        if not (last and e == 1):
                            scores(head0 + h + 1, forget)

                    unit(u0 + h, u0 + h, hn, (u0 + e) % 2, between=(2, between))
                    values(head0 + h)

            with pe.Fori(0, 3) as i:
                two_heads(i)
            two_heads(3, last=True)

        head_units(U_GA, 0)
        with pe.Fori(0, 2) as i:
            for e in range(2):
                unit(U_QA + e + i * 2, U_QA + e + i * 2, hn, (U_QA + e) % 2)
        unit(U_KA, U_KA, hn, U_KA % 2)
        by_token(U_VA, U_VA % 2)
        head_units(U_GB, HB)

        def merge_units(i, first=False):
            for e in range(2):
                u = U_WO + e + i * 2
                pair = (U_WO + e) % 2
                bank_free(u)
                for j in range(SLOTS):
                    if first and e == 0 and j == 2:
                        pe.wait_ge(o_ready, FREE + HEADS)
                    t = KC * ((j + 2) % SLOTS)
                    consume(u, j, 2 * pair + 4 * (j // 2), 2, range(t, t + KC), heads_o, j % 2 == 0, j % 2 == 1)

        merge_units(0, first=True)
        with pe.Fori(1, 4) as i:
            merge_units(i)

        def out_units(i, needs=None):
            for e in range(2):
                unit(U_OUT + e + i * 2, U_OUT + e + i * 2, mixed, (U_OUT + e) % 2, needs=None if e else needs)

        out_units(0, needs=(mix_ready, lambda j: 2 * j + 2))
        with pe.Fori(1, 4) as i:
            out_units(i)
        pe.wait_ge(p_loaded, 16)
        for t in range(KT_PLE):
            for b in range(2):
                mm = pe.transpose(side[:, 2, t * TOK + b * P:t * TOK + (b + 1) * P], p_tok[:, b, t * P:(t + 1) * P], ident[:, :])
        mm.then_inc(p_t, 1)

        def mean_squares(n):
            pe.wait_ge(sq_done, 8 * n)
            pe.matmul(side[:, 0, 0:TOK], ones[:, :], sq_sum[:, 0:TOK], start=True, stop=False)
            pe.matmul(side[:, 0, 0:TOK], ones[:, :], sq_sum[:, TOK:2 * TOK], start=False, stop=True).then_inc(ms_done, 1)

        def ffn_pair(i, first=False):
            for e in range(2):
                opening = first and e == 0
                unit(U_FFN + e + i * 2, U_FFN + e + i * 2, xg, (U_FFN + e) % 2,
                     needs=(xg_ready, lambda j: 4 * j + 4) if opening else None,
                     between=(2, lambda: mean_squares(1)) if opening else None)

        ffn_pair(0, first=True)
        with pe.Fori(1, N_FFN) as i:
            ffn_pair(i)

        def down_groups(i, first=False):
            for e in range(2):
                bank_free(G_DOWN + e + i * 2)
                t = 0
                for c, n in enumerate(DOWN_TILES):
                    if first and e == 0:
                        pe.wait_ge(ff_ready, (t + n + 1) // 2)
                    consume(U_DOWN + 3 * e + c // SLOTS + i * 6, c % SLOTS, 2 * ((G_DOWN + e) % 2), 2,
                            range(t, t + n), ff, c == 0, c == len(DOWN_TILES) - 1)
                    t += n

        down_groups(0, first=True)
        with pe.Fori(1, 4) as i:
            down_groups(i)
        pe.wait_ge(p_ready, 1)
        for c in range(SLOTS):
            if c > 0:
                pe.wait_ge(combined, G_PROJ + 2 * (c - 1))
            consume(U_PROJ, c, 4 * (1 - c % 2), 4, range(KT_PLE), p_cols, True, True, width=2 * GROUP)
        pe.wait_ge(combined, G_PLE - 2)
        mean_squares(2)

        def final_t(n, par):
            pe.wait_ge(fin_ready, 2 * n + 2)
            if not isinstance(n, int) or n > 0:
                pe.wait_ge(fin_read, n)
            for b in range(2):
                for m in range(2):
                    mm = pe.transpose(side[:, 1, b * TOK + m * P:b * TOK + (m + 1) * P], fin[:, par, m, b * P:(b + 1) * P], ident[:, :])
            mm.then_inc(fin_t, 1)

        def ple_unit(i, e, first=False):
            n = e + i * 2
            unit(U_PLE + n, G_PLE + n, xg, (G_PLE + e) % 2,
                 needs=(xg_ready, lambda j: 16 + 4 * j + 4) if first else None,
                 between=None if first else (3, lambda: final_t(n - 1, 1 - e)))

        ple_unit(0, 0, first=True)
        ple_unit(0, 1)
        with pe.Fori(1, 4) as i:
            ple_unit(i, 0)
            ple_unit(i, 1)
        pe.wait_ge(sq_done, 23)
        pe.wait_ge(last_sq, 1)
        for b in range(2):
            for m in range(2):
                for src in (sq_sum, s_a):
                    mm = pe.matmul(side[:, 2, b:b + 1], src[:, m * TOK + b * P:m * TOK + (b + 1) * P], ones[:, 0:1],
                                   start=m == 0 and src is sq_sum, stop=m == 1 and src is s_a)
        mm.then_inc(tok_done, 1)
        final_t(7, 1)

    block.__exit__(None, None, None)


def rope_constants():
    import numpy as np

    rows = np.zeros((P, 4), np.float32)

    def frequencies(half):
        return np.float32(THETA) ** (-np.arange(half, dtype=np.float32) / np.float32(half))

    for rot, col, starts in ((ROT_A, 0, (0,)), (ROT_IDX, 2, (0, D_IDX))):
        half = rot // 2
        for at in starts:
            for side in range(2):
                rows[at + side * half:at + (side + 1) * half, col] = frequencies(half)
                rows[at + side * half:at + (side + 1) * half, col + 1] = 1.0 if side else -1.0
    return rows


_INS = ["x", "p", "positions", "g_mix", "w_in", "b_f", "w_o_a", "w_o_b", "w_out", "g_ffn", "w_ffn_gate",
        "w_ffn_up", "w_ffn_down", "g_ple", "w_ple_gate", "w_ple_proj", "g_final"]


def kernel(**inputs):
    import numpy as np
    import concourse.bacc as bacc
    from concourse.bass_utils import run_bass_kernel_spmd

    nc = bacc.Bacc("TRN2", target_bir_lowering=False, num_devices=1)
    arrays, args = {}, []
    for name in [*_INS, "rope_rows"]:
        a = rope_constants() if name == "rope_rows" else np.ascontiguousarray(inputs[name])
        arrays[f"in_{name}"] = a
        args.append(nc.dram_tensor(f"in_{name}", a.shape, mybir.dt.from_np(a.dtype), kind="ExternalInput").ap())
    out = nc.dram_tensor("out_0", inputs["x"].shape, F32, kind="ExternalOutput").ap()
    hybrid_layer(nc, *args, out)
    r = run_bass_kernel_spmd(nc, [arrays], core_ids=[0])
    return np.asarray(r.results[0]["out_0"])
```

```python
import concourse.bass as bass
from concourse import mybir

F32 = mybir.dt.float32
F32R = mybir.dt.float32r
I32 = mybir.dt.int32
ALU = mybir.AluOpType
ACT = mybir.ActivationFunctionType
AX_X = mybir.AxisListType.X
ds = bass.ds

P = 128
D_MODEL, TOK, D_FF, D_PLE = 2048, 256, 5632, 256
HA, HA_KV, H_IDX, D_IDX, HB, HEAD = 8, 2, 16, 64, 8, 128
ROT_A, ROT_IDX, THETA = HEAD // 4, D_IDX // 4, 500000.0
TOP_K = 64
EPS = 1e-6
KT = D_MODEL // P
KT_O = HA * HEAD // P
KT_FF = D_FF // P
KT_PLE = D_PLE // P
GROUP = 256
SLOTS = 4
KC = 4
CHUNK = KC * GROUP
SCALE = HEAD ** -0.5
MASKED = -3.0e38
TAKEN = -3.4e38
TAKEN_BELOW = -3.2e38
FREE = 1
CAT = P + TOK

AT_QA = 0
AT_KA = AT_QA + HA * HEAD
AT_VA = AT_KA + HA_KV * HEAD
AT_QI = AT_VA + HA_KV * HEAD
AT_KI = AT_QI + H_IDX * D_IDX
AT_WI = AT_KI + D_IDX
AT_QB = AT_WI + H_IDX
AT_KB = AT_QB + HB * HEAD
AT_VB = AT_KB + HB * HEAD
AT_FB = AT_VB + HB * HEAD
AT_GA = AT_FB + HB
AT_GB = AT_GA + D_MODEL

U_SMALL = 0
U_QI = U_SMALL + 1
U_QB = U_QI + 4
U_KB = U_QB + 4
U_VB = U_KB + 4
U_GA = U_VB + 4
U_QA = U_GA + 8
U_KA = U_QA + 4
U_VA = U_KA + 1
U_GB = U_VA + 1
U_WO = U_GB + 8
U_OUT = U_WO + 8
U_FFN = U_OUT + 8
N_FFN = D_FF // GROUP
U_DOWN = U_FFN + 2 * N_FFN
U_PROJ = U_DOWN + 3 * 8
U_PLE = U_PROJ + 1
G_DOWN = U_DOWN
G_PROJ = G_DOWN + 8
G_PLE = G_PROJ + 2 * SLOTS
HALVES = (G_PLE % 2, 1 - G_PLE % 2)
DOWN_TILES = [4] * 8 + [3] * 4
HEADS = HB + HA
W_ROW = D_IDX
F_ROW = 96
F_ROWS = slice(F_ROW, F_ROW + HB)
SMALL = KC * P
STEPS_IDX = H_IDX * D_IDX // P


class Count:

    def __init__(self, eng, sem):
        self.eng, self.sem, self.fixed, self.moving = eng, sem, 0, 0

    def step(self, ins):
        ins.then_inc(self.sem, 1)
        self.fixed += 1
        self.eng.wait_ge(self.sem, self.moving + self.fixed)

    def enter(self, i, steps, first=0):
        self.fixed -= first * steps
        self.start, self.steps, self.moving = self.fixed, steps, i * steps

    def leave(self, end):
        assert self.fixed - self.start == self.steps, self.fixed - self.start
        self.fixed, self.moving = self.start + end * self.steps, 0


def hybrid_layer(nc, c_rows, x, p, positions, g_mix, w_in, b_f, w_o_a, w_o_b, w_out, g_ffn, w_ffn_gate,
                 w_ffn_up, w_ffn_down, g_ple, w_ple_gate, w_ple_proj, g_final, rope_rows, out):
    x_rows = x[0].rearrange("(b q) n -> q b n", q=P)
    p_rows = p[0, 0].rearrange("(b q) n -> q b n", q=P)
    out_rows = out[0].rearrange("(b q) n -> q b n", q=P)

    def tiles_of(w):
        return w[0].rearrange("(t q) n -> q t n", q=P)

    win_t, woa_t, wob_t, wout_t = map(tiles_of, (w_in, w_o_a, w_o_b, w_out))
    wgate_t, wup_t, wdown_t = map(tiles_of, (w_ffn_gate, w_ffn_up, w_ffn_down))
    wpg_t, wpp_t = map(tiles_of, (w_ple_gate, w_ple_proj))

    base = (nc.sbuf_base + 31) // 32 * 32

    def sb(name, kb, shape, dt=F32):
        return nc.alloc_sbuf_tensor_at(name, [P, *shape], dt, offset=base + int(kb * 1024))

    res = sb("res", 0, [KT, TOK])
    heads_o = sb("heads_o", 16, [KT, 2 * TOK], F32R)
    xg = sb("xg", 16, [KT, 2 * TOK], F32R)
    hn = sb("hn", 48, [KT, 2 * TOK], F32R)
    mixed = sb("mixed", 48, [KT, 2 * TOK], F32R)
    ff = sb("ff", 48, [KT_FF, 2 * TOK], F32R)
    gates = sb("gates", 80, [2, KT, TOK])
    q_idx = sb("q_idx", 80, [KT_O, TOK])
    rope = sb("rope", 104, [4, 2 * TOK])
    ang = sb("ang", 88, [2, TOK])
    ang_r = sb("ang_r", 90, [4, TOK])
    turn = sb("turn", 94, [2, TOK])
    relu_sb = sb("relu_sb", 96, [3 * TOK])
    c_keys = sb("c_keys", 96, [HB, TOK])
    kib = sb("kib", 99, [2 * TOK])
    junk = sb("junk", 64, [2, D_MODEL])
    x_tok = sb("x_tok", 112, [2, D_MODEL])
    q_cols = sb("q_cols", 112, [8, TOK])
    k_cols = sb("k_cols", 120, [8, TOK])
    v_rows = sb("v_rows", 128, [2, HB * HEAD])
    lo_ple = sb("lo_ple", 64, [4, 4 * TOK])
    y_ple = sb("y_ple", 48, [KT, TOK])
    out_tok = sb("out_tok", 64, [2, D_MODEL])
    fin = sb("fin", 80, [2, 2, TOK])
    ws = sb("ws", 136, [SLOTS, CHUNK])
    hs = sb("hs", 152, [SLOTS, CHUNK], F32R)
    ls = sb("ls", 168, [SLOTS, CHUNK], F32R)
    lo = sb("lo", 184, [2, 2 * TOK])
    s_a = sb("s_a", 188, [2 * TOK])
    s_b = sb("s_b", 190, [2 * TOK])
    lg = sb("lg", 192, [CAT])
    pt = sb("pt", 193.5, [CAT])
    mask = sb("mask", 196.5, [CAT])
    sel = sb("sel", 198, [CAT])
    kib_h = sb("kib_h", 192, [2 * TOK], F32R)
    kib_l = sb("kib_l", 194, [2 * TOK], F32R)
    qi_h = sb("qi_h", 200.5, [TOK], F32R)
    qi_l = sb("qi_l", 201.5, [TOK], F32R)
    q_st = sb("q_st", 199.5, [TOK])
    k_st = sb("k_st", 200.5, [TOK])
    v_st = sb("v_st", 201.5, [2, P])
    p_tok = sb("p_tok", 192, [2, D_PLE])
    silu_g = sb("silu_g", 192, [2 * TOK])
    lo_b = sb("lo_b", 194, [2, 2 * TOK])
    p_cols = sb("p_cols", 194, [KT_PLE, 2 * TOK], F32R)
    sq_sum = sb("sq_sum", 198, [2 * TOK])
    rms = sb("rms", 200, [2 * TOK])
    ident = sb("ident", 202.5, [P])
    ones = sb("ones", 203, [P])
    c_sum = sb("c_sum", 204, [TOK])
    gains = sb("gains", 205.5, [4 * KT])
    w_tok = sb("w_tok", 205.75, [2, H_IDX])
    c_tok = sb("c_tok", 205.875, [2, HB])
    top8 = sb("top8", 205.9375, [2, 8])
    neg_max = sb("neg_max", 206, [2])
    sums = sb("sums", 206 + 1 / 32, [2])
    rsum = sb("rsum", 206 + 2 / 32, [2])
    r_tok = sb("r_tok", 206 + 3 / 32, [4])
    eps = sb("eps", 206 + 4 / 32, [1])
    bias_f = sb("bias_f", 206 + 6 / 32, [1])
    rope_c = sb("rope_c", 206 + 7 / 32, [4])
    sq = sb("sq", 206.25, [TOK])
    pos_i = sb("pos_i", 101, [TOK], I32)
    pos_f = sb("pos_f", 102, [TOK])
    gain_rows = sb("gain_rows", 103, [P])
    full = sb("full", 80, [2, 2 * TOK])
    rms_x = sb("rms_x", 84, [2 * TOK])
    diag = sb("diag", 86, [2, P])
    f_w = sb("f_w", 112, [4, TOK])

    acc = nc.alloc_psum_tensor("acc", [P, 4, 512], F32)
    side = nc.alloc_psum_tensor("side", [P, 4, 512], F32)

    def x_bank(t):
        return (acc, side)[t % 4 // 2][:, 2 + t % 2, :]

    S = nc.alloc_semaphore
    x_loaded = [S(f"x_loaded{b}") for b in range(2)]
    gains_loaded = S("gains_loaded")
    bias_loaded = S("bias_loaded")
    const_loaded, p_loaded, out_stored = S("const_loaded"), S("p_loaded"), S("out_stored")
    w_loaded = [S(f"w_loaded{j}") for j in range(SLOTS)]
    h_split, l_split, chunk_used = S("h_split"), S("l_split"), S("chunk_used")
    lo_ready, combined = S("lo_ready"), S("combined")
    consts, ring_zero = S("consts"), S("ring_zero")
    pool_step, dve_step, act_step = S("pool_step"), S("dve_step"), S("act_step")
    angles, rope_sin = S("angles"), S("rope_sin")
    gain_t, gain_ready = S("gain_t"), S("gain_ready")
    x_squares, x_rms, diag_ready, rms_b, rms_sb = map(S, (
        "x_squares", "x_rms", "diag_ready", "rms_b", "rms_sb"))
    x_t, res_ready, hn_full, hn_high, hn_ready = map(S, ("x_t", "res_ready", "hn_full", "hn_high", "hn_ready"))
    f_z, f_e, f_l, f_c, small_t, c_t = map(S, (
        "f_z", "f_e", "f_l", "f_c", "small_t", "c_t"))
    small_s = S("small_s")
    staged, v_staged, rope_done = S("staged"), S("v_staged"), S("rope_done")
    dots_done, relu_done, idx_done = S("dots_done"), S("relu_done"), S("idx_done")
    c_stored, c_spread = S("c_stored"), S("c_spread")
    qk_done, max_ready, exp_done = map(S, ("qk_done", "max_ready", "exp_done"))
    prob_ready, pt_done, pt_ready, pv_done, o_high, o_ready = map(S, (
        "prob_ready", "pt_done", "pt_ready", "pv_done", "o_high", "o_ready"))
    gate_ready = S("gate_ready")
    mix_s, mix_high, mix_ready = S("mix_s"), S("mix_high"), S("mix_ready")
    x_new, xg_high, xg_ready, sq_done = S("x_new"), S("xg_high"), S("xg_ready"), S("sq_done")
    ms_done, ms_sqrt, rms_ready = S("ms_done"), S("ms_sqrt"), S("rms_ready")
    p_t, p_high, p_ready = S("p_t"), S("p_high"), S("p_ready")
    ffg_s, ffg_silu, ff_s, ff_high, ff_ready = map(S, ("ffg_s", "ffg_silu", "ff_s", "ff_high", "ff_ready"))
    pg_s, pg_sig, fin_ready, fin_t, fin_read = map(S, ("pg_s", "pg_sig", "fin_ready", "fin_t", "fin_read"))
    tok_done, tok_sqrt, tok_ready, last_sq = map(S, ("tok_done", "tok_sqrt", "tok_ready", "last_sq"))
    y_ready_0, y_ready_1 = S("y_ready_0"), S("y_ready_1")

    block = nc.Block()
    block.__enter__()

    @block.sync
    def _(sp):
        for b in range(2):
            sp.dma_start(x_tok[:, b, :], x_rows[:, b, :]).then_inc(x_loaded[b], 16)
        for n, g in enumerate((g_mix[0], g_ffn[0], g_ple[0], g_final)):
            sp.dma_start(gain_rows[n * KT:(n + 1) * KT, :], g.rearrange("(t q) -> t q", q=P)).then_inc(gains_loaded, 16)
        sp.dma_start(bias_f[F_ROWS, :], b_f[0].rearrange("(h o) -> h o", o=1)).then_inc(bias_loaded, 16)

        def slot_free(u, j):
            sp.wait_ge(l_split, 4 * (u - 1) + j + 1)

        def load(j, src, n=CHUNK):
            parts = src.shape[1]
            sp.dma_start(ws[:, j, 0:n].rearrange("p (t n) -> p t n", t=parts), src).then_inc(w_loaded[j], 16)

        sp.wait_ge(ring_zero, SLOTS)
        for j in range(SLOTS):
            slot = ws[:, j, 0:SMALL].rearrange("p (t n) -> p t n", t=KC)
            rows = win_t[:, KC * j:KC * j + KC, :]
            for at, col, n in ((0, AT_KI, D_IDX + H_IDX), (F_ROW, AT_FB, HB)):
                sp.dma_start(slot[:, :, at:at + n], rows[:, :, col:col + n]).then_inc(w_loaded[j], 16)

        def columns(u0, units, w, col0):
            with sp.Fori(0, units) as i:
                for j in range(SLOTS):
                    slot_free(u0 + i, j)
                    load(j, w[:, KC * j:KC * j + KC, ds(col0 + i * GROUP, GROUP)])

        columns(U_QI, 4, win_t, AT_QI)
        columns(U_QB, 12, win_t, AT_QB)
        columns(U_GA, 8, win_t, AT_GA)
        columns(U_QA, 6, win_t, AT_QA)
        columns(U_GB, 8, win_t, AT_GB)
        with sp.Fori(0, 8) as i:
            for j in range(SLOTS):
                slot_free(U_WO + i, j)
                w, t = (wob_t, woa_t)[j // 2], KC * (j % 2)
                load(j, w[:, t:t + KC, ds(i * GROUP, GROUP)])
        sp.wait_ge(o_ready, FREE + HEADS)
        sp.dma_start(p_tok[:, :, :], p_rows).then_inc(p_loaded, 16)
        columns(U_OUT, 8, wout_t, 0)
        with sp.Fori(0, N_FFN) as i:
            for half, w in enumerate((wgate_t, wup_t)):
                for j in range(SLOTS):
                    slot_free(U_FFN + half + i * 2, j)
                    load(j, w[:, KC * j:KC * j + KC, ds(i * GROUP, GROUP)])
        with sp.Fori(0, 8) as i:
            t = 0
            for c, n in enumerate(DOWN_TILES):
                slot_free(U_DOWN + c // SLOTS + i * 3, c % SLOTS)
                load(c % SLOTS, wdown_t[:, t:t + n, ds(i * GROUP, GROUP)], n * GROUP)
                t += n
        for j in range(SLOTS):
            slot_free(U_PROJ, j)
            load(j, wpp_t[:, :, 2 * GROUP * j:2 * GROUP * (j + 1)])
        columns(U_PLE, 8, wpg_t, 0)
        for n in range(4):
            cols = slice(D_MODEL // 4 * n, D_MODEL // 4 * (n + 1))
            for b in range(2):
                sp.wait_ge((y_ready_0, y_ready_1)[b], n + 1)
                sp.dma_start(out_rows[:, b, cols], out_tok[:, b, cols]).then_inc(out_stored, 16)
        sp.wait_ge(out_stored, 8 * 16)

    @block.gpsimd
    def _(pool):
        chain = Count(pool, pool_step)
        for sem in (dots_done, idx_done, relu_done, qk_done, pv_done, prob_ready, pt_ready, o_ready):
            pool.sem_inc(sem, FREE)
        for j in range(SLOTS):
            slot = ws[:, j, 0:SMALL].rearrange("p (t n) -> p t n", t=KC)
            pool.memset(slot[:, :, W_ROW + H_IDX:P], 0.0).then_inc(ring_zero, 1)
        pool.memset(ones[:, :], 1.0).then_inc(consts, 1)
        pool.memset(eps[:, :], EPS).then_inc(consts, 1)
        pool.memset(c_sum[:, :], 0.0).then_inc(consts, 1)
        pool.memset(kib[:, :], 0.0).then_inc(consts, 1)
        pool.memset(mask[:, :], 0.0).then_inc(consts, 1)
        chain.step(pool.memset(ident[:, :], 0.0))
        pool.wait_ge(consts, 5)
        pool.affine_select(out=ident[:, :], in_=ident[:, :], compare_op=ALU.not_equal, fill=1.0, base=0,
                           pattern=[[-1, P]], channel_multiplier=1).then_inc(consts, 1)
        for at in (0, CAT - P):
            tri = mask[:, at:at + P]
            pool.affine_select(out=tri, in_=tri, compare_op=ALU.is_ge, fill=MASKED, base=0,
                               pattern=[[-1, P]], channel_multiplier=1).then_inc(consts, 1)

        pool.wait_ge(rms_sb, 2)
        for t in range(KT // 2):
            pool.wait_ge(res_ready, t + 1)
            if t >= 2:
                pool.wait_ge(hn_ready, 2 * t - 2)
            pool.tensor_tensor(full[:, t % 2, :], res[:, 2 * t:2 * t + 2, :].rearrange("p m n -> p (m n)"), rms_x[:, :],
                               ALU.mult).then_inc(hn_full, 1)

        pool.wait_ge(rope_done, 4)
        for e in range(STEPS_IDX):
            pool.wait_ge(dots_done, FREE + e)
            chain.step(pool.tensor_copy(qi_h[:, :], q_idx[:, e, :]))
            pool.tensor_tensor(qi_l[:, :], q_idx[:, e, :], qi_h[:, :].bitcast(F32), ALU.subtract).then_inc(staged, 1)

        def stage_head(head, q_at, kv_at, values):
            pool.wait_ge(qk_done, FREE + head)
            pool.tensor_copy(q_st[:, :], q_cols[:, ds(q_at, 1), :]).then_inc(staged, 1)
            pool.tensor_copy(k_st[:, :], k_cols[:, ds(kv_at, 1), :]).then_inc(staged, 1)
            pool.wait_ge(combined, values)
            pool.wait_ge(pv_done, FREE + head)
            pool.tensor_copy(v_st[:, :, :], v_rows[:, :, ds(kv_at * P, P)]).then_inc(v_staged, 1)

        pool.wait_ge(dots_done, FREE + STEPS_IDX)
        pool.wait_ge(combined, U_VB)
        with pool.Fori(0, HB) as h:
            stage_head(h, h, h, U_VB + 4)
        pool.wait_ge(rope_done, 9)
        with pool.Fori(0, HA) as h:
            stage_head(HB + h, h, h // (HA // HA_KV), U_VA + 1)

        def square_sums(n0, groups=8):
            pool.wait_ge(x_new, n0 + 1)
            chain.step(pool.tensor_tensor(sq_sum[:, 0:TOK], res[:, 0, :], res[:, 0, :], ALU.mult))
            pool.tensor_tensor(sq_sum[:, TOK:2 * TOK], res[:, 1, :], res[:, 1, :], ALU.mult).then_inc(sq_done, 1)
            with pool.Fori(0, groups - 1) as i:
                chain.enter(i, 3)
                pool.wait_ge(sq_done, n0 + 1 + i)
                pool.wait_ge(x_new, n0 + 2 + i)
                even, odd = res[:, ds(i * 2 + 2, 1), :], res[:, ds(i * 2 + 3, 1), :]
                chain.step(pool.tensor_tensor(sq[:, :], even, even, ALU.mult))
                chain.step(pool.tensor_tensor(sq_sum[:, 0:TOK], sq_sum[:, 0:TOK], sq[:, :], ALU.add))
                chain.step(pool.tensor_tensor(sq[:, :], odd, odd, ALU.mult))
                pool.tensor_tensor(sq_sum[:, TOK:2 * TOK], sq_sum[:, TOK:2 * TOK], sq[:, :], ALU.add).then_inc(sq_done, 1)
            chain.leave(groups - 1)

        pool.wait_ge(o_ready, FREE + HEADS)
        square_sums(0)
        pool.wait_ge(ms_done, 1)
        square_sums(8)
        pool.wait_ge(ms_done, 2)
        square_sums(16, 7)

    @block.scalar
    def _(act):
        chain = Count(act, act_step)

        def split_high(u, j, n=CHUNK, first=False):
            if first:
                act.wait_ge(w_loaded[j], 2 * 16)
            else:
                act.wait_ge(w_loaded[j], 2 * 16 + 16 * u)
                act.wait_ge(chunk_used, 4 * (u - 1) + j + 1)
            act.activation(hs[:, j, 0:n], ws[:, j, 0:n], ACT.Copy).then_inc(h_split, 1)

        def take_lo(u_done, g, pair, scale=1.0, bank=acc, dst=None, when=None):
            act.wait_ge(chunk_used, 4 * (u_done + 1) if when is None else when)
            dst = lo[:, pair, :] if dst is None else dst
            act.activation(dst.rearrange("p (m n) -> p m n", m=2), bank[:, 2 * pair:2 * pair + 2, TOK:2 * TOK],
                           ACT.Copy, scale=scale).then_inc(lo_ready, 1)

        act.dma_start(pos_i[:, :], positions.partition_broadcast(P)).then_inc(const_loaded, 16)
        act.dma_start(rope_c[:, :], rope_rows).then_inc(const_loaded, 16)

        act.wait_ge(consts, 8)
        act.activation(neg_max[:, 0:1], eps[:, 0:1], ACT.Sqrt).then_inc(act_step, 1)
        chain.fixed += 1
        for b in range(2):
            act.wait_ge(x_loaded[b], 16)
            act.activation(junk[:, b, :], x_tok[:, b, :], ACT.Square, accum_out=r_tok[:, b:b + 1]).then_inc(x_squares, 1)
        act.wait_ge(x_squares, 2)
        act.activation(r_tok[:, 2:4], r_tok[:, 0:2], ACT.Sqrt, bias=eps[:, 0:1], scale=1.0 / D_MODEL).then_inc(x_rms, 1)
        def take_x(t):
            act.wait_ge(x_t, t + 1)
            act.activation(res[:, 2 * t:2 * t + 2, :].rearrange("p m n -> p (m n)"), x_bank(t), ACT.Copy).then_inc(res_ready, 1)

        take_x(0)
        take_x(1)
        act.wait_ge(gain_t, 1)
        act.activation(gains[:, :], side[:, 0, 0:4 * KT], ACT.Copy).then_inc(gain_ready, 1)
        act.wait_ge(rms_b, 1)
        for m in range(2):
            act.activation(rms_x[:, m * TOK:(m + 1) * TOK], side[:, 1, 0:TOK], ACT.Copy).then_inc(rms_sb, 1)
        act.wait_ge(gain_ready, 1)
        for t in range(KT // 2):
            if t % 2 == 0:
                split_high(0, t // 2, SMALL, first=True)
            act.wait_ge(hn_full, t + 1)
            for m in range(2):
                k = 2 * t + m
                act.activation(hn[:, k, 0:TOK], full[:, t % 2, m * TOK:(m + 1) * TOK], ACT.Copy,
                               scale=gains[:, k:k + 1]).then_inc(hn_high, 1)
            if t + 2 < KT // 2:
                take_x(t + 2)
        for j in range(SLOTS):
            split_high(1, j)
        act.wait_ge(chunk_used, SLOTS)
        act.activation(lo[:, 0, 0:TOK], acc[:, 0, TOK:2 * TOK], ACT.Copy).then_inc(lo_ready, 1)

        def sines(k):
            act.wait_ge(angles, k // 2 + 1)
            at = (0, 2, 1, 3)[k]
            for d in range(2):
                act.activation(rope[:, at, d * TOK:(d + 1) * TOK], ang_r[:, k, :], ACT.Sin).then_inc(rope_sin, 1)

        sines(0)
        sines(1)
        split_high(2, 0)
        sines(2)
        sines(3)
        split_high(2, 1)
        act.wait_ge(f_z, 1)
        act.activation(f_w[F_ROWS, 1, :], f_w[F_ROWS, 0, :], ACT.Abs).then_inc(act_step, 1)
        chain.fixed += 1
        act.wait_ge(act_step, chain.fixed)
        act.activation(f_w[F_ROWS, 2, :], f_w[F_ROWS, 1, :], ACT.Exp, scale=-1.0).then_inc(f_e, 1)
        split_high(2, 2)
        split_high(2, 3)
        act.wait_ge(f_l, 1)
        act.activation(f_w[F_ROWS, 1, :], f_w[F_ROWS, 3, :], ACT.Ln).then_inc(f_e, 1)
        take_lo(U_QI, None, U_QI % 2)
        for u in range(U_QI + 1, U_QB):
            for j in range(SLOTS):
                split_high(u + 1, j)
            take_lo(u, None, u % 2)

        act.wait_ge(f_c, 1)
        act.dma_start(c_rows, c_sum[F_ROWS, :]).then_inc(c_stored, 16)

        def plain_units(u0, units, scale=1.0):
            with act.Fori(0, units // 2) as i:
                for e in range(2):
                    for j in range(SLOTS):
                        split_high(u0 + e + 1 + i * 2, j)
                    take_lo(u0 + e + i * 2, None, (u0 + e) % 2, scale)

        def indexer_units(u0, scale, step0):
            with act.Fori(0, 2) as i:
                for e in range(2):
                    step = step0 + e + i * 2
                    for j in range(SLOTS):
                        split_high(u0 + e + 1 + i * 2, j)
                    take_lo(u0 + e + i * 2, None, (u0 + e) % 2, scale)
                    act.wait_ge(dots_done, FREE + 1 + step)
                    act.wait_ge(idx_done, FREE + step)
                    act.activation(relu_sb[:, 0:TOK], side[:, 0, 0:TOK], ACT.Relu).then_inc(relu_done, 1)
                    act.activation(relu_sb[:, TOK:3 * TOK], side[:, 1, :], ACT.Relu).then_inc(relu_done, 1)

        indexer_units(U_QB, SCALE, 0)
        indexer_units(U_KB, 1.0, 4)
        for i in range(4):
            for j in range(SLOTS):
                split_high(U_VB + 1 + i, j)
            if i == 0:
                act.wait_ge(c_stored, 16)
                act.wait_ge(idx_done, FREE + STEPS_IDX)
                act.dma_start(c_keys[:, :, :], c_rows.partition_broadcast(P)).then_inc(c_spread, 16)

        def head_units(u0, head0):
            with act.Fori(0, 4) as i:
                for e in range(2):
                    head = head0 + e + i * 2
                    act.wait_ge(max_ready, 2 * head + 2)
                    for b, cols in enumerate((slice(0, P), slice(P, CAT))):
                        act.activation(lg[:, cols], lg[:, cols], ACT.Exp, bias=neg_max[:, b:b + 1],
                                       accum_out=sums[:, b:b + 1]).then_inc(exp_done, 1)
                    split_high(u0 + e + 1 + i * 2, 0)
                    split_high(u0 + e + 1 + i * 2, 1)
                    split_high(u0 + e + 1 + i * 2, 2)
                    act.wait_ge(pt_done, head + 1)
                    act.activation(pt[:, :], side[:, 2, 0:CAT], ACT.Copy).then_inc(pt_ready, 1)
                    split_high(u0 + e + 1 + i * 2, 3)
                    take_lo(u0 + e + i * 2, None, (u0 + e) % 2)
                    act.wait_ge(pv_done, FREE + 1 + head)
                    tile = (KT_O if head0 == 0 else -HB) + head
                    act.activation(heads_o[:, ds(tile, 1), 0:TOK], side[:, 3, 0:TOK], ACT.Copy).then_inc(o_high, 1)

        head_units(U_GA, 0)
        plain_units(U_QA, 4, SCALE)
        for j in range(SLOTS):
            split_high(U_KA + 1, j)
        take_lo(U_KA, None, U_KA % 2)
        for j in range(SLOTS):
            split_high(U_VA + 1, j)
        head_units(U_GB, HB)

        def mixed_high(n):
            act.wait_ge(mix_s, n + 1)
            act.activation(mixed[:, ds(n * 2, 2), 0:TOK], s_a[:, :].rearrange("p (m n) -> p m n", m=2),
                           ACT.Copy).then_inc(mix_high, 1)

        def merge_unit(i, e, first=False):
            n = e + i * 2
            u = U_WO + n
            pair = (U_WO + e) % 2
            split_high(u + 1, 0)
            if not first:
                mixed_high(n - 1)
            split_high(u + 1, 1)
            for b in (1, 0):
                act.activation(gates[:, b, ds(n * 2, 2), :], gates[:, b, ds(n * 2, 2), :], ACT.Sigmoid).then_inc(gate_ready, 1)
            take_lo(None, None, pair, when=4 * u + 2)
            split_high(u + 1, 2)
            split_high(u + 1, 3)
            take_lo(u, None, pair, 1.0, side, lo_b[:, pair, :])

        act.wait_ge(combined, U_WO)
        merge_unit(0, 0, first=True)
        merge_unit(0, 1)
        with act.Fori(1, 4) as i:
            merge_unit(i, 0)
            merge_unit(i, 1)
        mixed_high(7)

        def new_x(n, gain):
            act.wait_ge(x_new, n + 1)
            tile = (n - (0 if gain == KT else 8)) * 2
            for m in range(2):
                act.activation(xg[:, ds(tile + m, 1), 0:TOK], res[:, ds(tile + m, 1), :], ACT.Copy,
                               scale=gains[:, ds(tile + (gain + m), 1)]).then_inc(xg_high, 1)

        with act.Fori(0, 4) as i:
            for e in range(2):
                for j in range(SLOTS):
                    split_high(U_OUT + e + 1 + i * 2, j)
                take_lo(U_OUT + e + i * 2, None, (U_OUT + e) % 2)
                new_x(e + i * 2, KT)
        act.wait_ge(p_t, 1)
        act.activation(p_cols[:, :, 0:TOK], side[:, 2, :].rearrange("p (m n) -> p m n", m=2), ACT.Copy).then_inc(p_high, 1)

        def root(n):
            act.wait_ge(ms_done, n)
            act.activation(sq[:, :], side[:, 0, 0:TOK], ACT.Sqrt, bias=eps[:, 0:1], scale=1.0 / D_MODEL).then_inc(ms_sqrt, 1)

        def ffn_pair(i, first=False):
            u = U_FFN + i * 2
            for j in range(SLOTS):
                if first and j == 3:
                    root(1)
                split_high(u + 1, j)
            take_lo(u, None, U_FFN % 2)
            act.wait_ge(ffg_s, 1 + i)
            act.activation(silu_g[:, :], s_a[:, :], ACT.Silu).then_inc(ffg_silu, 1)
            for j in range(SLOTS):
                split_high(u + 2, j)
            take_lo(u + 1, None, (U_FFN + 1) % 2)
            act.wait_ge(ff_s, 1 + i)
            act.activation(ff[:, ds(i * 2, 2), 0:TOK], s_b[:, :].rearrange("p (m n) -> p m n", m=2),
                           ACT.Copy).then_inc(ff_high, 1)

        ffn_pair(0, first=True)
        with act.Fori(1, N_FFN) as i:
            ffn_pair(i)

        def proj_lo(c):
            act.wait_ge(chunk_used, 4 * U_PROJ + c + 1)
            for m in HALVES:
                act.activation(lo_ple[:, c, 2 * m * TOK:2 * (m + 1) * TOK].rearrange("p (m n) -> p m n", m=2),
                               (side, acc)[c % 2][:, 2 * m:2 * m + 2, TOK:2 * TOK], ACT.Copy).then_inc(lo_ready, 1)

        def down_group(i, e, last=False):
            u = U_DOWN + 3 * e + i * 6
            for j in range(SLOTS):
                split_high(u + 1, j)
            for j in range(SLOTS):
                split_high(u + 2, j, 3 * GROUP)
            for j in range(SLOTS):
                split_high(u + 3, j)
            take_lo(u + 2, None, (G_DOWN + e) % 2)
            if last:
                proj_lo(0)
            new_x(8 + e + i * 2, 2 * KT)

        with act.Fori(0, 3) as i:
            down_group(i, 0)
            down_group(i, 1)
        down_group(3, 0)
        down_group(3, 1, last=True)
        for c in range(SLOTS):
            if c > 0:
                proj_lo(c)
            split_high(U_PLE, c)
        root(2)

        def ple_unit(i, e, first=False):
            n = e + i * 2
            for j in range(SLOTS):
                split_high(U_PLE + 1 + n, j)
            take_lo(U_PLE + n, None, (G_PLE + e) % 2)
            if not first:
                take_fin(n - 1)
            act.wait_ge(pg_s, n + 1)
            act.activation(s_b[:, :], s_a[:, :], ACT.Sigmoid).then_inc(pg_sig, 1)
            act.wait_ge(x_new, 17 + n)
            for m in range(2):
                act.activation(fin[:, e, m, :], res[:, ds(n * 2 + m, 1), :], ACT.Copy,
                               scale=gains[:, ds(n * 2 + (3 * KT + m), 1)]).then_inc(fin_ready, 1)

        def take_fin(n):
            act.wait_ge(fin_t, n + 1)
            act.activation(out_tok[:, :, ds(n * GROUP, GROUP)], side[:, 1, :].rearrange("p (b n) -> p b n", b=2),
                           ACT.Copy).then_inc(fin_read, 1)

        ple_unit(0, 0, first=True)
        ple_unit(0, 1)
        with act.Fori(1, 3) as i:
            ple_unit(i, 0)
            ple_unit(i, 1)
        ple_unit(3, 0)
        pair = (G_PLE + 1) % 2
        for m in range(2):
            half = slice(m * TOK, (m + 1) * TOK)
            act.wait_ge(chunk_used, 4 * (U_PLE + 7) + 2 * m + 2)
            act.activation(lo[:, pair, half], acc[:, 2 * pair + m, TOK:2 * TOK], ACT.Copy).then_inc(lo_ready, 1)
            if m == 0:
                take_fin(6)
            act.wait_ge(pg_s, 8 + m)
            act.activation(s_b[:, half], s_a[:, half], ACT.Sigmoid).then_inc(pg_sig, 1)
            if m == 1:
                act.activation(neg_max[:, 0:1], eps[:, 0:1], ACT.Sqrt).then_inc(act_step, 1)
            act.wait_ge(x_new, 24 + m)
            act.activation(fin[:, 1, m, :], res[:, 14 + m, :], ACT.Copy,
                           scale=gains[:, 3 * KT + 14 + m:3 * KT + 15 + m]).then_inc(fin_ready, 1)
        take_fin(7)
        act.wait_ge(tok_done, 1)
        act.activation(r_tok[:, 2:4].rearrange("p (b o) -> p b o", o=1), side[:, 2:4, 0:1], ACT.Sqrt,
                       bias=eps[:, 0:1], scale=1.0 / D_MODEL).then_inc(tok_sqrt, 1)
        act.wait_ge(tok_ready, 1)
        act.wait_ge(fin_read, 8)
        for n in range(4):
            cols = slice(D_MODEL // 4 * n, D_MODEL // 4 * (n + 1))
            act.activation(out_tok[:, 1, cols], out_tok[:, 1, cols], ACT.Copy, scale=r_tok[:, 1:2]).then_inc(y_ready_1, 1)

    @block.vector
    def _(dve):
        chain = Count(dve, dve_step)

        def split_low(u, j, n=CHUNK):
            dve.wait_ge(h_split, 4 * u + j + 1)
            dve.tensor_tensor(ls[:, j, 0:n], ws[:, j, 0:n], hs[:, j, 0:n].bitcast(F32), ALU.subtract).then_inc(l_split, 1)

        def two(t):
            return t.rearrange("p (m n) -> p m n", m=2)

        def combine(dst, g, pair, lo_count, scale=1.0, tables=False):
            dve.wait_ge(lo_ready, lo_count)
            dve.scalar_tensor_tensor(dst, acc[:, 2 * pair:2 * pair + 2, 0:TOK], scale, two(lo[:, pair, :]),
                                     ALU.mult, ALU.add).then_inc(combined, 1)
            if tables:
                dve.wait_ge(rope_sin, 10)
            dve.wait_ge(combined, g + 1)

        two_pi = 6.283185307179586
        parts = (6.28125, 0.0019350051879882812, 3.0199159819568e-07)
        rounder = 12582912.0
        dve.wait_ge(const_loaded, 2 * 16)
        chain.step(dve.tensor_copy(pos_f[:, :], pos_i[:, :]))
        for k, col in enumerate((2, 0)):
            chain.step(dve.tensor_scalar(ang[:, k, :], pos_f[:, :], rope_c[:, col:col + 1], None, ALU.mult))

        def whole_turns(k):
            chain.step(dve.tensor_scalar(turn[:, :, :], ang[:, :, :], 1.0 / two_pi, (0.25, 0.0)[k], ALU.mult, ALU.add))
            chain.step(dve.tensor_scalar(turn[:, :, :], turn[:, :, :], rounder, None, ALU.add))
            chain.step(dve.tensor_scalar(turn[:, :, :], turn[:, :, :], rounder, None, ALU.subtract))

        def less_turns(k, n):
            r = ang_r[:, 2 * k:2 * k + 2, :]
            chain.step(dve.scalar_tensor_tensor(r, turn[:, :, :], -parts[n], r if n else ang[:, :, :], ALU.mult, ALU.add))

        def clamp_angles(k):
            r = ang_r[:, 2 * k:2 * k + 2, :]
            chain.step(dve.tensor_scalar(r, r, (0.25, 0.0)[k] * two_pi, 3.1415925, ALU.add, ALU.min))
            dve.tensor_scalar(r, r, -3.1415925, None, ALU.max).then_inc(angles, 1)

        whole_turns(0)

        dve.wait_ge(x_rms, 1)
        chain.step(dve.reciprocal(r_tok[:, 0:2], r_tok[:, 2:4]))
        for b in range(2):
            dve.tensor_scalar(diag[:, b, :], ident[:, :], r_tok[:, b:b + 1], None, ALU.mult).then_inc(diag_ready, 1)
        dve.wait_ge(gain_ready, 1)
        for t in range(KT // 2):
            if t % 2 == 0:
                split_low(0, t // 2, SMALL)
            dve.wait_ge(hn_full, t + 1)
            for m in range(2):
                k = 2 * t + m
                dve.wait_ge(hn_high, k + 1)
                dve.scalar_tensor_tensor(hn[:, k, TOK:2 * TOK], full[:, t % 2, m * TOK:(m + 1) * TOK], gains[:, k:k + 1],
                                         hn[:, k, 0:TOK].bitcast(F32), ALU.mult, ALU.subtract).then_inc(hn_ready, 1)
            if t < len(parts):
                less_turns(0, t)
        for j in range(SLOTS):
            split_low(1, j)
        clamp_angles(0)
        dve.wait_ge(lo_ready, 1)
        dve.tensor_tensor(s_a[:, 0:TOK], acc[:, 0, 0:TOK], lo[:, 0, 0:TOK], ALU.add).then_inc(combined, 1)
        dve.wait_ge(combined, 1)
        dve.wait_ge(bias_loaded, 16)
        dve.tensor_scalar(f_w[F_ROWS, 0, :], s_a[F_ROWS, 0:TOK], bias_f[F_ROWS, 0:1], None, ALU.add).then_inc(f_z, 1)
        whole_turns(1)
        for n in range(len(parts)):
            less_turns(1, n)
        clamp_angles(1)
        split_low(2, 0)
        dve.wait_ge(rope_sin, 8)
        for at, col in ((1, 3), (3, 1)):
            dve.tensor_scalar(rope[:, at, :], rope[:, at, :], rope_c[:, col:col + 1], None, ALU.mult).then_inc(rope_sin, 1)

        swap_idx = [8 + i if i < 8 else i - 8 if i < 16 else i for i in range(32)]
        swap_a = [(i + 16) % 32 for i in range(32)]

        split_low(2, 1)
        dve.wait_ge(rope_sin, 10)
        k_rows = slice(0, D_IDX)
        chain.step(dve.stream_shuffle(s_b[k_rows, 0:TOK], s_a[k_rows, 0:TOK], swap_idx))
        chain.step(dve.tensor_tensor(s_b[k_rows, 0:TOK], s_b[k_rows, 0:TOK], rope[k_rows, 1, 0:TOK], ALU.mult))
        chain.step(dve.tensor_tensor(s_b[k_rows, TOK:2 * TOK], s_a[k_rows, 0:TOK], rope[k_rows, 0, 0:TOK], ALU.mult))
        for m in range(2):
            dve.tensor_tensor(kib[D_IDX * m:D_IDX * (m + 1), m * TOK:(m + 1) * TOK], s_b[k_rows, 0:TOK],
                              s_b[k_rows, TOK:2 * TOK], ALU.add).then_inc(small_s, 1)

        def split_keys():
            dve.tensor_copy(kib_h[:, :], kib[:, :]).then_inc(small_s, 1)
            dve.wait_ge(small_s, 3)
            dve.tensor_tensor(kib_l[:, :], kib[:, :], kib_h[:, :].bitcast(F32), ALU.subtract).then_inc(small_s, 1)

        def forget_exp():
            dve.wait_ge(f_e, 1)
            dve.tensor_scalar(f_w[F_ROWS, 3, :], f_w[F_ROWS, 2, :], 1.0, None, ALU.add).then_inc(f_l, 1)

        def forget_sums():
            dve.wait_ge(f_e, 2)
            chain.step(dve.scalar_tensor_tensor(f_w[F_ROWS, 2, :], f_w[F_ROWS, 0, :], 0.0, f_w[F_ROWS, 1, :], ALU.min, ALU.subtract))
            chain.step(dve.memset(f_w[F_ROWS, 3, :], 1.0))
            dve.tensor_tensor_scan(c_sum[F_ROWS, :], f_w[F_ROWS, 3, :], f_w[F_ROWS, 2, :], 0.0, ALU.mult, ALU.add).then_inc(f_c, 1)

        def index_weights():
            dve.wait_ge(small_t, 1)
            for b in range(2):
                chain.step(dve.tensor_scalar(w_tok[:, b, :], side[:, 2, b * P + W_ROW:b * P + W_ROW + H_IDX],
                                             H_IDX ** -0.5 * D_IDX ** -0.5, None, ALU.mult))
            chain.step(dve.memset(sel[:, :], 0.0))

        def rotate(dst, t, table, swap, mask_rows):
            rows = slice(0, mask_rows)
            chain.step(dve.stream_shuffle(s_b[rows, :], t[rows, :], swap))
            chain.step(dve.tensor_tensor(s_b[rows, :], s_b[rows, :], rope[rows, table + 1, :], ALU.mult))
            chain.step(dve.tensor_tensor(t[rows, :], t[rows, :], rope[rows, table, :], ALU.mult))
            dve.tensor_tensor(dst[rows], two(t[rows, :]), two(s_b[rows, :]), ALU.add).then_inc(rope_done, 1)

        dve.wait_ge(small_s, 2)
        for n in range(4):
            g = U_QI + n
            for j in range((2, 1, 0, 0)[n], SLOTS):
                split_low(g + 1, j)
                if n == 0 and j == 2:
                    forget_exp()
            if n == 0:
                index_weights()
            if n == 1:
                forget_sums()
            if n == 2:
                split_keys()
            combine(two(s_a[:, :]), g, g % 2, g + 1)
            if n == 0:
                split_low(g + 2, 0)
            rotate(q_idx[:, 2 * n:2 * n + 2, :], s_a, 0, swap_idx, P)
            dve.wait_ge(rope_done, 1 + n)
        dve.wait_ge(f_c, 1)

        cats = (slice(0, P), slice(P, CAT))

        def indexer_units(u0, dst, scale, step0):
            with dve.Fori(0, 2) as i:
                chain.enter(i, 6)
                for e in range(2):
                    step = step0 + e + i * 2
                    g = u0 + e + i * 2
                    for j in range(SLOTS):
                        split_low(g + 1, j)
                    combine(dst[:, ds((e + i * 2) * 2, 2), :], g, (u0 + e) % 2, g + 1, scale)
                    dve.wait_ge(relu_done, FREE + 2 + step * 2)
                    for hh in range(2):
                        w_col = step * 2 + hh
                        dots = (relu_sb[:, hh * P:(hh + 1) * P], relu_sb[:, TOK * (1 + hh):TOK * (2 + hh)])
                        for b in range(2):
                            ins = dve.scalar_tensor_tensor(sel[:, cats[b]], dots[b], w_tok[:, b, ds(w_col, 1)],
                                                           sel[:, cats[b]], ALU.mult, ALU.add)
                            if hh == 1 and b == 1:
                                ins.then_inc(idx_done, 1)
                                dve.wait_ge(idx_done, FREE + 1 + step)
                            else:
                                chain.step(ins)
            chain.leave(2)

        indexer_units(U_QB, q_cols, SCALE, 0)
        indexer_units(U_KB, k_cols, 1.0, 4)
        chain.step(dve.tensor_tensor(sel[:, :], sel[:, :], mask[:, :], ALU.add))

        dve.wait_ge(c_t, 1)
        for b in range(2):
            chain.step(dve.tensor_copy(c_tok[:, b, :], side[:, 3, b * P + F_ROW:b * P + F_ROW + HB]))

        for i in range(4):
            g = U_VB + i
            for _ in range(TOP_K // 8 // 4):
                for b in range(2):
                    chain.step(dve.max(top8[:, b, :], sel[:, cats[b]]))
                    chain.step(dve.match_replace(sel[:, cats[b]], top8[:, b, :], sel[:, cats[b]], TAKEN))
            for j in range(SLOTS):
                split_low(g + 1, j)
            dve.wait_ge(chunk_used, 4 * g + 4)
            dve.tensor_copy(v_rows[:, :, i * GROUP:(i + 1) * GROUP],
                            acc[:, 2 * (g % 2):2 * (g % 2) + 2, 0:TOK]).then_inc(combined, 1)
        chain.step(dve.tensor_scalar(sel[:, :], sel[:, :], TAKEN_BELOW, 1.0, ALU.is_le, ALU.subtract))
        chain.step(dve.scalar_tensor_tensor(sel[:, :], sel[:, :], -MASKED, mask[:, :], ALU.mult, ALU.min))

        def head_units(u0, head0, lo_off, per_pass):
            forget = head0 == 0
            with dve.Fori(0, 4) as i:
                chain.enter(i, per_pass)
                for e in range(2):
                    h = e + i * 2
                    head = head0 + h
                    g = u0 + h
                    dve.wait_ge(qk_done, FREE + 1 + head)
                    if forget:
                        for b in range(2):
                            chain.step(dve.scalar_tensor_tensor(lg[:, cats[b]], side[:, 0, cats[b]], c_tok[:, b, ds(h, 1)],
                                                                mask[:, cats[b]], ALU.add, ALU.add))
                            chain.step(dve.tensor_tensor(lg[:, cats[b]], lg[:, cats[b]],
                                                         c_keys[:, ds(h, 1), 0:(b + 1) * P].rearrange("p o n -> p (o n)"),
                                                         ALU.subtract))
                    else:
                        chain.step(dve.tensor_tensor(lg[:, :], side[:, 0, 0:CAT], sel[:, :], ALU.add))
                    for b in range(2):
                        dve.tensor_reduce(neg_max[:, b:b + 1], lg[:, cats[b]], AX_X, ALU.max, negate=True).then_inc(max_ready, 1)
                    dve.wait_ge(exp_done, 2 * head + 2)
                    chain.step(dve.reciprocal(rsum[:, :], sums[:, :]))
                    for b in range(2):
                        dve.tensor_scalar(lg[:, cats[b]], lg[:, cats[b]], rsum[:, b:b + 1], None, ALU.mult).then_inc(prob_ready, 1)
                    for j in range(SLOTS):
                        split_low(g + 1, j)
                    combine(gates[:, head0 // HB, ds(h * 2, 2), :], g, (u0 + e) % 2, g + 1 - lo_off)
                    dve.wait_ge(o_high, head + 1)
                    tile = (KT_O if forget else 0) + h
                    dve.tensor_tensor(heads_o[:, ds(tile, 1), TOK:2 * TOK], side[:, 3:4, 0:TOK],
                                      heads_o[:, ds(tile, 1), 0:TOK].bitcast(F32), ALU.subtract).then_inc(o_ready, 1)
            chain.leave(4)

        dve.wait_ge(c_spread, 16)
        head_units(U_GA, 0, 4, 10)

        def rotate_a(dst):
            rows = slice(0, ROT_A)
            chain.step(dve.stream_shuffle(s_b[rows, :], s_a[rows, :], swap_a))
            chain.step(dve.tensor_tensor(s_b[rows, :], s_b[rows, :], rope[rows, 3, :], ALU.mult))
            chain.step(dve.tensor_tensor(s_a[rows, :], s_a[rows, :], rope[rows, 2, :], ALU.mult))
            chain.step(dve.tensor_tensor(s_a[rows, :], s_a[rows, :], s_b[rows, :], ALU.add))
            dve.tensor_copy(dst, two(s_a[:, :])).then_inc(rope_done, 1)

        with dve.Fori(0, 2) as i:
            chain.enter(i, 8)
            for e in range(2):
                g = U_QA + e + i * 2
                for j in range(SLOTS):
                    split_low(g + 1, j)
                dve.wait_ge(rope_done, 4 + e + i * 2)
                combine(two(s_a[:, :]), g, (U_QA + e) % 2, g + 1 - 4, SCALE, tables=True)
                rotate_a(q_cols[:, ds((e + i * 2) * 2, 2), :])
        chain.leave(2)
        for j in range(SLOTS):
            split_low(U_KA + 1, j)
        dve.wait_ge(rope_done, 8)
        combine(two(s_a[:, :]), U_KA, U_KA % 2, U_KA + 1 - 4)
        rotate_a(k_cols[:, 0:2, :])
        dve.wait_ge(rope_done, 9)
        for j in range(SLOTS):
            split_low(U_VA + 1, j)
        dve.wait_ge(chunk_used, 4 * U_VA + 4)
        pair = U_VA % 2
        dve.wait_ge(v_staged, HB)
        dve.tensor_copy(v_rows[:, :, 0:GROUP], acc[:, 2 * pair:2 * pair + 2, 0:TOK]).then_inc(combined, 1)
        head_units(U_GB, HB, 5, 4)

        def mixed_low(n):
            dve.wait_ge(mix_high, n + 1)
            dve.tensor_tensor(mixed[:, ds(n * 2, 2), TOK:2 * TOK], two(s_a[:, :]),
                              mixed[:, ds(n * 2, 2), 0:TOK].bitcast(F32), ALU.subtract).then_inc(mix_ready, 1)
            dve.wait_ge(mix_ready, n + 1)

        def merge_unit(i, e, first=False):
            n = e + i * 2
            g = U_WO + n
            pair = (U_WO + e) % 2
            split_low(g + 1, 0)
            if not first:
                mixed_low(n - 1)
            split_low(g + 1, 1)
            dve.wait_ge(lo_ready, U_WO - 5 + 1 + n * 2)
            chain.step(dve.tensor_tensor(two(s_a[:, :]), acc[:, 2 * pair:2 * pair + 2, 0:TOK], two(lo[:, pair, :]), ALU.add))
            dve.wait_ge(gate_ready, 2 * n + 1)
            chain.step(dve.tensor_tensor(two(s_a[:, :]), two(s_a[:, :]), gates[:, 1, ds(n * 2, 2), :], ALU.mult))
            split_low(g + 1, 2)
            split_low(g + 1, 3)
            dve.wait_ge(lo_ready, U_WO - 5 + 2 + n * 2)
            dve.tensor_tensor(two(s_b[:, :]), side[:, 2 * pair:2 * pair + 2, 0:TOK], two(lo_b[:, pair, :]),
                              ALU.add).then_inc(combined, 1)
            dve.wait_ge(gate_ready, 2 * n + 2)
            dve.wait_ge(combined, g + 1)
            chain.step(dve.tensor_tensor(two(s_b[:, :]), two(s_b[:, :]), gates[:, 0, ds(n * 2, 2), :], ALU.mult))
            dve.tensor_tensor(s_a[:, :], s_a[:, :], s_b[:, :], ALU.add).then_inc(mix_s, 1)

        merge_unit(0, 0, first=True)
        merge_unit(0, 1)
        with dve.Fori(1, 4) as i:
            chain.enter(i, 6, first=1)
            merge_unit(i, 0)
            merge_unit(i, 1)
        chain.leave(4)
        mixed_low(7)

        LO_OUT = U_OUT - 5 + 8

        def new_x(n, n0, gain, between=None):
            tile = (n - n0) * 2
            dve.tensor_tensor(res[:, ds(tile, 2), :], two(s_a[:, :]), res[:, ds(tile, 2), :], ALU.add).then_inc(x_new, 1)
            if between is not None:
                between()
            dve.wait_ge(xg_high, 2 * n + 2)
            for m in range(2):
                dve.scalar_tensor_tensor(xg[:, ds(tile + m, 1), TOK:2 * TOK], res[:, ds(tile + m, 1), :],
                                         gains[:, ds(tile + (gain + m), 1)], xg[:, ds(tile + m, 1), 0:TOK].bitcast(F32),
                                         ALU.mult, ALU.subtract).then_inc(xg_ready, 1)

        with dve.Fori(0, 4) as i:
            for e in range(2):
                n = e + i * 2
                for j in range(SLOTS):
                    split_low(U_OUT + 1 + n, j)
                combine(two(s_a[:, :]), U_OUT + n, (U_OUT + e) % 2, LO_OUT + 1 + n)
                new_x(n, 0, KT)
        dve.wait_ge(p_high, 1)
        dve.tensor_tensor(p_cols[:, :, TOK:2 * TOK], two(side[:, 2, :]), p_cols[:, :, 0:TOK].bitcast(F32),
                          ALU.subtract).then_inc(p_ready, 1)

        def reciprocal_rms(n):
            dve.wait_ge(ms_sqrt, n)
            dve.reciprocal(rms[:, 0:TOK], sq[:, :]).then_inc(rms_ready, 1)
            dve.wait_ge(rms_ready, 2 * n - 1)
            dve.tensor_copy(rms[:, TOK:2 * TOK], rms[:, 0:TOK]).then_inc(rms_ready, 1)
            dve.wait_ge(rms_ready, 2 * n)

        LO_FFN = LO_OUT + 8
        dve.wait_ge(x_new, 8)

        def ffn_pair(i, first=False):
            g = U_FFN + i * 2
            for j in range(SLOTS):
                if first and j == 3:
                    reciprocal_rms(1)
                split_low(g + 1, j)
            combine(two(s_a[:, :]), g, U_FFN % 2, LO_FFN + 1 + i * 2)
            dve.tensor_tensor(s_a[:, :], s_a[:, :], rms[:, :], ALU.mult).then_inc(ffg_s, 1)
            for j in range(SLOTS):
                split_low(g + 2, j)
            combine(two(s_b[:, :]), g + 1, (U_FFN + 1) % 2, LO_FFN + 2 + i * 2)
            chain.step(dve.tensor_tensor(s_b[:, :], s_b[:, :], rms[:, :], ALU.mult))
            dve.wait_ge(ffg_silu, 1 + i)
            dve.tensor_tensor(s_b[:, :], s_b[:, :], silu_g[:, :], ALU.mult).then_inc(ff_s, 1)
            dve.wait_ge(ff_high, 1 + i)
            dve.tensor_tensor(ff[:, ds(i * 2, 2), TOK:2 * TOK], two(s_b[:, :]), ff[:, ds(i * 2, 2), 0:TOK].bitcast(F32),
                              ALU.subtract).then_inc(ff_ready, 1)
            dve.wait_ge(ff_ready, 1 + i)

        ffn_pair(0, first=True)
        with dve.Fori(1, N_FFN) as i:
            chain.enter(i, 1, first=1)
            ffn_pair(i)
        chain.leave(N_FFN)

        LO_DOWN = LO_FFN + 2 * N_FFN
        LO_PROJ = LO_DOWN + 8

        def proj_chunk(c):
            for at, m in enumerate(HALVES):
                dve.wait_ge(lo_ready, LO_PROJ + 2 * c + at + 1)
                dve.tensor_tensor(y_ple[:, 4 * c + 2 * m:4 * c + 2 * m + 2, :], (side, acc)[c % 2][:, 2 * m:2 * m + 2, 0:TOK],
                                  two(lo_ple[:, c, 2 * m * TOK:2 * (m + 1) * TOK]), ALU.add).then_inc(combined, 1)

        def down_group(i, e, last=False):
            u = U_DOWN + 3 * e + i * 6
            n = e + i * 2
            for j in range(SLOTS):
                split_low(u + 1, j)
            for j in range(SLOTS):
                split_low(u + 2, j, 3 * GROUP)
            for j in range(SLOTS):
                split_low(u + 3, j)
            combine(two(s_a[:, :]), G_DOWN + n, (G_DOWN + e) % 2, LO_DOWN + 1 + n)
            new_x(8 + n, 8, 2 * KT, between=(lambda: proj_chunk(0)) if last else None)

        with dve.Fori(0, 3) as i:
            down_group(i, 0)
            down_group(i, 1)
        down_group(3, 0)
        down_group(3, 1, last=True)
        dve.wait_ge(x_new, 16)
        for c in range(SLOTS):
            if c > 0:
                proj_chunk(c)
            split_low(U_PLE, c)
        reciprocal_rms(2)
        LO_PLE = LO_PROJ + 2 * SLOTS

        def ple_unit(i, e):
            n = e + i * 2
            for j in range(SLOTS):
                split_low(U_PLE + 1 + n, j)
            combine(two(s_a[:, :]), G_PLE + n, (G_PLE + e) % 2, LO_PLE + 1 + n)
            dve.tensor_tensor(s_a[:, :], s_a[:, :], rms[:, :], ALU.mult).then_inc(pg_s, 1)
            dve.wait_ge(pg_sig, n + 1)
            chain.step(dve.tensor_tensor(two(s_b[:, :]), two(s_b[:, :]), y_ple[:, ds(n * 2, 2), :], ALU.mult))
            dve.tensor_tensor(res[:, ds(n * 2, 2), :], two(s_b[:, :]), res[:, ds(n * 2, 2), :], ALU.add).then_inc(x_new, 1)

        with dve.Fori(0, 3) as i:
            chain.enter(i, 2)
            ple_unit(i, 0)
            ple_unit(i, 1)
        chain.leave(3)
        ple_unit(3, 0)
        pair = (G_PLE + 1) % 2
        for m in range(2):
            half, tile = slice(m * TOK, (m + 1) * TOK), 14 + m
            dve.wait_ge(lo_ready, LO_PLE + 8 + m)
            chain.step(dve.tensor_tensor(s_a[:, half], acc[:, 2 * pair + m, 0:TOK], lo[:, pair, half], ALU.add))
            dve.tensor_tensor(s_a[:, half], s_a[:, half], rms[:, half], ALU.mult).then_inc(pg_s, 1)
            dve.wait_ge(pg_sig, 8 + m)
            chain.step(dve.tensor_tensor(s_b[:, half], s_b[:, half], y_ple[:, tile, :], ALU.mult))
            dve.tensor_tensor(res[:, tile, :], s_b[:, half], res[:, tile, :], ALU.add).then_inc(x_new, 1)
            dve.wait_ge(x_new, 24 + m)
            dve.tensor_tensor(s_a[:, half], res[:, tile, :], res[:, tile, :], ALU.mult).then_inc(last_sq, 1)
        dve.wait_ge(tok_sqrt, 1)
        dve.reciprocal(r_tok[:, 0:2], r_tok[:, 2:4]).then_inc(tok_ready, 1)
        dve.wait_ge(tok_ready, 1)
        dve.wait_ge(fin_read, 8)
        for n in range(4):
            cols = slice(D_MODEL // 4 * n, D_MODEL // 4 * (n + 1))
            dve.tensor_scalar(out_tok[:, 0, cols], out_tok[:, 0, cols], r_tok[:, 0:1], None, ALU.mult).then_inc(y_ready_0, 1)

    @block.tensor
    def _(pe):
        def bank_free(g):
            pe.wait_ge(combined, g - 1)

        def consume(u, j, bank, banks, tiles, src, first, last, width=GROUP, tile=None, signal=1):
            pe.wait_ge(l_split, 4 * u + j + 1)
            for m in range(banks) if tile is None else (tile,):
                for q, k in enumerate(tiles):
                    at = slice(q * width + m * P, q * width + (m + 1) * P)
                    begins, ends = first and q == 0, last and q == len(tiles) - 1
                    high, low = (hs[:, j, at], src[:, k, :]), (ls[:, j, at], src[:, k, 0:TOK])
                    whole, half = acc_of(bank + m, 2 * TOK), acc_of(bank + m, TOK)
                    if ends:
                        pe.matmul(half, *low, start=False, stop=False)
                        mm = pe.matmul(whole, *high, start=False, stop=True)
                    else:
                        pe.matmul(whole, *high, start=begins, stop=False)
                        mm = pe.matmul(half, *low, start=False, stop=False)
            if signal:
                mm.then_inc(chunk_used, signal)

        def acc_of(bank, n):
            return (acc if bank < 4 else side)[:, bank % 4, 0:n]

        def unit(u, g, src, pair, between=None, needs=None):
            if not isinstance(g, int) or g >= 2:
                bank_free(g)
            for j in range(SLOTS):
                if needs is not None:
                    pe.wait_ge(needs[0], needs[1](j))
                consume(u, j, 2 * pair, 2, range(KC * j, KC * j + KC), src, j == 0, j == 3)
                if between is not None and j == between[0]:
                    between[1]()

        def x_transposes(t):
            if t >= 4:
                pe.wait_ge(res_ready, t - 3)
            for m in range(2):
                for b in range(2):
                    mm = pe.transpose(x_bank(t)[:, m * TOK + b * P:m * TOK + (b + 1) * P],
                                      x_tok[:, b, (2 * t + m) * P:(2 * t + m + 1) * P], ident[:, :])
            mm.then_inc(x_t, 1)

        pe.wait_ge(consts, 8)
        for b in range(2):
            pe.wait_ge(x_loaded[b], 16)
        for t in range(2):
            x_transposes(t)
        pe.wait_ge(gains_loaded, 4 * 16)
        pe.transpose(side[:, 0, 0:4 * KT], gain_rows[0:4 * KT, :], ident[0:4 * KT, 0:4 * KT]).then_inc(gain_t, 1)
        x_transposes(2)
        pe.wait_ge(diag_ready, 2)
        for b in range(2):
            mm = pe.matmul(side[:, 1, b * P:(b + 1) * P], ones[:, :], diag[:, b, :], start=True, stop=True)
        mm.then_inc(rms_b, 1)
        for t in range(3, KT // 2):
            x_transposes(t)

        for j in range(SLOTS):
            pe.wait_ge(hn_ready, 4 * j + 4)
            consume(0, j, 0, 1, range(KC * j, KC * j + KC), hn, j == 0, j == 3, width=P)

        pe.wait_ge(res_ready, KT // 2)

        def small_by_token():
            pe.wait_ge(combined, 1)
            for b in range(2):
                mm = pe.transpose(side[:, 2, b * P:(b + 1) * P], s_a[:, b * P:(b + 1) * P], ident[:, :])
            mm.then_inc(small_t, 1)

        unit(U_QI, U_QI, hn, U_QI % 2, between=(1, small_by_token))

        def decay_by_token():
            pe.wait_ge(f_c, 1)
            for b in range(2):
                mm = pe.transpose(side[:, 3, b * P:(b + 1) * P], c_sum[:, b * P:(b + 1) * P], ident[:, :])
            mm.then_inc(c_t, 1)

        for u in range(U_QI + 1, U_QB):
            unit(u, u, hn, u % 2, between=(1, decay_by_token) if u == U_QB - 1 else None)

        def dots(step):
            pe.wait_ge(staged, step + 1)
            pe.wait_ge(relu_done, FREE + step * 2)
            for b in range(2):
                own, n = slice(b * P, (b + 1) * P), (b + 1) * P
                dst = side[:, b, 0:2 * n].rearrange("p (h n) -> p h n", h=2)
                keys_h, keys_l = (t[:, :].rearrange("p (h n) -> p h n", h=2)[:, :, 0:n] for t in (kib_h, kib_l))
                pe.matmul(dst, qi_h[:, own], keys_h, start=True, stop=False)
                pe.matmul(dst, qi_h[:, own], keys_l, start=False, stop=False)
                mm = pe.matmul(dst, qi_l[:, own], keys_h, start=False, stop=True)
            mm.then_inc(dots_done, 1)

        pe.wait_ge(small_s, 4)
        with pe.Fori(0, 4) as i:
            for e in range(2):
                n = e + i * 2
                unit(U_QB + n, U_QB + n, hn, (U_QB + e) % 2)
                dots(n)

        def by_token(u, pair):
            bank_free(u)
            for j in range(SLOTS):
                pe.wait_ge(l_split, 4 * u + j + 1)
                for t in range(2):
                    for q in range(KC):
                        k = KC * j + q
                        wh, wl = hs[:, j, q * GROUP:(q + 1) * GROUP], ls[:, j, q * GROUP:(q + 1) * GROUP]
                        xh, xl = hn[:, k, t * P:(t + 1) * P], hn[:, k, TOK + t * P:TOK + (t + 1) * P]
                        dst = acc[:, 2 * pair + t, 0:TOK]
                        pe.matmul(dst, xh, wh, start=k == 0, stop=False)
                        pe.matmul(dst, xh, wl, start=False, stop=False)
                        mm = pe.matmul(dst, xl, wh, start=False, stop=k == KT - 1)
                mm.then_inc(chunk_used, 1)

        with pe.Fori(0, 2) as i:
            for e in range(2):
                by_token(U_VB + e + i * 2, (U_VB + e) % 2)

        def scores(head):
            pe.wait_ge(staged, STEPS_IDX + 2 + head * 2)
            pe.wait_ge(prob_ready, FREE + head * 2)
            pe.matmul(side[:, 0, 0:P], q_st[:, 0:P], k_st[:, 0:P], start=True, stop=True)
            pe.matmul(side[:, 0, P:CAT], q_st[:, P:TOK], k_st[:, :], start=True, stop=True).then_inc(qk_done, 1)

        def probs_by_key(head):
            pe.wait_ge(prob_ready, FREE + 2 + head * 2)
            pe.wait_ge(pt_ready, FREE + head)
            for c in range(3):
                mm = pe.transpose(side[:, 2, c * P:(c + 1) * P], lg[:, c * P:(c + 1) * P], ident[:, :])
            mm.then_inc(pt_done, 1)

        def values(head):
            pe.wait_ge(pt_ready, FREE + 1 + head)
            pe.wait_ge(v_staged, head + 1)
            pe.wait_ge(o_ready, FREE + head)
            pe.matmul(side[:, 3, 0:P], v_st[:, 0, :], pt[:, 0:P], start=True, stop=True)
            pe.matmul(side[:, 3, P:TOK], v_st[:, 0, :], pt[:, P:2 * P], start=True, stop=False)
            pe.matmul(side[:, 3, P:TOK], v_st[:, 1, :], pt[:, 2 * P:CAT], start=False, stop=True).then_inc(pv_done, 1)

        def head_units(u0, head0):
            scores(head0)

            def two_heads(i, last=False):
                for e in range(2):
                    h = e + i * 2

                    def between():
                        probs_by_key(head0 + h)
                        if not (last and e == 1):
                            scores(head0 + h + 1)

                    unit(u0 + h, u0 + h, hn, (u0 + e) % 2, between=(2, between))
                    values(head0 + h)

            with pe.Fori(0, 3) as i:
                two_heads(i)
            two_heads(3, last=True)

        head_units(U_GA, 0)
        with pe.Fori(0, 2) as i:
            for e in range(2):
                unit(U_QA + e + i * 2, U_QA + e + i * 2, hn, (U_QA + e) % 2)
        unit(U_KA, U_KA, hn, U_KA % 2)
        by_token(U_VA, U_VA % 2)
        head_units(U_GB, HB)

        def merge_units(i, first=False):
            for e in range(2):
                u = U_WO + e + i * 2
                pair = (U_WO + e) % 2
                bank_free(u)
                for j in range(SLOTS):
                    if first and e == 0 and j == 2:
                        pe.wait_ge(o_ready, FREE + HEADS)
                    t = KC * ((j + 2) % SLOTS)
                    consume(u, j, 2 * pair + 4 * (j // 2), 2, range(t, t + KC), heads_o, j % 2 == 0, j % 2 == 1)

        merge_units(0, first=True)
        with pe.Fori(1, 4) as i:
            merge_units(i)

        def out_units(i, needs=None):
            for e in range(2):
                unit(U_OUT + e + i * 2, U_OUT + e + i * 2, mixed, (U_OUT + e) % 2, needs=None if e else needs)

        out_units(0, needs=(mix_ready, lambda j: 2 * j + 2))
        with pe.Fori(1, 4) as i:
            out_units(i)
        pe.wait_ge(p_loaded, 16)
        for t in range(KT_PLE):
            for b in range(2):
                mm = pe.transpose(side[:, 2, t * TOK + b * P:t * TOK + (b + 1) * P], p_tok[:, b, t * P:(t + 1) * P], ident[:, :])
        mm.then_inc(p_t, 1)

        def mean_squares(n):
            pe.wait_ge(sq_done, 8 * n)
            pe.matmul(side[:, 0, 0:TOK], ones[:, :], sq_sum[:, 0:TOK], start=True, stop=False)
            pe.matmul(side[:, 0, 0:TOK], ones[:, :], sq_sum[:, TOK:2 * TOK], start=False, stop=True).then_inc(ms_done, 1)

        def ffn_pair(i, first=False):
            for e in range(2):
                opening = first and e == 0
                unit(U_FFN + e + i * 2, U_FFN + e + i * 2, xg, (U_FFN + e) % 2,
                     needs=(xg_ready, lambda j: 4 * j + 4) if opening else None,
                     between=(2, lambda: mean_squares(1)) if opening else None)

        ffn_pair(0, first=True)
        with pe.Fori(1, N_FFN) as i:
            ffn_pair(i)

        def down_groups(i, first=False):
            for e in range(2):
                bank_free(G_DOWN + e + i * 2)
                t = 0
                for c, n in enumerate(DOWN_TILES):
                    if first and e == 0:
                        pe.wait_ge(ff_ready, (t + n + 1) // 2)
                    consume(U_DOWN + 3 * e + c // SLOTS + i * 6, c % SLOTS, 2 * ((G_DOWN + e) % 2), 2,
                            range(t, t + n), ff, c == 0, c == len(DOWN_TILES) - 1)
                    t += n

        down_groups(0, first=True)
        with pe.Fori(1, 4) as i:
            down_groups(i)
        pe.wait_ge(p_ready, 1)
        for c in range(SLOTS):
            if c > 0:
                pe.wait_ge(combined, G_PROJ + 2 * (c - 1))
            consume(U_PROJ, c, 4 * (1 - c % 2), 4, range(KT_PLE), p_cols, True, True, width=2 * GROUP)
        pe.wait_ge(combined, G_PLE - 2)
        mean_squares(2)

        def final_t(n, par):
            pe.wait_ge(fin_ready, 2 * n + 2)
            if not isinstance(n, int) or n > 0:
                pe.wait_ge(fin_read, n)
            for b in range(2):
                for m in range(2):
                    mm = pe.transpose(side[:, 1, b * TOK + m * P:b * TOK + (m + 1) * P], fin[:, par, m, b * P:(b + 1) * P], ident[:, :])
            mm.then_inc(fin_t, 1)

        def ple_unit(i, e, first=False):
            n = e + i * 2
            unit(U_PLE + n, G_PLE + n, xg, (G_PLE + e) % 2,
                 needs=(xg_ready, lambda j: 16 + 4 * j + 4) if first else None,
                 between=None if first else (2, lambda: final_t(n - 1, 1 - e)))

        ple_unit(0, 0, first=True)
        ple_unit(0, 1)
        with pe.Fori(1, 3) as i:
            ple_unit(i, 0)
            ple_unit(i, 1)
        ple_unit(3, 0)
        u, g = U_PLE + 7, G_PLE + 7
        bank_free(g)
        for m in range(2):
            for j in range(SLOTS):
                consume(u, j, 2 * (g % 2), 2, range(KC * j, KC * j + KC), xg, j == 0, j == 3, tile=m, signal=2 * (j == 3))
                if m == 1 and j == 0:
                    final_t(6, 0)

        pe.wait_ge(sq_done, 23)
        pe.wait_ge(fin_read, 7)
        for step in range(3):
            if step:
                pe.wait_ge(last_sq, step)
            for b in range(2):
                for m in range(2) if step == 0 else (step - 1,):
                    src = s_a if step else sq_sum
                    mm = pe.matmul(side[:, 2 + b, 0:1], src[:, m * TOK + b * P:m * TOK + (b + 1) * P], ones[:, 0:1],
                                   start=step == 0 and m == 0, stop=step == 2)
            if step == 2:
                mm.then_inc(tok_done, 1)
            if step:
                m = step - 1
                pe.wait_ge(fin_ready, 15 + m)
                for b in range(2):
                    mm = pe.transpose(side[:, 1, b * TOK + m * P:b * TOK + (m + 1) * P], fin[:, 1, m, b * P:(b + 1) * P],
                                      ident[:, :])
        mm.then_inc(fin_t, 1)

    block.__exit__(None, None, None)


def rope_constants():
    import numpy as np

    rows = np.zeros((P, 4), np.float32)

    def frequencies(half):
        return np.float32(THETA) ** (-np.arange(half, dtype=np.float32) / np.float32(half))

    for rot, col, starts in ((ROT_A, 0, (0,)), (ROT_IDX, 2, (0, D_IDX))):
        half = rot // 2
        for at in starts:
            for side in range(2):
                rows[at + side * half:at + (side + 1) * half, col] = frequencies(half)
                rows[at + side * half:at + (side + 1) * half, col + 1] = 1.0 if side else -1.0
    return rows


_INS = ["x", "p", "positions", "g_mix", "w_in", "b_f", "w_o_a", "w_o_b", "w_out", "g_ffn", "w_ffn_gate",
        "w_ffn_up", "w_ffn_down", "g_ple", "w_ple_gate", "w_ple_proj", "g_final"]


def kernel(**inputs):
    import numpy as np
    import concourse.bacc as bacc
    from concourse.bass_utils import run_bass_kernel_spmd

    nc = bacc.Bacc("TRN2", target_bir_lowering=False, num_devices=1)
    arrays, args = {}, []
    for name in [*_INS, "rope_rows"]:
        a = rope_constants() if name == "rope_rows" else np.ascontiguousarray(inputs[name])
        arrays[f"in_{name}"] = a
        args.append(nc.dram_tensor(f"in_{name}", a.shape, mybir.dt.from_np(a.dtype), kind="ExternalInput").ap())
    out = nc.dram_tensor("out_0", inputs["x"].shape, F32, kind="ExternalOutput").ap()
    c_rows = nc.dram_tensor("c_rows", (HB, TOK), F32, kind="Internal").ap()
    hybrid_layer(nc, c_rows, *args, out)
    r = run_bass_kernel_spmd(nc, [arrays], core_ids=[0])
    return np.asarray(r.results[0]["out_0"])
```
